# Optimizing a Trainium2 kernel written in Bass

```python
import jax, jax.numpy as jnp
from jax import lax
import numpy as np

D_MODEL = 1024
BATCH = 1
SEQ = 512
DEPTH = 2

GRID_W = 64
CTX_LEN = 256
N_MIXERS = 2
N_FNET_LAYERS = (DEPTH + 1) // 2
N_RWKV_LAYERS = DEPTH // 2
N_VRES_LAYERS = N_RWKV_LAYERS - 1
FNET_GROUPS = 4
FNET_GROUP_DIM = D_MODEL // FNET_GROUPS
HEAD_SIZE = 64
N_HEADS = D_MODEL // HEAD_SIZE
D_DECAY_LORA = 64
D_AAA_LORA = 64
D_MV_LORA = 32
D_GATE_LORA = 128
N_DIRS = 2
N_EXPERTS = 16
D_EXPERT = 1024
CAPACITY_FACTOR = 2
NORM_EPS = 1e-6
LNX_EPS = 64e-5


def rmsnorm(h, g):
    hf = h.astype(jnp.float32)
    hf = hf * lax.rsqrt(jnp.mean(hf * hf, axis=-1, keepdims=True) + NORM_EPS)
    return (hf * g.astype(jnp.float32)).astype(h.dtype)

def adaln_params(cvec, w, b):
    return jnp.split(jax.nn.silu(cvec) @ w + b, 6, axis=-1)

def fourier_mix(h, w_o, b_o):
    bsz, t, _ = h.shape
    hg = h.astype(jnp.float32).reshape(bsz, t, FNET_GROUPS, FNET_GROUP_DIM)
    f = jnp.fft.fft2(hg, axes=(1, 3), norm='ortho').real
    return f.reshape(bsz, t, D_MODEL).astype(h.dtype) @ w_o + b_o

def qshift_grid(h):
    bsz, t, d = h.shape
    rows = t // GRID_W
    g = h.reshape(bsz, rows, GRID_W, d)
    q = d // 4
    left = jnp.pad(g[:, :, :-1, :q], ((0, 0), (0, 0), (1, 0), (0, 0)))
    right = jnp.pad(g[:, :, 1:, q:2 * q], ((0, 0), (0, 0), (0, 1), (0, 0)))
    up = jnp.pad(g[:, :-1, :, 2 * q:3 * q], ((0, 0), (1, 0), (0, 0), (0, 0)))
    down = jnp.pad(g[:, 1:, :, 3 * q:], ((0, 0), (0, 1), (0, 0), (0, 0)))
    return jnp.concatenate([left, right, up, down], axis=-1).reshape(bsz, t, d)

def shift_seq(h):
    half = h.shape[-1] // 2
    prev = jnp.pad(h[:, :-1, :half], ((0, 0), (1, 0), (0, 0)))
    nxt = jnp.pad(h[:, 1:, half:], ((0, 0), (0, 1), (0, 0)))
    return jnp.concatenate([prev, nxt], axis=-1)

def to_heads(t):
    return t.reshape(t.shape[0], t.shape[1], N_HEADS, HEAD_SIZE)

def rwkv_project(h, h_shift, mix, wr, wk, wv, w0, w1, w2, a0, a1, a2, g1, g2, k_k, k_a, v_first, vres):
    xx = h_shift - h
    xr, xw, xk, xv, xa, xg = [h + xx * mix[j] for j in range(6)]
    r = xr @ wr
    k = xk @ wk
    v = xv @ wv
    if vres is not None:
        v0, v1, v2 = vres
        v = v + (v_first - v) * jax.nn.sigmoid(v0 + (xv @ v1) @ v2)
    g = jax.nn.sigmoid(xg @ g1) @ g2
    kk = to_heads((k * k_k).astype(jnp.float32))
    kk = kk * lax.rsqrt(jnp.sum(kk * kk, axis=-1, keepdims=True) + 1e-12)
    kf = k.astype(jnp.float32)
    dirs = []
    for d in range(N_DIRS):
        wlog = (w0[d] + jnp.tanh(xw @ w1[d]) @ w2[d]).astype(jnp.float32)
        wlog = -jax.nn.softplus(-wlog) - 0.5
        decay = jnp.exp(-jnp.exp(wlog))
        a = jax.nn.sigmoid((a0[d] + (xa @ a1[d]) @ a2[d]).astype(jnp.float32))
        k_d = kf * (1.0 + (a - 1.0) * k_a.astype(jnp.float32))
        dirs.append((to_heads(decay), to_heads(k_d), to_heads(a)))
    return to_heads(r.astype(jnp.float32)), v, g, kk, dirs

def wkv_scan(r, decay, k, v, a_vec, b_vec, s0, reverse):
    def step(s, inp):
        r_t, w_t, k_t, v_t, a_t, b_t = inp
        sa = jnp.einsum('bhvk,bhk->bhv', s, a_t)
        s = s * w_t[:, :, None, :] + sa[..., None] * b_t[:, :, None, :] + v_t[..., None] * k_t[:, :, None, :]
        return s, jnp.einsum('bhvk,bhk->bhv', s, r_t)
    xs = tuple(jnp.swapaxes(t, 0, 1) for t in (r, decay, k, v, a_vec, b_vec))
    s_final, ys = lax.scan(step, s0, xs, reverse=reverse)
    return jnp.swapaxes(ys, 0, 1), s_final

def rwkv_output(y, r, v, g, k_dirs, r_k, lnx_w, lnx_b, wo, dtype):
    mu = jnp.mean(y, axis=-1, keepdims=True)
    var = jnp.mean(jnp.square(y - mu), axis=-1, keepdims=True)
    yn = (y - mu) * lax.rsqrt(var + LNX_EPS)
    bsz, t = y.shape[:2]
    yn = yn.reshape(bsz, t, D_MODEL) * lnx_w.astype(jnp.float32) + lnx_b.astype(jnp.float32)
    rk = r_k.astype(jnp.float32)
    bonus = sum(jnp.sum(r * k_d * rk, axis=-1, keepdims=True) for k_d in k_dirs) * v
    out = (yn + bonus.reshape(bsz, t, D_MODEL)).astype(dtype) * g
    return out @ wo

def ec_moe(h, router, wg, wu, wd):
    bsz, t, d = h.shape
    cap = CAPACITY_FACTOR * t // N_EXPERTS
    aff = jax.nn.softmax((h @ router).astype(jnp.float32), axis=-1)
    gates, idx = lax.top_k(jnp.swapaxes(aff, 1, 2), cap)
    xs = jax.vmap(lambda hb, ib: hb[ib])(h, idx)
    hid = jax.nn.silu(jnp.einsum('becd,edf->becf', xs, wg)) * jnp.einsum('becd,edf->becf', xs, wu)
    ys = jnp.einsum('becf,efd->becd', hid, wd) * gates[..., None].astype(h.dtype)
    return jax.vmap(lambda ib, yb: jnp.zeros((t, d), h.dtype).at[ib.reshape(-1)].add(yb.reshape(-1, d)))(idx, ys)

def first_inputs(seed: int = 0) -> dict:
    key = jax.random.key(seed)
    ks = iter(jax.random.split(key, 40))

    def nrm(shape, scale):
        return jax.random.normal(next(ks), shape, jnp.float32) * scale

    D = D_MODEL
    inv = D ** -0.5
    NR = N_RWKV_LAYERS
    NV = N_VRES_LAYERS
    return {
        'x': nrm((BATCH, SEQ, D), 1.0),
        'c': nrm((BATCH, D), 1.0),
        'ctx': nrm((BATCH, CTX_LEN, D), 1.0),
        'c_ctx': nrm((D,), 1.0),
        'ada_w': nrm((DEPTH, D, 6 * D), 0.5 * inv),
        'ada_b': nrm((DEPTH, 6 * D), 0.01),
        'norm_g': 1.0 + nrm((DEPTH, 2, D), 0.1),
        'fnet_wo': nrm((N_FNET_LAYERS, D, D), inv),
        'fnet_bo': nrm((N_FNET_LAYERS, D), 0.01),
        'rw_mix': jax.random.uniform(next(ks), (NR, 6, D), jnp.float32),
        'rw_wr': nrm((NR, D, D), inv),
        'rw_wk': nrm((NR, D, D), inv),
        'rw_wv': nrm((NR, D, D), inv),
        'rw_wo': nrm((NR, D, D), inv),
        'rw_w0': jax.random.uniform(next(ks), (NR, N_DIRS, D), jnp.float32, -6.0, 1.0),
        'rw_w1': nrm((NR, N_DIRS, D, D_DECAY_LORA), inv),
        'rw_w2': nrm((NR, N_DIRS, D_DECAY_LORA, D), 0.1),
        'rw_a0': nrm((NR, N_DIRS, D), 0.5),
        'rw_a1': nrm((NR, N_DIRS, D, D_AAA_LORA), inv),
        'rw_a2': nrm((NR, N_DIRS, D_AAA_LORA, D), 0.1),
        'rw_v0': nrm((NV, D), 0.5),
        'rw_v1': nrm((NV, D, D_MV_LORA), inv),
        'rw_v2': nrm((NV, D_MV_LORA, D), 0.1),
        'rw_g1': nrm((NR, D, D_GATE_LORA), inv),
        'rw_g2': nrm((NR, D_GATE_LORA, D), D_GATE_LORA ** -0.5),
        'rw_kk': 0.85 + nrm((NR, D), 0.1),
        'rw_ka': 1.0 + nrm((NR, D), 0.1),
        'rw_rk': nrm((NR, N_HEADS, HEAD_SIZE), 0.1),
        'rw_lnx_w': 1.0 + nrm((NR, D), 0.1),
        'rw_lnx_b': nrm((NR, D), 0.01),
        'moe_router': nrm((DEPTH, D, N_EXPERTS), inv),
        'moe_wg': nrm((DEPTH, N_EXPERTS, D, D_EXPERT), inv),
        'moe_wu': nrm((DEPTH, N_EXPERTS, D, D_EXPERT), inv),
        'moe_wd': nrm((DEPTH, N_EXPERTS, D_EXPERT, D), D_EXPERT ** -0.5),
        'final_g': 1.0 + nrm((D,), 0.1),
    }

def first_block(x, c, ctx, c_ctx, ada_w, ada_b, norm_g, fnet_wo, fnet_bo, rw_mix, rw_wr, rw_wk, rw_wv, rw_wo,
              rw_w0, rw_w1, rw_w2, rw_a0, rw_a1, rw_a2, rw_v0, rw_v1, rw_v2, rw_g1, rw_g2, rw_kk, rw_ka, rw_rk,
              rw_lnx_w, rw_lnx_b, moe_router, moe_wg, moe_wu, moe_wd, final_g):
    dtype = x.dtype
    v_first_x = None
    v_first_c = None
    for i in range(DEPTH):
        need_ctx = i < DEPTH - 1
        sh1x, sc1x, g1x, sh2x, sc2x, g2x = [m[:, None, :] for m in adaln_params(c, ada_w[i], ada_b[i])]
        sh1c, sc1c, g1c, sh2c, sc2c, g2c = adaln_params(c_ctx, ada_w[i], ada_b[i])
        hx = rmsnorm(x, norm_g[i, 0]) * (1.0 + sc1x) + sh1x
        if i % N_MIXERS == 0:
            fi = i // N_MIXERS
            x = x + g1x * fourier_mix(hx, fnet_wo[fi], fnet_bo[fi])
            if need_ctx:
                hc = rmsnorm(ctx, norm_g[i, 0]) * (1.0 + sc1c) + sh1c
                ctx = ctx + g1c * fourier_mix(hc, fnet_wo[fi], fnet_bo[fi])
        else:
            ri = i // N_MIXERS
            hc = rmsnorm(ctx, norm_g[i, 0]) * (1.0 + sc1c) + sh1c
            vres = None if ri == 0 else (rw_v0[ri - 1], rw_v1[ri - 1], rw_v2[ri - 1])
            prm = (rw_mix[ri], rw_wr[ri], rw_wk[ri], rw_wv[ri], rw_w0[ri], rw_w1[ri], rw_w2[ri],
                   rw_a0[ri], rw_a1[ri], rw_a2[ri], rw_g1[ri], rw_g2[ri], rw_kk[ri], rw_ka[ri])
            r_x, v_x, gt_x, kk_x, dirs_x = rwkv_project(hx, qshift_grid(hx), *prm, v_first_x, vres)
            r_c, v_c, gt_c, kk_c, dirs_c = rwkv_project(hc, shift_seq(hc), *prm, v_first_c, vres)
            if ri == 0:
                v_first_x, v_first_c = v_x, v_c
            vh_x = to_heads(v_x.astype(jnp.float32))
            vh_c = to_heads(v_c.astype(jnp.float32))
            s0 = jnp.zeros((x.shape[0], N_HEADS, HEAD_SIZE, HEAD_SIZE), jnp.float32)
            ys_x = []
            ys_c = []
            for d in range(N_DIRS):
                reverse = d == 1
                dec_c, k_c, a_c = dirs_c[d]
                yc_d, s_ctx = wkv_scan(r_c, dec_c, k_c, vh_c, -kk_c, kk_c * a_c, s0, reverse)
                dec_x, k_x, a_x = dirs_x[d]
                yx_d, _ = wkv_scan(r_x, dec_x, k_x, vh_x, -kk_x, kk_x * a_x, s_ctx, reverse)
                ys_x.append(yx_d)
                ys_c.append(yc_d)
            x = x + g1x * rwkv_output(ys_x[0] + ys_x[1], r_x, vh_x, gt_x, [dd[1] for dd in dirs_x],
                                      rw_rk[ri], rw_lnx_w[ri], rw_lnx_b[ri], rw_wo[ri], dtype)
            if need_ctx:
                ctx = ctx + g1c * rwkv_output(ys_c[0] + ys_c[1], r_c, vh_c, gt_c, [dd[1] for dd in dirs_c],
                                              rw_rk[ri], rw_lnx_w[ri], rw_lnx_b[ri], rw_wo[ri], dtype)
        hx = rmsnorm(x, norm_g[i, 1]) * (1.0 + sc2x) + sh2x
        x = x + g2x * ec_moe(hx, moe_router[i], moe_wg[i], moe_wu[i], moe_wd[i])
        if need_ctx:
            hc = rmsnorm(ctx, norm_g[i, 1]) * (1.0 + sc2c) + sh2c
            ctx = ctx + g2c * ec_moe(hc, moe_router[i], moe_wg[i], moe_wu[i], moe_wd[i])
    return rmsnorm(x, final_g)


HEAD_DIM = 64
N_GROUP_HEADS = 4
GROUP_WIDTH = N_GROUP_HEADS * HEAD_DIM
MIX_WIDTH = 4 * GROUP_WIDTH
MLA_Q_RANK = 256
MLA_KV_RANK = 128
MLA_NOPE = 64
MLA_ROPE = 32
MLA_V = 64
SWA_KV_HEADS = 2
SWA_WINDOW = 128
IDX_HEADS = 8
IDX_DIM = 32
DSA_TOPK = 256
FOX_HEADS = 4
D_FF = 4 * D_MODEL
ROPE_THETA = 10000.0
Q_BLOCK = 128
EPS = 1e-6

IN_SPLITS = (
    MLA_Q_RANK, MLA_KV_RANK, MLA_ROPE,
    GROUP_WIDTH, SWA_KV_HEADS * HEAD_DIM, SWA_KV_HEADS * HEAD_DIM,
    GROUP_WIDTH, GROUP_WIDTH, GROUP_WIDTH, IDX_HEADS * IDX_DIM, IDX_DIM, IDX_HEADS,
    GROUP_WIDTH, GROUP_WIDTH, GROUP_WIDTH, FOX_HEADS,
)
IN_WIDTH = sum(IN_SPLITS)


def rms_norm(x, g):
    xf = x.astype(jnp.float32)
    y = xf * lax.rsqrt(jnp.mean(xf * xf, axis=-1, keepdims=True) + EPS)
    return (y * g.astype(jnp.float32)).astype(x.dtype)

def rope(x, pos):
    d = x.shape[-1]
    half = d // 2
    inv_freq = 1.0 / (ROPE_THETA ** (jnp.arange(0, half, dtype=jnp.float32) * 2.0 / d))
    ang = pos[:, None] * inv_freq[None, :]
    cos = jnp.cos(ang)[:, None, :]
    sin = jnp.sin(ang)[:, None, :]
    xf = x.astype(jnp.float32)
    x1, x2 = xf[..., :half], xf[..., half:]
    out = jnp.concatenate([x1 * cos - x2 * sin, x2 * cos + x1 * sin], axis=-1)
    return out.astype(x.dtype)

def split_cols(proj):
    offs, acc = [], 0
    for n in IN_SPLITS[:-1]:
        acc += n
        offs.append(acc)
    return jnp.split(proj, offs, axis=-1)

def causal_block_attention(q, k, v, scale, log_f_cum=None):
    B, S, H, dk = q.shape
    dv = v.shape[-1]
    nb = S // Q_BLOCK
    q_blocks = q.reshape(B, nb, Q_BLOCK, H, dk).swapaxes(0, 1)
    starts = jnp.arange(nb, dtype=jnp.int32) * Q_BLOCK
    key_pos = jnp.arange(S, dtype=jnp.int32)
    if log_f_cum is None:
        xs = (q_blocks, starts)
    else:
        cum_blocks = log_f_cum.reshape(B, nb, Q_BLOCK, H).swapaxes(0, 1)
        cum_keys = log_f_cum.transpose(0, 2, 1)[:, :, None, :]
        xs = (q_blocks, starts, cum_blocks)

    def block(args):
        q_blk, start = args[0], args[1]
        s = jnp.einsum('bqhd,bkhd->bhqk', q_blk, k).astype(jnp.float32) * scale
        if log_f_cum is not None:
            s = s + (args[2].transpose(0, 2, 1)[..., None] - cum_keys)
        qpos = start + jnp.arange(Q_BLOCK, dtype=jnp.int32)
        causal = key_pos[None, :] <= qpos[:, None]
        s = jnp.where(causal, s, -jnp.inf)
        p = jax.nn.softmax(s, axis=-1).astype(v.dtype)
        return jnp.einsum('bhqk,bkhd->bqhd', p, v)

    out = lax.map(block, xs)
    return out.swapaxes(0, 1).reshape(B, S, H, dv)

def sliding_window_attention(q, k, v, sinks, scale):
    B, S, H, d = q.shape
    Hk = k.shape[2]
    G = H // Hk
    W = SWA_WINDOW
    nb = S // W
    qb = q.reshape(B, nb, W, Hk, G, d)

    def with_prev(t):
        tb = t.reshape(B, nb, W, Hk, d)
        prev = jnp.concatenate([jnp.zeros_like(tb[:, :1]), tb[:, :-1]], axis=1)
        return jnp.concatenate([prev, tb], axis=2)

    kb, vb = with_prev(k), with_prev(v)
    s = jnp.einsum('bnqkgd,bnjkd->bnkgqj', qb, kb).astype(jnp.float32) * scale
    blk = jnp.arange(nb, dtype=jnp.int32)[:, None, None]
    qi = jnp.arange(W, dtype=jnp.int32)[None, :, None]
    kj = jnp.arange(2 * W, dtype=jnp.int32)[None, None, :]
    qpos = blk * W + qi
    kpos = blk * W - W + kj
    mask = (kpos >= 0) & (kpos <= qpos) & (qpos - kpos < SWA_WINDOW)
    s = jnp.where(mask[None, :, None, None], s, -jnp.inf)
    sink = jnp.broadcast_to(sinks.astype(jnp.float32).reshape(1, 1, Hk, G, 1, 1),
                            s.shape[:-1] + (1,))
    p = jax.nn.softmax(jnp.concatenate([s, sink], axis=-1), axis=-1)[..., :-1]
    o = jnp.einsum('bnkgqj,bnjkd->bnqkgd', p.astype(v.dtype), vb)
    return o.reshape(B, S, H, d)

def dsa_attention(q, k, v, q_idx, k_idx, w_idx, top_k, scale):
    B, S, H, d = q.shape
    nb = S // Q_BLOCK

    def blocks(t):
        return t.reshape((B, nb, Q_BLOCK) + t.shape[2:]).swapaxes(0, 1)

    starts = jnp.arange(nb, dtype=jnp.int32) * Q_BLOCK
    key_pos = jnp.arange(S, dtype=jnp.int32)

    def block(args):
        q_blk, qi_blk, w_blk, start = args
        qpos = start + jnp.arange(Q_BLOCK, dtype=jnp.int32)
        rel = jax.nn.relu(jnp.einsum('bqhd,bkd->bqhk', qi_blk, k_idx).astype(jnp.float32))
        score = jnp.einsum('bqhk,bqh->bqk', rel, w_blk.astype(jnp.float32))
        score = jnp.where(key_pos[None, None, :] <= qpos[None, :, None], score, -jnp.inf)
        _, idx = lax.top_k(score, top_k)
        k_sel = jax.vmap(lambda kb, ib: kb[ib])(k, idx)
        v_sel = jax.vmap(lambda vb, ib: vb[ib])(v, idx)
        s = jnp.einsum('bqhd,bqkhd->bqhk', q_blk, k_sel).astype(jnp.float32) * scale
        valid = (idx <= qpos[None, :, None])[:, :, None, :]
        s = jnp.where(valid, s, -jnp.inf)
        p = jax.nn.softmax(s, axis=-1).astype(v.dtype)
        return jnp.einsum('bqhk,bqkhd->bqhd', p, v_sel)

    out = lax.map(block, (blocks(q), blocks(q_idx), blocks(w_idx), starts))
    return out.swapaxes(0, 1).reshape(B, S, H, d)

def second_inputs(seed: int = 0) -> dict:
    key = jax.random.key(seed)
    ks = jax.random.split(key, 16)
    H = N_GROUP_HEADS
    f32 = jnp.float32

    def nrm(k, shape, fan_in):
        return jax.random.normal(k, shape, f32) * (fan_in ** -0.5)

    def gain(k, shape):
        return 1.0 + 0.05 * jax.random.normal(k, shape, f32)

    return {
        "x": jax.random.normal(ks[0], (BATCH, SEQ, D_MODEL), f32),
        "norm1": gain(ks[1], (DEPTH, D_MODEL)),
        "w_in": nrm(ks[2], (DEPTH, D_MODEL, IN_WIDTH), D_MODEL),
        "mla_q_norm": gain(ks[3], (DEPTH, MLA_Q_RANK)),
        "mla_kv_norm": gain(ks[4], (DEPTH, MLA_KV_RANK)),
        "mla_w_uq": nrm(ks[5], (DEPTH, MLA_Q_RANK, H * (MLA_NOPE + MLA_ROPE)), MLA_Q_RANK),
        "mla_w_ukv": nrm(ks[6], (DEPTH, MLA_KV_RANK, H * (MLA_NOPE + MLA_V)), MLA_KV_RANK),
        "swa_sinks": 0.5 * jax.random.normal(ks[7], (DEPTH, H), f32),
        "fox_b_f": 0.1 * jax.random.normal(ks[8], (DEPTH, FOX_HEADS), f32),
        "w_out": nrm(ks[9], (DEPTH, MIX_WIDTH, D_MODEL), MIX_WIDTH),
        "norm2": gain(ks[10], (DEPTH, D_MODEL)),
        "w_up": nrm(ks[11], (DEPTH, D_MODEL, D_FF), D_MODEL),
        "w_down": nrm(ks[12], (DEPTH, D_FF, D_MODEL), D_FF),
        "final_norm": gain(ks[13], (D_MODEL,)),
    }

def second_block(x, norm1, w_in, mla_q_norm, mla_kv_norm, mla_w_uq, mla_w_ukv, swa_sinks,
              fox_b_f, w_out, norm2, w_up, w_down, final_norm):
    B, S, _ = x.shape
    H = N_GROUP_HEADS
    Dh = HEAD_DIM
    pos = jnp.arange(S, dtype=jnp.float32)
    top_k = min(DSA_TOPK, S // 4)
    for l in range(DEPTH):
        h = rms_norm(x, norm1[l])
        proj = h @ w_in[l]
        (a_cq, a_ckv, a_kr, b_q, b_k, b_v, c_q, c_k, c_v, c_qi, c_ki, c_w,
         d_q, d_k, d_v, d_f) = split_cols(proj)

        qa = (rms_norm(a_cq, mla_q_norm[l]) @ mla_w_uq[l]).reshape(B, S, H, MLA_NOPE + MLA_ROPE)
        q_a = jnp.concatenate([qa[..., :MLA_NOPE], rope(qa[..., MLA_NOPE:], pos)], axis=-1)
        kv = (rms_norm(a_ckv, mla_kv_norm[l]) @ mla_w_ukv[l]).reshape(B, S, H, MLA_NOPE + MLA_V)
        k_rope = rope(a_kr.reshape(B, S, 1, MLA_ROPE), pos)
        k_a = jnp.concatenate([kv[..., :MLA_NOPE],
                               jnp.broadcast_to(k_rope, (B, S, H, MLA_ROPE))], axis=-1)
        o_a = causal_block_attention(q_a, k_a, kv[..., MLA_NOPE:],
                                     (MLA_NOPE + MLA_ROPE) ** -0.5)

        q_b = rope(b_q.reshape(B, S, H, Dh), pos)
        k_b = rope(b_k.reshape(B, S, SWA_KV_HEADS, Dh), pos)
        v_b = b_v.reshape(B, S, SWA_KV_HEADS, Dh)
        o_b = sliding_window_attention(q_b, k_b, v_b, swa_sinks[l], Dh ** -0.5)

        q_c = rope(c_q.reshape(B, S, H, Dh), pos)
        k_c = rope(c_k.reshape(B, S, H, Dh), pos)
        v_c = c_v.reshape(B, S, H, Dh)
        qi = rope(c_qi.reshape(B, S, IDX_HEADS, IDX_DIM), pos)
        ki = rope(c_ki.reshape(B, S, 1, IDX_DIM), pos)[:, :, 0, :]
        o_c = dsa_attention(q_c, k_c, v_c, qi, ki, c_w, top_k, Dh ** -0.5)

        log_f = jax.nn.log_sigmoid((d_f + fox_b_f[l]).astype(jnp.float32))
        cum = lax.cumsum(log_f, axis=1)
        o_d = causal_block_attention(d_q.reshape(B, S, FOX_HEADS, Dh),
                                     d_k.reshape(B, S, FOX_HEADS, Dh),
                                     d_v.reshape(B, S, FOX_HEADS, Dh),
                                     Dh ** -0.5, log_f_cum=cum)

        mixed = jnp.concatenate([o_a.reshape(B, S, GROUP_WIDTH), o_b.reshape(B, S, GROUP_WIDTH),
                                 o_c.reshape(B, S, GROUP_WIDTH), o_d.reshape(B, S, GROUP_WIDTH)],
                                axis=-1)
        x = x + mixed @ w_out[l]

        h2 = rms_norm(x, norm2[l])
        x = x + jnp.square(jax.nn.relu(h2 @ w_up[l])) @ w_down[l]
    return rms_norm(x, final_norm)


def setup_inputs(seed=0):
    out = dict(first_inputs(seed))
    for name, value in second_inputs(seed + 1).items():
        if name != "x":
            out[name + "_2"] = value
    return out


def reference(
    x, c, ctx, c_ctx, ada_w, ada_b, norm_g, fnet_wo, fnet_bo, rw_mix, rw_wr, rw_wk, rw_wv,
    rw_wo, rw_w0, rw_w1, rw_w2, rw_a0, rw_a1, rw_a2, rw_v0, rw_v1, rw_v2, rw_g1, rw_g2, rw_kk,
    rw_ka, rw_rk, rw_lnx_w, rw_lnx_b, moe_router, moe_wg, moe_wu, moe_wd, final_g, norm1_2,
    w_in_2, mla_q_norm_2, mla_kv_norm_2, mla_w_uq_2, mla_w_ukv_2, swa_sinks_2, fox_b_f_2,
    w_out_2, norm2_2, w_up_2, w_down_2, final_norm_2,
):
    x = first_block(
        x, c, ctx, c_ctx, ada_w, ada_b, norm_g, fnet_wo, fnet_bo, rw_mix, rw_wr, rw_wk, rw_wv,
        rw_wo, rw_w0, rw_w1, rw_w2, rw_a0, rw_a1, rw_a2, rw_v0, rw_v1, rw_v2, rw_g1, rw_g2,
        rw_kk, rw_ka, rw_rk, rw_lnx_w, rw_lnx_b, moe_router, moe_wg, moe_wu, moe_wd, final_g,
    )
    return second_block(
        x, norm1_2, w_in_2, mla_q_norm_2, mla_kv_norm_2, mla_w_uq_2, mla_w_ukv_2, swa_sinks_2,
        fox_b_f_2, w_out_2, norm2_2, w_up_2, w_down_2, final_norm_2,
    )


_drawn_inputs = setup_inputs


def setup_inputs(seed=0):
    import zlib

    import numpy as np

    out = dict(_drawn_inputs(seed))
    spreads = {}
    factors = {'ada_b': 3.033,
     'fnet_bo': 7.535,
     'rw_w1': 3.38,
     'rw_w2': 3.361,
     'rw_lnx_b': 8.0,
     'mla_q_norm_2': 8.0,
     'mla_kv_norm_2': 5.794,
     'swa_sinks_2': 8.0,
     'fox_b_f_2': 3.88}
    for name, (base, spread) in spreads.items():
        noise = np.random.default_rng([zlib.crc32(name.encode()), seed]).standard_normal(out[name].shape)
        drawn = base * np.exp(spread * noise) if base else spread * noise
        out[name] = __import__('jax').numpy.asarray(drawn.astype(out[name].dtype))
    for name, factor in factors.items():
        out[name] = (out[name] * factor).astype(out[name].dtype)
    return out
```

```python
import concourse.bass as bass
from concourse import mybir
from contextlib import ExitStack, contextmanager
import math
import numpy as np

D = 1024
KT = D // 128
NX, NC = 512, 256
NE = 16
CAPX, CAPC = 2 * NX // NE, 2 * NC // NE
HALF = 512
RING = 3
ADA_SLABS, FNET_SLABS, EXPERT_SLABS, RWKV_SLABS, LAYER_SLABS = 24, 4, 6, 10, 24
SLABS = ADA_SLABS + FNET_SLABS + 2 * NE * EXPERT_SLABS + RWKV_SLABS + 2 * LAYER_SLABS
CH = 64
GC = 4
HEADS = 4
TOPK = 128
NEG = -1e30
F_TILES = 18
TM_W = 652

VEC = {}
_n = 0
for _name, _w in [("c", 16), ("ada_b", 96), ("norm_g", 32), ("fnet_bo", 8), ("final_g", 8), ("mix", 48),
                  ("rwp", 72), ("router", 256), ("layer2", 54), ("final2", 8)]:
    VEC[_name] = (_n, _n + _w)
    _n += _w
NVEC = _n
TAB1 = {}
_n = 0
for _name, _w in [("ident", 128), ("ones", 128), ("headones", 128), ("iota_row", 96), ("iota_col", 1),
                  ("chunk", 256), ("level", 12 * 128), ("strict", 256), ("incl", 128)]:
    TAB1[_name] = (_n, _n + _w)
    _n += _w
NTAB1 = _n
TAB2 = {}
_n = 0
for _name, _w in [("cos64", 512), ("sin64", 512), ("cos32", 512), ("sin32", 512), ("rot64", 128), ("rot32", 128),
                  ("causal", 896), ("window", 896), ("upto", 896)]:
    TAB2[_name] = (_n, _n + _w)
    _n += _w
NTAB2 = _n

PER = {
    "expert_ctx": dict(slab=6, filled=26, fed=4, asked=2, answered=2),
    "expert": dict(slab=6, filled=18, fed=4, asked=2, answered=2),
    "pair": dict(slab=0, filled=238, fed=153, asked=10, answered=10),
    "layer": dict(slab=24, filled=335, fed=61, asked=22, answered=21),
    "ada": dict(slab=3, filled=0, fed=0, asked=0, answered=0),
}


class Tally:

    def __init__(self):
        self.n = 0
        self.loops = []

    def at(self, more=0):
        v = self.n + more
        for i, per in self.loops:
            v = i * per + v
        return v


class Side:

    def __init__(self, eng, K):
        self.eng, self.K = eng, K
        self.t = {k: Tally() for k in ("slab", "filled", "fed", "asked", "answered")}
        self.bank = 0

    def add(self, name):
        self.t[name].n += 1
        return 1

    def next(self, name):
        self.t[name].n += 1
        return self.t[name].at()

    def first_bank(self):
        self.bank = 0
        return self.t["filled"].at()

    def reuses(self):
        return self.bank >= 8

    def reused(self):
        return self.t["filled"].at(-7)

    def next_bank(self):
        self.bank += 1
        return self.K.banks[(self.bank - 1) % 8]

    def slot(self):
        return self.t["slab"].n % RING

    def landed(self):
        turn = self.t["slab"]
        v = 16 * (turn.n // RING + 1)
        for i, per in turn.loops:
            v = i * (16 * per // RING) + v
        return v

    def next_slab(self):
        self.t["slab"].n += 1
        return self.K.ring[(self.t["slab"].n - 1) % RING]

    @contextmanager
    def loop(self, name, turns):
        first = {k: t.n for k, t in self.t.items()}
        with self.eng.Fori(0, turns) as i:
            for k, t in self.t.items():
                t.loops.append((i, PER[name][k]))
            yield i
            for k, t in self.t.items():
                t.loops.pop()
                got = t.n - first[k]
                if got and got != PER[name][k]:
                    self.K.wrong.add((name, k, got))
                if got:
                    t.n = first[k] + PER[name][k] * turns


def build(nc, slabs_d, vecs_d, tabs1_d, tabs2_d, aux_d, x_d, ctx_d, out_d):
    f32 = mybir.dt.float32
    ALU = mybir.AluOpType
    ACT = mybir.ActivationFunctionType
    AX = mybir.AxisListType.X
    stack = ExitStack()
    with stack:
        def sb(name, shape):
            return stack.enter_context(nc.sbuf_tensor(name, shape, f32))

        def sem(name):
            return stack.enter_context(nc.semaphore(name))

        ring = [sb(f"ring{s}", [128, KT, HALF]) for s in range(RING)]
        resx, resc = sb("resx", [128, KT, NX]), sb("resc", [128, KT, NC])
        hx, hc = sb("hx", [128, KT, NX]), sb("hc", [128, KT, NC])
        vecs, tabs1 = sb("vecs_sb", [128, NVEC]), sb("tabs1_sb", [128, NTAB1])
        mod = sb("mod", [128, 2, 6, KT, 2])
        cs = sb("cs", [128, KT, 2])
        cell = sb("cell", [1, 1])[:, :]
        work = sb("work", [128, 24 * 1024])
        P = [stack.enter_context(nc.psum_tensor(f"bank{i}", [128, 512], f32)) for i in range(8)]

        slab_loaded = [sem(f"slab_loaded{s}") for s in range(RING)]
        slab_used, filled, drained, fed, mix_used = (sem(n) for n in ("slab_used", "filled", "drained", "fed", "mix_used"))
        asked, answered, tables_loaded, aux_loaded, stored = (sem(n) for n in ("asked", "answered", "tables_loaded", "aux_loaded", "stored"))

        class K:
            wrong = set()
            banks = P

        K.ring = ring

        def vec(name):
            return vecs[:, VEC[name][0]:VEC[name][1]]

        def tab(name):
            return tabs1[:, TAB1[name][0]:TAB1[name][1]]

        def cut(whole, at, *shape):
            n = math.prod(shape)
            v = whole[:, at:at + n]
            if len(shape) == 2:
                v = v.rearrange("p (a b) -> p a b", a=shape[0])
            if len(shape) == 3:
                v = v.rearrange("p (a b c) -> p a b c", a=shape[0], b=shape[1])
            return v

        def flat(t):
            return t[:, :, :].rearrange("p a b -> p (a b)")

        ident, ones, headones = tab("ident"), tab("ones"), tab("headones")
        levels = tab("level").rearrange("p (d l c) -> p d l c", d=2, l=6)
        strict = tab("strict").rearrange("p (d c) -> p d c", d=2)
        incl = tab("incl").rearrange("p (d c) -> p d c", d=2)
        norm_g = vec("norm_g").rearrange("p (l j k) -> p l j k", l=2, j=2)
        mixes = vec("mix").rearrange("p (j k) -> p j k", j=6)
        rwp = vec("rwp").rearrange("p (q j) -> p q j", q=KT)
        router = vec("router").rearrange("p (l k e) -> p l k e", l=2, k=KT)
        layer2 = vec("layer2").rearrange("p (l j) -> p l j", l=2)
        segx = (resx, hx, NX, 0)
        segc = (resc, hc, NC, 1)

        sqx, sqc = cut(work, 0, KT, NX), cut(work, KT * NX, KT, NC)
        rstd = cut(work, KT * (NX + NC), NX + NC)

        AB = cut(work, 0, 6, 4 * 512)

        htok = cut(work, 0, 6, D)
        o = 6 * D
        aff, o = cut(work, o, 6, NE), o + 6 * NE
        stok, o = cut(work, o, 6, NE), o + 6 * NE
        amax, o = cut(work, o, 6), o + 6
        affe, o = cut(work, o, 6), o + 6
        affT, o = cut(work, o, 768), o + 768
        left, o = cut(work, o, 768), o + 768
        slot, o = cut(work, o, 768), o + 768
        top8, o = cut(work, o, 8), o + 8
        pick, o = cut(work, o, 6, 96), o + 6 * 96
        esel, o = cut(work, o, 96), o + 96
        xsT, o = cut(work, o, KT, 96), o + KT * 96
        hid, o = cut(work, o, KT, 96), o + KT * 96
        gact, o = cut(work, o, 4, 96), o + 4 * 96
        put, o = cut(work, o, 768), o + 768
        gate, o = cut(work, o, 1), o + 1
        ys, o = cut(work, o, D), o + D
        ones768, o = cut(work, o, 768), o + 768

        Rx, o = cut(work, 0, KT, NX), KT * NX
        Kx, o = cut(work, o, KT, NX), o + KT * NX
        Vx, o = cut(work, o, KT, NX), o + KT * NX
        Kc, o = cut(work, o, KT, NC), o + KT * NC
        Vc, o = cut(work, o, KT, NC), o + KT * NC
        HW, o = cut(work, o, 768), o + 768
        HA, o = cut(work, o, 768), o + 768
        HG, o = cut(work, o, NX), o + NX
        rw0 = o
        diff = cut(work, o, 768)
        mixed = [cut(work, o + 768 * (j + 1), 768) for j in range(2)]
        bb, o = cut(work, o, GC, 128), o + 512
        kb, o = cut(work, o, GC, 128), o + 512
        vb, o = cut(work, o, GC, 128), o + 512
        NT, o = cut(work, o, GC, 128), o + 512
        MT, o = cut(work, o, GC, 128), o + 512
        QQ, o = cut(work, o, 2 * GC, CH), o + 512
        Bt, o = cut(work, o, GC, 128), o + 512
        Kt, o = cut(work, o, GC, 128), o + 512
        Vt, o = cut(work, o, GC, 128), o + 512
        XT, o = cut(work, o, GC, 128), o + 512
        assert o <= 24 * 1024
        kkv = work[:, rw0 + 3 * 512:rw0 + 3 * 512 + 768]
        ksq = work[:, rw0 + 6 * 512:rw0 + 6 * 512 + 768]
        ta, tb, tc = (work[:, rw0 + j * 512:rw0 + (j + 1) * 512] for j in (3, 4, 6))
        hxf, hcf, rcf = flat(hx), flat(hc), flat(resc)
        lw, av, kkn, kd = (hxf[:, j * 768:(j + 1) * 768] for j in range(4))
        Y, ksum = hxf[:, 3072:3584], hxf[:, 3584:4096]
        ar = hcf[:, 0:768].rearrange("p (c n) -> p c n", c=GC)
        Lc, E1, E3 = (hcf[:, 768 + j * 256:1024 + j * 256] for j in range(3))
        w2p, a2p, g2p = (hcf[:, 1536 + j * 128:1664 + j * 128] for j in range(3))
        ET, pp = hcf[:, 1920:1924], hcf[:, 1924:1934]
        G, U, Z = (rcf[:, j * 128:(j + 1) * 128] for j in range(3))
        NL, T, X = (rcf[:, 512 + j * 512:1024 + j * 512].rearrange("p (c n) -> p c n", c=GC) for j in range(3))

        tabs2 = cut(work, 0, NTAB2)
        o = NTAB2
        o2 = o

        def tab2(name):
            return tabs2[:, TAB2[name][0]:TAB2[name][1]]

        Fm, o = cut(work, o, F_TILES, NX), o + F_TILES * NX
        VT, o = cut(work, o, 4, TM_W), o + 4 * TM_W
        QN, o = cut(work, o, 2, NX), o + 2 * NX
        QR, o = cut(work, o, NX), o + NX
        KN, o = cut(work, o, 2, NX), o + 2 * NX
        VA, o = cut(work, o, 4, 256), o + 4 * 256
        S, o = cut(work, o, HEADS, NX), o + HEADS * NX
        PT, o = cut(work, o, HEADS, NX), o + HEADS * NX
        assert o <= 24 * 1024, o
        up = cut(work, o2, 32, NX)
        sq2 = cut(work, o2, KT, NX)
        score, rest, keep = Fm[:, 0, :], Fm[:, 1, :], Fm[:, 2, :]
        cumk = rcf.rearrange("p (h n) -> p h n", h=HEADS)
        aux = hcf[:, 0:1280]
        pv = hcf[:, 1280:1307]
        lf = hcf[:, 1312:1328].rearrange("p (j h) -> p j h", j=4)
        le = hcf[:, 1328:1344].rearrange("p (j h) -> p j h", j=4)
        mx, mxn, sums, esink = (hcf[:, 1344 + 4 * j:1348 + 4 * j] for j in range(4))
        t8 = hcf[:, 1360:1368]
        lfb = hcf[:, 1408:1920].rearrange("p (j n) -> p j n", j=4)
        rstd2 = PT[:, 0, :]
        OT = hx

        def heads(v):
            out = []
            for h in range(HEADS):
                r, r32 = 64 * (h % 2), 32 * h
                rows, rows32 = slice(r, r + 64), slice(r32, r32 + 32)
                if v == "mla":
                    out.append(([(QN, h // 2, KN, h // 2, rows), (QR, None, Fm, 16, rows32)],
                                (VA, 128 * (h // 2)), h // 2, rows))
                elif v == "swa":
                    out.append(([(Fm, 3 + h // 2, Fm, 5, rows)], (VT, 0), 2 + h // 2, rows))
                elif v == "dsa":
                    out.append(([(Fm, 6 + h // 2, Fm, 8 + h // 2, rows)], (VT, 128 + 128 * (h // 2)), 4 + h // 2, rows))
                else:
                    out.append(([(Fm, 12 + h // 2, Fm, 14 + h // 2, rows)], (VT, 384 + 128 * (h // 2)), 6 + h // 2, rows))
            return out

        SCALE = {"mla": 96 ** -0.5, "swa": 64 ** -0.5, "dsa": 64 ** -0.5, "fox": 64 ** -0.5}
        VARIANTS = ("mla", "swa", "dsa", "fox")
        ROPED = [(Fm, 3, 64), (Fm, 4, 64), (Fm, 5, 64), (Fm, 6, 64), (Fm, 7, 64), (Fm, 8, 64), (Fm, 9, 64),
                 (QR, None, 32), (Fm, 10, 32), (Fm, 11, 32), (Fm, 16, 32), (Fm, 17, 32)]

        def tile(t, j):
            return t if j is None else t[:, j, :]

        def span(v, i):
            return (128 * max(0, i - 1) if v == "swa" else 0), 128 * (i + 1)

        WALK = [(0, 0, (0, 1, 2, 3)), (0, 1, (0, 1, 2, 3)), (0, 2, (0, 1, 2, 3)),
                (1, 0, (3, 2, 1, 0)), (1, 2, (3, 2, 1, 0)), (1, 1, (3, 2, 1, 0))]
        W_MIX = [(1, "w", 1, 1), (4, "a", 1, 1), (5, "g", 1, 1), (0, "r", 4, 2), (2, "k", 4, 2), (3, "v", 4, 2)]

        block = stack.enter_context(nc.Block())

        @block.sync
        def _(sp):
            sp.dma_start(vecs[:, :], vecs_d).then_inc(tables_loaded, 16)
            sp.dma_start(tabs1[:, :], tabs1_d).then_inc(tables_loaded, 16)
            sp.dma_start(resx[:, :, :], x_d.rearrange("(k p) t -> p k t", p=128)).then_inc(tables_loaded, 16)
            sp.dma_start(resc[:, :, :], ctx_d.rearrange("(k p) t -> p k t", p=128)).then_inc(tables_loaded, 16)
            for s in range(RING):
                sp.dma_start(flat(ring[s]), slabs_d[s]).then_inc(slab_loaded[s], 16)
            rounds = SLABS // RING
            with sp.Fori(1, rounds) as i:
                for s in range(RING):
                    sp.wait_ge(slab_used, i * RING + (s - RING + 1))
                    sp.dma_start(flat(ring[s]), slabs_d[i * RING + s]).then_inc(slab_loaded[s], 16)
            for n in range(rounds * RING, SLABS):
                sp.wait_ge(slab_used, n - RING + 1)
                sp.dma_start(flat(ring[n % RING]), slabs_d[n]).then_inc(slab_loaded[n % RING], 16)

        @block.tensor
        def _(pe):
            me = Side(pe, K)
            t = me.t

            def mm(out, lhsT, rhs, k, n):
                return pe.matmul(out, lhsT, rhs, start=(k == 0), stop=(k == n - 1))

            def square_sums(parts):
                pe.wait_ge(fed, me.next("fed"))
                pe.wait_ge(drained, me.first_bank())
                for sq, n, w in parts:
                    if me.reuses():
                        pe.wait_ge(drained, me.reused())
                    b = me.next_bank()
                    for k in range(n):
                        m = mm(b[:, 0:w], ones, sq[:, k, 0:w], k, n)
                    m.then_inc(filled, me.add("filled"))

            def transposed(parts):
                if me.reuses():
                    pe.wait_ge(drained, me.reused())
                b = me.next_bank()
                for in_, rows, at in parts:
                    m = pe.transpose(b[0:in_.shape[1], at:at + rows], in_, ident[0:rows, 0:rows])
                m.then_inc(filled, me.add("filled"))

            def dense(src, segs, then=None):
                pe.wait_ge(slab_loaded[me.slot()], me.landed())
                w = me.next_slab()
                for j in range(4):
                    for h, n in segs:
                        if me.reuses():
                            pe.wait_ge(drained, me.reused())
                        b = me.next_bank()
                        for k in range(KT):
                            m = mm(b[:, 0:n], w[:, k, j * 128:(j + 1) * 128], h[:, k, :], k, KT)
                        m.then_inc(filled, me.add("filled"))
                pe.drain().then_inc(slab_used, 1)

            pe.wait_ge(tables_loaded, 64)
            pe.wait_ge(answered, 1)
            with me.loop("ada", ADA_SLABS // RING) as i:
                for s in range(RING):
                    pe.wait_ge(slab_loaded[me.slot()], me.landed())
                    w = me.next_slab()
                    for j in range(4):
                        for k in range(KT):
                            m = mm(P[0][:, bass.ds(i * 8 * RING + 8 * s + 2 * j, 2)],
                                   w[:, k, j * 128:(j + 1) * 128], cs[:, k, :], k, KT)
                    m.then_inc(slab_used, 1)
            pe.drain().then_inc(filled, me.add("filled"))

            square_sums([(sqx, KT, NX), (sqc, KT, NC)])
            pe.wait_ge(fed, me.next("fed"))
            pe.wait_ge(drained, me.first_bank())
            pe.wait_ge(slab_loaded[me.slot()], me.landed())
            w = me.next_slab()
            wf = w[:, :, :].rearrange("p a b -> p (a b)")
            for tt in range(6):
                for g in range(4):
                    if me.reuses():
                        pe.wait_ge(drained, me.reused())
                    b = me.next_bank()
                    for k in range(2):
                        src = hx[:, 2 * g + k, tt * 128:(tt + 1) * 128] if tt < 4 else hc[:, 2 * g + k, (tt - 4) * 128:(tt - 3) * 128]
                        m = mm(b[:, :], src, wf[:, 512 * k:512 * k + 512], k, 2)
                    m.then_inc(filled, me.add("filled"))
            pe.wait_ge(fed, me.next("fed"))
            pe.wait_ge(drained, me.first_bank())
            pe.wait_ge(slab_loaded[me.slot()], me.landed())
            wx = me.next_slab()
            for f in range(KT):
                g, half = f // 2, f % 2
                for seg, tiles in ((0, range(0, 4)), (1, range(4, 6))):
                    if me.reuses():
                        pe.wait_ge(drained, me.reused())
                    b = me.next_bank()
                    n = 0
                    for part in range(2):
                        for j, tt in enumerate(tiles):
                            at = g * 512 + part * 256 + half * 128
                            if seg == 0:
                                rhs, wdt = wx[:, part * 4 + j, :], NX
                            else:
                                rhs, wdt = wf[:, 1024 + (part * 2 + j) * 256:1024 + (part * 2 + j + 1) * 256], NC
                            m = mm(b[:, 0:wdt], AB[:, tt, at:at + 128], rhs, n, 2 * len(tiles))
                            n += 1
                    m.then_inc(filled, me.add("filled"))
            pe.drain().then_inc(slab_used, 2)
            pe.wait_ge(fed, me.next("fed"))
            pe.wait_ge(drained, me.first_bank())
            for _ in range(2):
                dense(None, [(hx, NX), (hc, NC)])

            def moe(l, ctx):
                tiles = 6 if ctx else 4
                S_ = CAPX + CAPC if ctx else CAPX
                W = NX + NC * ctx
                square_sums([(sqx, KT, NX)] + [(sqc, KT, NC)] * ctx)
                pe.wait_ge(fed, me.next("fed"))
                pe.wait_ge(drained, me.first_bank())

                def htile(k, tt):
                    return hx[:, k, tt * 128:(tt + 1) * 128] if tt < 4 else hc[:, k, (tt - 4) * 128:(tt - 3) * 128]

                if me.reuses():
                    pe.wait_ge(drained, me.reused())
                b = me.next_bank()
                for tt in range(tiles):
                    for k in range(KT):
                        m = mm(b[:, tt * NE:(tt + 1) * NE], htile(k, tt), router[:, l, k, :], k, KT)
                m.then_inc(filled, me.add("filled"))
                for tt in range(tiles):
                    for half in range(2):
                        transposed([(htile(4 * half + j, tt), 128, 128 * j) for j in range(4)])
                pe.wait_ge(fed, me.next("fed"))
                transposed([(aff[:, tt, :], 128, 128 * tt) for tt in range(4)])
                if ctx:
                    transposed([(aff[:, tt, :], 128, 128 * (tt - 4)) for tt in range(4, 6)])
                pe.wait_ge(fed, me.next("fed"))
                if me.reuses():
                    pe.wait_ge(drained, me.reused())
                b = me.next_bank()
                for tt in range(tiles):
                    m = pe.transpose(b[:, tt * NE:(tt + 1) * NE], slot[0:NE, tt * 128:(tt + 1) * 128], ident[0:NE, 0:NE])
                m.then_inc(filled, me.add("filled"))
                with me.loop("expert_ctx" if ctx else "expert", NE):
                    pe.wait_ge(fed, me.next("fed"))
                    pe.wait_ge(drained, me.first_bank())
                    for half in range(2):
                        if me.reuses():
                            pe.wait_ge(drained, me.reused())
                        b = me.next_bank()
                        for j in range(4):
                            f = 4 * half + j
                            for tt in range(tiles):
                                m = mm(b[:, j * S_:(j + 1) * S_], htok[:, tt, f * 128:(f + 1) * 128], pick[:, tt, 0:S_], tt, tiles)
                        if half:
                            for tt in range(tiles):
                                m = mm(b[0:S_, 4 * S_:4 * S_ + 1], pick[:, tt, 0:S_], affe[:, tt:tt + 1], tt, tiles)
                        m.then_inc(filled, me.add("filled"))
                    if me.reuses():
                        pe.wait_ge(drained, me.reused())
                    b = me.next_bank()
                    mm(b[0:S_, 0:NX], esel[0:NE, 0:S_], slot[0:NE, 0:NX], 0, 1).then_inc(filled, me.add("filled"))
                    if me.reuses():
                        pe.wait_ge(drained, me.reused())
                    b = me.next_bank()
                    n = NC if ctx else 1
                    mm(b[0:S_, 0:n], esel[0:NE, 0:S_], slot[0:NE, W - n:W], 0, 1).then_inc(filled, me.add("filled"))
                    pe.wait_ge(fed, me.next("fed"))
                    for j in range(2):
                        for _ in range(2):
                            pe.wait_ge(slab_loaded[me.slot()], me.landed())
                            w = me.next_slab()
                            if me.reuses():
                                pe.wait_ge(drained, me.reused())
                            b = me.next_bank()
                            for m4 in range(4):
                                for k in range(KT):
                                    m = mm(b[:, m4 * S_:(m4 + 1) * S_], w[:, k, m4 * 128:(m4 + 1) * 128], xsT[:, k, 0:S_], k, KT)
                            m.then_inc(filled, me.add("filled"))
                            pe.drain().then_inc(slab_used, 1)
                    pe.wait_ge(fed, me.next("fed"))
                    for half in range(2):
                        pe.wait_ge(slab_loaded[me.slot()], me.landed())
                        w = me.next_slab()
                        if me.reuses():
                            pe.wait_ge(drained, me.reused())
                        b = me.next_bank()
                        for k in range(KT):
                            m = mm(b[0:S_, :], hid[:, k, 0:S_], w[:, k, :], k, KT)
                        m.then_inc(filled, me.add("filled"))
                        pe.drain().then_inc(slab_used, 1)
                    pe.wait_ge(fed, me.next("fed"))
                    for f in range(KT):
                        if me.reuses():
                            pe.wait_ge(drained, me.reused())
                        b = me.next_bank()
                        mm(b[:, 0:NX], ys[0:S_, f * 128:(f + 1) * 128], put[0:S_, 0:NX], 0, 1).then_inc(filled, me.add("filled"))
                        if ctx:
                            if me.reuses():
                                pe.wait_ge(drained, me.reused())
                            b = me.next_bank()
                            mm(b[:, 0:NC], ys[0:S_, f * 128:(f + 1) * 128], put[0:S_, NX:NX + NC], 0, 1).then_inc(filled, me.add("filled"))

            moe(0, True)

            square_sums([(sqx, KT, NX), (sqc, KT, NC)])
            pe.wait_ge(slab_loaded[me.slot()], me.landed())
            lora = me.next_slab()
            for j, what, mt, ns in W_MIX:
                segs = [(256, NX)] if what in "rg" else [(256, NX), (0, NC)]
                for half in range(ns):
                    if what in "wag":
                        w, first = lora, 128 * "wag".index(what)
                    else:
                        pe.wait_ge(slab_loaded[me.slot()], me.landed())
                        w, first = me.next_slab(), 0
                    pe.wait_ge(drained, me.first_bank())
                    banks = {(m4, at): me.next_bank() for m4 in range(mt) for at, _ in segs}
                    for k in range(KT):
                        pe.wait_ge(fed, me.next("fed"))
                        for m4 in range(mt):
                            for at, n in segs:
                                m = mm(banks[m4, at][:, 0:n], w[:, k, first + m4 * 128:first + (m4 + 1) * 128],
                                       mixed[k % 2][:, at:at + n], k, KT)
                                if k == KT - 1:
                                    m.then_inc(filled, me.add("filled"))
                        if k < KT - 1:
                            m.then_inc(mix_used, 1)
                    if what not in "wa":
                        pe.drain().then_inc(slab_used, 1)
            pe.wait_ge(slab_loaded[me.slot()], me.landed())
            me.next_slab()
            with me.loop("pair", KT):
                pe.wait_ge(fed, me.next("fed"))
                pe.wait_ge(drained, me.first_bank())
                for a, n in ((0, NC), (NC, NX)):
                    if me.reuses():
                        pe.wait_ge(drained, me.reused())
                    b = me.next_bank()
                    mm(b[:, 0:n], headones, ksq[:, a:a + n], 0, 1).then_inc(filled, me.add("filled"))
                for d, g, chunks in WALK:
                    x = g > 0
                    if g == 0:
                        pe.wait_ge(drained, me.first_bank())
                        rows = slice(64 * d, 64 * d + 64)
                        for lhsT, rhs in ((w2p, HW), (a2p, HA)):
                            for a, n in ((0, NC), (NC, NX)):
                                if me.reuses():
                                    pe.wait_ge(drained, me.reused())
                                b = me.next_bank()
                                mm(b[:, 0:n], lhsT[rows, :], rhs[rows, a:a + n], 0, 1).then_inc(filled, me.add("filled"))
                    pe.wait_ge(fed, me.next("fed"))
                    pe.wait_ge(drained, me.first_bank())
                    if me.reuses():
                        pe.wait_ge(drained, me.reused())
                    b = me.next_bank()
                    for c in range(GC):
                        m = mm(b[:, c * 128:(c + 1) * 128], bb[:, c, :], ar[:, c, 0:128], 0, 1)
                    m.then_inc(filled, me.add("filled"))
                    if me.reuses():
                        pe.wait_ge(drained, me.reused())
                    b = me.next_bank()
                    for c in range(GC):
                        m = mm(b[:, c * 128:(c + 1) * 128], kb[:, c, :], ar[:, c, 0:128], 0, 1)
                    m.then_inc(filled, me.add("filled"))
                    if x:
                        if me.reuses():
                            pe.wait_ge(drained, me.reused())
                        b = me.next_bank()
                        for c in range(GC):
                            for q, l_ in enumerate((bb, kb)):
                                at = (q * GC + c) * CH
                                m = mm(b[:, at:at + CH], l_[:, c, :], ar[:, c, 128:192], 0, 1)
                        m.then_inc(filled, me.add("filled"))
                    for src in (bb, kb, vb):
                        transposed([(src[:, c, :], 128, 128 * c) for c in range(GC)])
                    for l in range(6):
                        pe.wait_ge(fed, me.next("fed"))
                        if me.reuses():
                            pe.wait_ge(drained, me.reused())
                        b = me.next_bank()
                        for c in range(GC):
                            m = mm(b[:, c * 128:(c + 1) * 128], NL[:, c, :], X[:, c, :], 0, 1)
                        m.then_inc(filled, me.add("filled"))
                        pe.wait_ge(fed, me.next("fed"))
                        if l < 5:
                            if me.reuses():
                                pe.wait_ge(drained, me.reused())
                            b = me.next_bank()
                            for c in range(GC):
                                m = mm(b[:, c * 128:(c + 1) * 128], XT[:, c, :], T[:, c, :], 0, 1)
                            m.then_inc(filled, me.add("filled"))
                        if me.reuses():
                            pe.wait_ge(drained, me.reused())
                        b = me.next_bank()
                        for c in range(GC):
                            m = mm(b[:, c * 128:(c + 1) * 128], T[:, c, :], XT[:, c, :], 0, 1)
                        m.then_inc(filled, me.add("filled"))
                    for c in chunks:
                        pe.wait_ge(fed, me.next("fed"))
                        if me.reuses():
                            pe.wait_ge(drained, me.reused())
                        b = me.next_bank()
                        mm(b[:, 0:128], ar[:, c, 0:128], Z, 0, 2)
                        mm(b[:, 0:128], MT[:, c, :], Vt[:, c, :], 1, 2).then_inc(filled, me.add("filled"))
                        pe.wait_ge(fed, me.next("fed"))
                        if me.reuses():
                            pe.wait_ge(drained, me.reused())
                        b = me.next_bank()
                        mm(b[:, 0:128], XT[:, c, :], G, 0, 1).then_inc(filled, me.add("filled"))
                        pe.wait_ge(fed, me.next("fed"))
                        if x:
                            if me.reuses():
                                pe.wait_ge(drained, me.reused())
                            b = me.next_bank()
                            mm(b[:, 0:CH], Z, ar[:, c, 128:192], 0, 3)
                            mm(b[:, 0:CH], U, QQ[:, c, :], 1, 3)
                            mm(b[:, 0:CH], Vt[:, c, :], QQ[:, GC + c, :], 2, 3).then_inc(filled, me.add("filled"))
                        if me.reuses():
                            pe.wait_ge(drained, me.reused())
                        b = me.next_bank()
                        mm(b[:, 0:128], Bt[:, c, :], U, 0, 2)
                        mm(b[:, 0:128], Kt[:, c, :], Vt[:, c, :], 1, 2).then_inc(filled, me.add("filled"))
                pe.wait_ge(fed, me.next("fed"))
                pe.wait_ge(drained, me.first_bank())
                if me.reuses():
                    pe.wait_ge(drained, me.reused())
                b = me.next_bank()
                mm(b[:, :], headones, Y, 0, 1).then_inc(filled, me.add("filled"))
                if me.reuses():
                    pe.wait_ge(drained, me.reused())
                b = me.next_bank()
                mm(b[:, :], headones, tb, 0, 1).then_inc(filled, me.add("filled"))
                if me.reuses():
                    pe.wait_ge(drained, me.reused())
                b = me.next_bank()
                mm(b[:, :], g2p, HG, 0, 1).then_inc(filled, me.add("filled"))
                pe.wait_ge(fed, me.next("fed"))
                if me.reuses():
                    pe.wait_ge(drained, me.reused())
                b = me.next_bank()
                mm(b[:, :], headones, tc, 0, 1).then_inc(filled, me.add("filled"))
            pe.wait_ge(fed, me.next("fed"))
            pe.wait_ge(drained, me.first_bank())
            for _ in range(2):
                dense(None, [(Rx, NX)])
            moe(1, False)
            square_sums([(sqx, KT, NX)])

            with me.loop("layer", 2):
                square_sums([(sq2, KT, NX)])
                pe.wait_ge(fed, me.next("fed"))
                pe.wait_ge(drained, me.first_bank())
                for sl in range(5):
                    pe.wait_ge(slab_loaded[me.slot()], me.landed())
                    w = me.next_slab()
                    for j in range(4 if sl < 4 else 2):
                        if me.reuses():
                            pe.wait_ge(drained, me.reused())
                        b = me.next_bank()
                        for k in range(KT):
                            m = mm(b[:, :], w[:, k, j * 128:(j + 1) * 128], hx[:, k, :], k, KT)
                        m.then_inc(filled, me.add("filled"))
                    if sl < 4:
                        pe.drain().then_inc(slab_used, 1)
                pe.wait_ge(slab_loaded[me.slot()], me.landed())
                w5 = me.next_slab()
                for ww, c0, n in ((w, 256, 256), (w5, 0, TM_W - 256)):
                    for tt in range(4):
                        if me.reuses():
                            pe.wait_ge(drained, me.reused())
                        b = me.next_bank()
                        for k in range(KT):
                            m = mm(b[:, 0:n], hx[:, k, tt * 128:(tt + 1) * 128], ww[:, k, c0:c0 + n], k, KT)
                        m.then_inc(filled, me.add("filled"))
                pe.drain().then_inc(slab_used, 2)
                pe.wait_ge(fed, me.next("fed"))
                pe.wait_ge(drained, me.first_bank())
                for tiles in ((0, 1), (2,)):
                    if me.reuses():
                        pe.wait_ge(drained, me.reused())
                    b = me.next_bank()
                    for k, j in enumerate(tiles):
                        m = mm(b[:, :], ones, S[:, j, :], k, len(tiles))
                    m.then_inc(filled, me.add("filled"))
                pe.wait_ge(fed, me.next("fed"))
                uq = aux[:, 0:768].rearrange("p (k n) -> p k n", k=2)
                ukv = aux[:, 768:1280]
                for j in range(3):
                    if me.reuses():
                        pe.wait_ge(drained, me.reused())
                    b = me.next_bank()
                    for k in range(2):
                        m = mm(b[:, :], uq[:, k, j * 128:(j + 1) * 128], Fm[:, k, :], k, 2)
                    m.then_inc(filled, me.add("filled"))
                for j in range(2):
                    if me.reuses():
                        pe.wait_ge(drained, me.reused())
                    b = me.next_bank()
                    mm(b[:, :], ukv[:, j * 128:(j + 1) * 128], Fm[:, 2, :], 0, 1).then_inc(filled, me.add("filled"))
                for tt in range(4):
                    if me.reuses():
                        pe.wait_ge(drained, me.reused())
                    b = me.next_bank()
                    mm(b[:, 0:256], Fm[:, 2, tt * 128:(tt + 1) * 128], ukv[:, 256:512], 0, 1).then_inc(filled, me.add("filled"))
                pe.wait_ge(fed, me.next("fed"))
                pe.wait_ge(drained, me.first_bank())
                for tl, j, d in ROPED:
                    if me.reuses():
                        pe.wait_ge(drained, me.reused())
                    b = me.next_bank()
                    mm(b[:, :], tab2(f"rot{d}"), tile(tl, j), 0, 1).then_inc(filled, me.add("filled"))
                for h in range(HEADS):
                    pe.wait_ge(fed, me.next("fed"))
                    if me.reuses():
                        pe.wait_ge(drained, me.reused())
                    b = me.next_bank()
                    for j in range(4):
                        at = 384 - 128 * j
                        m = mm(b[:, :], lfb[:, j, :], tab2("upto")[:, at:at + NX], j, 4)
                    m.then_inc(filled, me.add("filled"))
                for v in VARIANTS:
                    for i in range(4):
                        k0, k1 = span(v, i)
                        q = slice(128 * i, 128 * i + 128)
                        pe.wait_ge(fed, me.next("fed"))
                        pe.wait_ge(drained, me.first_bank())
                        if v == "dsa" and i > 0:
                            for h in range(8):
                                rows = slice(32 * (h % 4), 32 * (h % 4) + 32)
                                if me.reuses():
                                    pe.wait_ge(drained, me.reused())
                                b = me.next_bank()
                                mm(b[:, 0:k1], Fm[rows, 10 + h // 4, q], Fm[rows, 17, 0:k1], 0, 1).then_inc(filled, me.add("filled"))
                        for parts, _, _, _ in heads(v):
                            for qt, qj, kt_, kj, rows in parts:
                                if me.reuses():
                                    pe.wait_ge(drained, me.reused())
                                b = me.next_bank()
                                mm(b[:, 0:k1 - k0], tile(qt, qj)[rows, q], tile(kt_, kj)[rows, k0:k1], 0, 1).then_inc(filled, me.add("filled"))
                        pe.wait_ge(fed, me.next("fed"))
                        for h in range(HEADS):
                            transposed([(S[:, h, a:a + 128], 128, a) for a in range(0, k1 - k0, 128)])
                        pe.wait_ge(fed, me.next("fed"))
                        for h, (_, (vt, vc), _, _) in enumerate(heads(v)):
                            if me.reuses():
                                pe.wait_ge(drained, me.reused())
                            b = me.next_bank()
                            nk = (k1 - k0) // 128
                            for kk in range(nk):
                                m = mm(b[:, 0:128], vt[:, k0 // 128 + kk, vc:vc + 128], PT[:, h, kk * 128:(kk + 1) * 128], kk, nk)
                            m.then_inc(filled, me.add("filled"))
                pe.wait_ge(fed, me.next("fed"))
                pe.wait_ge(drained, me.first_bank())
                for _ in range(2):
                    dense(None, [(OT, NX)])
                square_sums([(sq2, KT, NX)])
                pe.wait_ge(fed, me.next("fed"))
                pe.wait_ge(drained, me.first_bank())
                for _ in range(8):
                    dense(None, [(hx, NX)])
                pe.wait_ge(fed, me.next("fed"))
                pe.wait_ge(drained, me.first_bank())
                for half in range(2):
                    banks = [me.next_bank() for _ in range(4)]
                    for kg in range(4):
                        pe.wait_ge(slab_loaded[me.slot()], me.landed())
                        w = me.next_slab()
                        for j in range(4):
                            for k in range(KT):
                                m = mm(banks[j][:, :], w[:, k, j * 128:(j + 1) * 128], up[:, kg * KT + k, :], kg * KT + k, 32)
                            if kg == 3:
                                m.then_inc(filled, me.add("filled"))
                        pe.drain().then_inc(slab_used, 1)
            square_sums([(sq2, KT, NX)])

        @block.scalar
        def _(act):
            me = Side(act, K)
            t = me.t

            def root(x):
                act.wait_ge(asked, me.next("asked"))
                act.activation(x, x, ACT.Sqrt)
                act.drain().then_inc(answered, me.add("answered"))

            act.wait_ge(tables_loaded, 64)
            act.activation(cs[:, :, :], vec("c").rearrange("p (k j) -> p k j", j=2), ACT.Silu)
            act.drain().then_inc(answered, me.add("answered"))
            root(rstd)

            def moe(l, ctx):
                tiles = 6 if ctx else 4
                S_ = CAPX + CAPC if ctx else CAPX
                root(rstd[:, 0:NX + NC * ctx])
                act.wait_ge(asked, me.next("asked"))
                act.activation(aff[:, 0:tiles, :], aff[:, 0:tiles, :], ACT.Exp)
                act.drain().then_inc(answered, me.add("answered"))
                with me.loop("expert_ctx" if ctx else "expert", NE):
                    for j in range(2):
                        act.wait_ge(asked, me.next("asked"))
                        act.activation(gact[:, :, 0:S_], P[4 + 2 * j][:, 0:4 * S_].rearrange("p (a b) -> p a b", a=4), ACT.Silu)
                        act.drain().then_inc(answered, me.add("answered"))

            moe(0, True)
            root(rstd)
            for what, dst in (("w", HW), ("g", HG)):
                act.wait_ge(asked, me.next("asked"))
                if what == "w":
                    act.activation(HW[:, NC:NC + NX], P[0][:, :], ACT.Tanh)
                    act.activation(HW[:, 0:NC], P[1][:, 0:NC], ACT.Tanh)
                else:
                    act.activation(HG, P[0][:, :], ACT.Sigmoid)
                act.drain().then_inc(answered, me.add("answered"))
            with me.loop("pair", KT):
                root(ksq)
                for d, g, chunks in WALK:
                    if g == 0:
                        act.wait_ge(asked, me.next("asked"))
                        for q, dst in ((0, lw), (1, av)):
                            act.activation(dst[:, 0:NC], P[2 * q][:, 0:NC], ACT.Sigmoid, bias=pp[:, 2 * q + d:2 * q + d + 1])
                            act.activation(dst[:, NC:NC + NX], P[2 * q + 1][:, :], ACT.Sigmoid, bias=pp[:, 2 * q + d:2 * q + d + 1])
                        act.drain().then_inc(answered, me.add("answered"))
                    act.wait_ge(asked, me.next("asked"))
                    act.activation(E1, E1, ACT.Exp)
                    act.activation(E3, Lc, ACT.Exp, scale=-1.0)
                    act.activation(ET, ET, ACT.Exp)
                    act.drain()
                    act.activation(Lc, Lc, ACT.Exp)
                    act.drain().then_inc(answered, me.add("answered"))
                root(ta)
            moe(1, False)
            root(rstd[:, 0:NX])

            act.wait_ge(asked, me.next("asked"))
            act.dma_start(tabs2, tabs2_d).then_inc(tables_loaded, 16)
            with me.loop("layer", 2) as l:
                act.wait_ge(asked, me.next("asked"))
                act.dma_start(aux, aux_d[l]).then_inc(aux_loaded, 16)
                root(rstd2)
                root(S[:, 0:2, :])
                act.wait_ge(asked, me.next("asked"))
                act.activation(le, le, ACT.Exp)
                act.drain().then_inc(answered, me.add("answered"))
                act.wait_ge(asked, me.next("asked"))
                act.activation(le, le, ACT.Ln)
                act.drain().then_inc(answered, me.add("answered"))
                for v in VARIANTS:
                    for i in range(4):
                        n = span(v, i)[1] - span(v, i)[0]
                        act.wait_ge(asked, me.next("asked"))
                        for h in range(HEADS):
                            act.activation(S[:, h, 0:n], S[:, h, 0:n], ACT.Exp, bias=mxn[:, h:h + 1], accum_out=sums[:, h:h + 1])
                        if v == "swa":
                            act.activation(esink, esink, ACT.Exp)
                        act.drain().then_inc(answered, me.add("answered"))
                root(rstd2)
            root(rstd2)
            act.wait_ge(asked, me.next("asked"))
            act.dma_start(out_d.rearrange("(k p) t -> p k t", p=128), hx[:, :, :]).then_inc(stored, 16)
            act.wait_ge(stored, 16)

        @block.vector
        def _(v):
            me = Side(v, K)
            t = me.t

            def pass_on():
                v.memset(cell, 0.0)

            def tt(out, a, b, op):
                v.tensor_tensor(out, a, b, op)

            def ts(out, a, s1, op0, s2=None, op1=None):
                if op1 is None:
                    v.tensor_scalar(out, a, s1, None, op0)
                else:
                    v.tensor_scalar(out, a, s1, s2, op0, op1)

            def stt(out, a, s, b, op0, op1):
                v.scalar_tensor_tensor(out, a, s, b, op0, op1)

            def bc(x, *shape):
                return x.to_broadcast(list(shape))

            def inverse_roots(parts, root, eps):
                at = 0
                for w, n in parts:
                    v.wait_ge(filled, me.next("filled"))
                    b = me.next_bank()
                    ts(root[:, at:at + w], b[:, 0:w], 1.0 / n, ALU.mult, eps, ALU.add)
                    v.drain().then_inc(drained, 1)
                    at += w
                v.drain().then_inc(asked, me.add("asked"))
                v.wait_ge(answered, me.next("answered"))
                v.reciprocal(root[:, 0:at], root[:, 0:at])
                v.drain()

            def norm(segs, sqs, root, gains):
                for (res, h, n, j), sq in zip(segs, sqs):
                    tt(sq, res[:, :, :], res[:, :, :], ALU.mult)
                v.drain().then_inc(fed, me.add("fed"))
                me.first_bank()
                inverse_roots([(s[2], D) for s in segs], root, 1e-6)
                at = 0
                for res, h, n, j in segs:
                    tt(h[:, :, :], res[:, :, :], bc(root[:, at:at + n].unsqueeze(1), 128, KT, n), ALU.mult)
                    at += n
                v.drain()
                for res, h, n, j in segs:
                    for k in range(KT):
                        gain, shift = gains(k, j)
                        if shift is None:
                            ts(h[:, k, :], h[:, k, :], gain, ALU.mult)
                        else:
                            ts(h[:, k, :], h[:, k, :], gain, ALU.mult, shift, ALU.add)

            def modulated(l, which):
                return lambda k, j: (mod[:, l, 3 * which + 1, k, j:j + 1], mod[:, l, 3 * which, k, j:j + 1])

            v.wait_ge(tables_loaded, 64)
            t["answered"].n += 1
            v.wait_ge(filled, me.next("filled"))
            b = me.next_bank()
            mods = mod[:, :, :, :, :].rearrange("p l j k c -> p (l j k) c")
            tt(mods, b[:, 0:192].rearrange("p (q c) -> p q c", c=2), bc(vec("ada_b").unsqueeze(2), 128, 96, 2), ALU.add)
            v.drain().then_inc(drained, 1)
            for l in range(2):
                for j in range(2):
                    m = mod[:, l, 3 * j + 1, :, :]
                    stt(m, m, 1.0, bc(norm_g[:, l, j, :].unsqueeze(2), 128, KT, 2), ALU.add, ALU.mult)
            v.drain()

            norm([segx, segc], [sqx, sqc], rstd, modulated(0, 0))
            v.drain().then_inc(fed, me.add("fed"))
            me.first_bank()
            for tile_ in range(6):
                for g in range(4):
                    v.wait_ge(filled, me.next("filled"))
                    b = me.next_bank()
                    v.tensor_copy(AB[:, tile_, g * 512:(g + 1) * 512], b[:, :])
                    v.drain().then_inc(drained, 1)
            v.drain().then_inc(fed, me.add("fed"))
            me.first_bank()
            for f in range(KT):
                for h, n in ((hx, NX), (hc, NC)):
                    v.wait_ge(filled, me.next("filled"))
                    b = me.next_bank()
                    v.tensor_copy(h[:, f, :], b[:, 0:n])
                    v.drain().then_inc(drained, 1)
            v.drain().then_inc(fed, me.add("fed"))
            me.first_bank()
            tmp = cut(work, 0, NX)
            for f in range(KT):
                for res, h, n, j in (segx, segc):
                    v.wait_ge(filled, me.next("filled"))
                    b = me.next_bank()
                    ts(tmp[:, 0:n], b[:, 0:n], vec("fnet_bo")[:, f:f + 1], ALU.add, mod[:, 0, 2, f, j:j + 1], ALU.mult)
                    v.drain().then_inc(drained, 1)
                    tt(res[:, f, :], res[:, f, :], tmp[:, 0:n], ALU.add)
                    v.drain()

            def moe(l, ctx):
                tiles = 6 if ctx else 4
                S_ = CAPX + CAPC if ctx else CAPX
                W = NX + NC * ctx
                segs = [segx, segc] if ctx else [segx]
                norm(segs, [sqx, sqc], rstd, modulated(l, 1))
                v.drain().then_inc(fed, me.add("fed"))
                me.first_bank()
                v.wait_ge(filled, me.next("filled"))
                b = me.next_bank()
                lg = b[:, 0:tiles * NE].rearrange("p (t e) -> p t e", e=NE)
                af, am = aff[:, 0:tiles, :], amax[:, 0:tiles]
                v.tensor_reduce(am, lg, AX, ALU.max)
                v.drain()
                tt(af, lg, bc(am.unsqueeze(2), 128, tiles, NE), ALU.subtract)
                v.drain().then_inc(drained, 1)
                v.drain().then_inc(asked, me.add("asked"))
                v.wait_ge(answered, me.next("answered"))
                v.tensor_reduce(am, af, AX, ALU.add)
                v.drain()
                v.reciprocal(am, am)
                v.drain()
                tt(af, af, bc(am.unsqueeze(2), 128, tiles, NE), ALU.mult)
                v.drain().then_inc(fed, me.add("fed"))
                for tile_ in range(tiles):
                    for half in range(2):
                        v.wait_ge(filled, me.next("filled"))
                        b = me.next_bank()
                        v.tensor_copy(htok[:, tile_, half * 512:(half + 1) * 512], b[:, :])
                        v.drain().then_inc(drained, 1)
                v.wait_ge(filled, me.next("filled"))
                b = me.next_bank()
                v.tensor_copy(affT[0:NE, 0:NX], b[0:NE, :])
                v.drain().then_inc(drained, 1)
                if ctx:
                    v.wait_ge(filled, me.next("filled"))
                    b = me.next_bank()
                    v.tensor_copy(affT[0:NE, NX:W], b[0:NE, 0:NC])
                    v.drain().then_inc(drained, 1)
                v.memset(ones768[0:NE, 0:W], 1.0)
                v.tensor_copy(left[0:NE, 0:W], affT[0:NE, 0:W])
                for a, n, cap, first in ((0, NX, CAPX, 0.0), (NX, NC, CAPC, float(CAPX)))[:1 + ctx]:
                    part = left[0:NE, a:a + n]
                    for _ in range(cap // 8):
                        v.drain()
                        v.max(top8[0:NE, :], part)
                        v.drain()
                        v.match_replace(part, top8[0:NE, :], part, -1.0)
                v.drain()
                ts(left[0:NE, 0:W], left[0:NE, 0:W], -1.0, ALU.is_equal)
                v.drain()
                for a, n, first in ((0, NX, 0.0), (NX, NC, float(CAPX)))[:1 + ctx]:
                    v.tensor_tensor_scan(slot[0:NE, a:a + n], ones768[0:NE, a:a + n], left[0:NE, a:a + n], first, ALU.mult, ALU.add)
                v.drain()
                tt(slot[0:NE, 0:W], slot[0:NE, 0:W], left[0:NE, 0:W], ALU.mult)
                v.drain()
                ts(slot[0:NE, 0:W], slot[0:NE, 0:W], -1.0, ALU.add)
                v.drain().then_inc(fed, me.add("fed"))
                v.wait_ge(filled, me.next("filled"))
                b = me.next_bank()
                v.tensor_copy(stok[:, 0:tiles, :], b[:, 0:tiles * NE].rearrange("p (t e) -> p t e", e=NE))
                v.drain().then_inc(drained, 1)
                with me.loop("expert_ctx" if ctx else "expert", NE) as e:
                    me.first_bank()
                    tt(pick[:, 0:tiles, 0:S_], bc(tab("iota_row")[:, 0:S_].unsqueeze(1), 128, tiles, S_),
                       bc(stok[:, 0:tiles, bass.ds(e, 1)], 128, tiles, S_), ALU.is_equal)
                    v.tensor_copy(esel[0:NE, 0:S_], bc(ident[0:NE, bass.ds(e, 1)], NE, S_))
                    v.tensor_copy(affe[:, 0:tiles].unsqueeze(2), aff[:, 0:tiles, bass.ds(e, 1)])
                    v.drain().then_inc(fed, me.add("fed"))
                    for half in range(2):
                        v.wait_ge(filled, me.next("filled"))
                        b = me.next_bank()
                        v.tensor_copy(xsT[:, 4 * half:4 * half + 4, 0:S_], b[:, 0:4 * S_].rearrange("p (a b) -> p a b", a=4))
                        if half:
                            v.tensor_copy(gate[0:S_, :], b[0:S_, 4 * S_:4 * S_ + 1])
                        v.drain().then_inc(drained, 1)
                    v.drain().then_inc(fed, me.add("fed"))
                    v.wait_ge(filled, me.next("filled"))
                    b = me.next_bank()
                    ts(put[0:S_, 0:NX], b[0:S_, :], tab("iota_col")[0:S_, :], ALU.is_equal)
                    v.drain().then_inc(drained, 1)
                    v.wait_ge(filled, me.next("filled"))
                    b = me.next_bank()
                    if ctx:
                        ts(put[0:S_, NX:W], b[0:S_, 0:NC], tab("iota_col")[0:S_, :], ALU.is_equal)
                    else:
                        pass_on()
                    v.drain().then_inc(drained, 1)
                    for j in range(2):
                        v.wait_ge(filled, me.next("filled"))
                        me.next_bank()
                        v.wait_ge(filled, me.next("filled"))
                        bu = me.next_bank()
                        pass_on()
                        v.drain().then_inc(asked, me.add("asked"))
                        v.wait_ge(answered, me.next("answered"))
                        tt(hid[:, 4 * j:4 * j + 4, 0:S_], gact[:, :, 0:S_], bu[:, 0:4 * S_].rearrange("p (a b) -> p a b", a=4), ALU.mult)
                        v.drain().then_inc(drained, 2)
                    v.drain().then_inc(fed, me.add("fed"))
                    for half in range(2):
                        v.wait_ge(filled, me.next("filled"))
                        b = me.next_bank()
                        ts(ys[0:S_, half * 512:(half + 1) * 512], b[0:S_, :], gate[0:S_, :], ALU.mult)
                        v.drain().then_inc(drained, 1)
                    v.drain().then_inc(fed, me.add("fed"))
                    for f in range(KT):
                        for res, h, n, j in segs:
                            v.wait_ge(filled, me.next("filled"))
                            b = me.next_bank()
                            stt(res[:, f, :], b[:, 0:n], mod[:, l, 5, f, j:j + 1], res[:, f, :], ALU.mult, ALU.add)
                            v.drain().then_inc(drained, 1)

            moe(0, True)

            norm([segx, segc], [sqx, sqc], rstd, modulated(1, 0))
            v.drain()
            hxg = hx[:, :, :].rearrange("p k (r c) -> p k r c", c=64)
            dx, dxg = diff[:, NC:NC + NX], diff[:, NC:NC + NX].rearrange("p (r c) -> p r c", c=64)
            dc = diff[:, 0:NC]

            def shifted(k):
                g = hxg[:, k, :, :]
                src, dst, edge = [
                    ((slice(None), slice(0, 63)), (slice(None), slice(1, 64)), (slice(None), slice(0, 1))),
                    ((slice(None), slice(1, 64)), (slice(None), slice(0, 63)), (slice(None), slice(63, 64))),
                    ((slice(0, 7), slice(None)), (slice(1, 8), slice(None)), (slice(0, 1), slice(None))),
                    ((slice(1, 8), slice(None)), (slice(0, 7), slice(None)), (slice(7, 8), slice(None)))][k // 2]
                tt(dxg[:, dst[0], dst[1]], g[:, src[0], src[1]], g[:, dst[0], dst[1]], ALU.subtract)
                ts(dxg[:, edge[0], edge[1]], g[:, edge[0], edge[1]], -1.0, ALU.mult)
                c = hc[:, k, :]
                s, d, e = ((slice(0, NC - 1), slice(1, NC), slice(0, 1)) if k < KT // 2 else
                           (slice(1, NC), slice(0, NC - 1), slice(NC - 1, NC)))
                tt(dc[:, d], c[:, s], c[:, d], ALU.subtract)
                ts(dc[:, e], c[:, e], -1.0, ALU.mult)

            stream = 0
            for j, what, mt, ns in W_MIX:
                for half in range(ns):
                    me.first_bank()
                    for k in range(KT):
                        shifted(k)
                        v.drain()
                        if k >= 2:
                            v.wait_ge(mix_used, stream * (KT - 1) + k - 1)
                        m = mixed[k % 2]
                        stt(m[:, NC:NC + NX], dx, mixes[:, j, k:k + 1], hx[:, k, :], ALU.mult, ALU.add)
                        stt(m[:, 0:NC], dc, mixes[:, j, k:k + 1], hc[:, k, :], ALU.mult, ALU.add)
                        v.drain().then_inc(fed, me.add("fed"))
                    stream += 1
                    if what in "wg":
                        v.wait_ge(filled, me.next("filled"))
                        me.next_bank()
                        if what == "w":
                            v.wait_ge(filled, me.next("filled"))
                            me.next_bank()
                        v.drain().then_inc(asked, me.add("asked"))
                        v.wait_ge(answered, me.next("answered"))
                        v.drain().then_inc(drained, 2 if what == "w" else 1)
                        continue
                    if what == "a":
                        v.wait_ge(filled, me.next("filled"))
                        b = me.next_bank()
                        v.tensor_copy(HA[:, NC:NC + NX], b[:, :])
                        v.drain().then_inc(drained, 1)
                        v.wait_ge(filled, me.next("filled"))
                        b = me.next_bank()
                        v.tensor_copy(HA[:, 0:NC], b[:, 0:NC])
                        v.drain().then_inc(drained, 1)
                        continue
                    for m4 in range(mt):
                        f = half * 4 + m4
                        v.wait_ge(filled, me.next("filled"))
                        b = me.next_bank()
                        v.tensor_copy({"r": Rx, "k": Kx, "v": Vx}[what][:, f, :], b[:, :])
                        v.drain().then_inc(drained, 1)
                        if what != "r":
                            v.wait_ge(filled, me.next("filled"))
                            b = me.next_bank()
                            v.tensor_copy({"k": Kc, "v": Vc}[what][:, f, :], b[:, 0:NC])
                            v.drain().then_inc(drained, 1)

            s = t["slab"]
            s.n = ADA_SLABS + FNET_SLABS + NE * EXPERT_SLABS + 7
            lora = ring[s.n % RING]
            v.wait_ge(slab_loaded[s.n % RING], 16 * (s.n // RING + 1))
            lora2 = lora[:, :, :].rearrange("p a b -> p (a b)")
            v.drain()
            for z in (bb, kb, vb):
                v.memset(z, 0.0)
            v.memset(ar[:, :, 0:128], 0.0)
            with me.loop("pair", KT) as p:
                v.tensor_copy(pp[:, 0:9], rwp[:, bass.ds(p, 1), :].rearrange("p a b -> p (a b)"))
                for q, dst in enumerate((w2p, a2p, g2p)):
                    v.tensor_copy(dst, lora2[:, bass.ds(p * 128 + 1024 * q, 128)])
                v.drain()
                kx, kc, vx, vc, rx = (z[:, bass.ds(p, 1), :].rearrange("p a b -> p (a b)") for z in (Kx, Kc, Vx, Vc, Rx))
                ts(pp[:, 9:10], pp[:, 5:6], -1.0, ALU.mult, 1.0, ALU.add)
                ts(kkv[:, 0:NC], kc, pp[:, 4:5], ALU.mult)
                ts(kkv[:, NC:768], kx, pp[:, 4:5], ALU.mult)
                v.drain()
                tt(ksq, kkv, kkv, ALU.mult)
                v.drain().then_inc(fed, me.add("fed"))
                me.first_bank()
                for a, n in ((0, NC), (NC, NX)):
                    v.wait_ge(filled, me.next("filled"))
                    b = me.next_bank()
                    ts(ksq[:, a:a + n], b[:, 0:n], 1e-12, ALU.add)
                    v.drain().then_inc(drained, 1)
                v.drain().then_inc(asked, me.add("asked"))
                v.wait_ge(answered, me.next("answered"))
                v.reciprocal(ksq, ksq)
                v.drain()
                tt(kkn, kkv, ksq, ALU.mult)
                for d, g, chunks in WALK:
                    x = g > 0
                    if g == 0:
                        me.first_bank()
                        for _ in range(4):
                            v.wait_ge(filled, me.next("filled"))
                            me.next_bank()
                        pass_on()
                        v.drain().then_inc(asked, me.add("asked"))
                        v.wait_ge(answered, me.next("answered"))
                        pass_on()
                        v.drain().then_inc(drained, 4)
                        ts(lw, lw, -math.exp(-0.5), ALU.mult)
                        ts(kd, av, pp[:, 5:6], ALU.mult, pp[:, 9:10], ALU.add)
                        v.drain()
                        tt(kd[:, 0:NC], kd[:, 0:NC], kc, ALU.mult)
                        tt(kd[:, NC:768], kd[:, NC:768], kx, ALU.mult)
                        tt(av, av, kkn, ALU.mult)
                        v.memset(Z, 0.0)
                        v.drain()
                        if d == 0:
                            v.tensor_copy(ksum, kd[:, NC:768])
                        else:
                            tt(ksum, ksum, kd[:, NC:768], ALU.add)
                    cols = slice(256 * g, 256 * g + 256)
                    xc = slice(256 * (g - 1), 256 * g)
                    chunked = "p (c n) -> p c n"
                    v.drain()
                    v.tensor_tensor_scan(Lc, tab("chunk"), lw[:, cols], 0.0, ALU.mult, ALU.add)
                    v.drain()
                    L3 = Lc.rearrange(chunked, c=GC)
                    v.tensor_copy(ET.unsqueeze(2), L3[:, :, CH - 1:CH])
                    v.drain()
                    if d == 1:
                        tt(L3, bc(ET.unsqueeze(2), 128, GC, CH), L3, ALU.subtract)
                        v.drain()
                        tt(Lc, Lc, lw[:, cols], ALU.add)
                        v.drain()
                    tt(E1, Lc, lw[:, cols], ALU.subtract)
                    v.drain().then_inc(asked, me.add("asked"))
                    v.wait_ge(answered, me.next("answered"))
                    for hrow in range(2):
                        rows = slice(64 * hrow, 64 * hrow + 64)
                        blk = slice(64 * hrow, 64 * hrow + 64)
                        stt(ar[rows, :, blk], kkn[rows, cols].rearrange(chunked, c=GC), -1.0,
                            E1[rows, :].rearrange(chunked, c=GC), ALU.mult, ALU.mult)
                        tt(bb[rows, :, blk], av[rows, cols].rearrange(chunked, c=GC), E3[rows, :].rearrange(chunked, c=GC), ALU.mult)
                        tt(kb[rows, :, blk], kd[rows, cols].rearrange(chunked, c=GC), E3[rows, :].rearrange(chunked, c=GC), ALU.mult)
                        vsrc = vx[rows, xc] if x else vc[rows, :]
                        v.tensor_copy(vb[rows, :, blk], vsrc.rearrange(chunked, c=GC))
                    if x:
                        tt(ar[:, :, 128:192], rx[:, xc].rearrange(chunked, c=GC), Lc.rearrange(chunked, c=GC), ALU.mult)
                    v.drain().then_inc(fed, me.add("fed"))
                    me.first_bank()
                    four = "p (c n) -> p c n"
                    v.wait_ge(filled, me.next("filled"))
                    b = me.next_bank()
                    v.tensor_copy(NT, b[:, :].rearrange(four, c=GC))
                    v.drain().then_inc(drained, 1)
                    v.wait_ge(filled, me.next("filled"))
                    b = me.next_bank()
                    tt(MT, b[:, :].rearrange(four, c=GC), bc(strict[:, d, :].unsqueeze(1), 128, GC, 128), ALU.mult)
                    v.drain().then_inc(drained, 1)
                    if x:
                        v.wait_ge(filled, me.next("filled"))
                        b = me.next_bank()
                        tt(QQ, b[:, :].rearrange(four, c=2 * GC), bc(incl[:, d, :].unsqueeze(1), 128, 2 * GC, CH), ALU.mult)
                        v.drain().then_inc(drained, 1)
                    for dst in (Bt, Kt, Vt):
                        v.wait_ge(filled, me.next("filled"))
                        b = me.next_bank()
                        v.tensor_copy(dst, b[:, :].rearrange(four, c=GC))
                        v.drain().then_inc(drained, 1)
                    for z in (X, XT):
                        v.tensor_copy(z, bc(ident.unsqueeze(1), 128, GC, 128))
                    for l in range(6):
                        tt(NL, NT, bc(levels[:, d, l, :].unsqueeze(1), 128, GC, 128), ALU.mult)
                        v.drain().then_inc(fed, me.add("fed"))
                        v.wait_ge(filled, me.next("filled"))
                        b = me.next_bank()
                        v.tensor_copy(T, b[:, :].rearrange(four, c=GC))
                        v.drain().then_inc(drained, 1)
                        v.drain().then_inc(fed, me.add("fed"))
                        for z in ((X, XT) if l < 5 else (XT,)):
                            v.wait_ge(filled, me.next("filled"))
                            b = me.next_bank()
                            tt(z, z, b[:, :].rearrange(four, c=GC), ALU.add)
                            v.drain().then_inc(drained, 1)
                    for c in chunks:
                        v.drain().then_inc(fed, me.add("fed"))
                        v.wait_ge(filled, me.next("filled"))
                        b = me.next_bank()
                        v.tensor_copy(G, b[:, 0:128])
                        v.drain().then_inc(drained, 1)
                        v.drain().then_inc(fed, me.add("fed"))
                        v.wait_ge(filled, me.next("filled"))
                        b = me.next_bank()
                        v.tensor_copy(U, b[:, 0:128])
                        v.drain().then_inc(drained, 1)
                        v.drain().then_inc(fed, me.add("fed"))
                        if x:
                            v.wait_ge(filled, me.next("filled"))
                            b = me.next_bank()
                            at = 256 * (g - 1) + CH * c
                            if d == 0:
                                v.tensor_copy(Y[:, at:at + CH], b[:, 0:CH])
                            else:
                                tt(Y[:, at:at + CH], Y[:, at:at + CH], b[:, 0:CH], ALU.add)
                            v.drain().then_inc(drained, 1)
                        v.wait_ge(filled, me.next("filled"))
                        b = me.next_bank()
                        tt(Z, Z, b[:, 0:128], ALU.add)
                        v.drain().then_inc(drained, 1)
                        ts(Z, Z, ET[:, c:c + 1], ALU.mult)
                        v.drain()
                tt(tb, rx, ksum, ALU.mult)
                v.drain()
                ts(tb, tb, pp[:, 6:7], ALU.mult)
                v.drain().then_inc(fed, me.add("fed"))
                me.first_bank()
                v.wait_ge(filled, me.next("filled"))
                b = me.next_bank()
                stt(Y, b[:, :], -1.0 / CH, Y, ALU.mult, ALU.add)
                v.drain().then_inc(drained, 1)
                tt(tc, Y, Y, ALU.mult)
                v.drain().then_inc(fed, me.add("fed"))
                v.wait_ge(filled, me.next("filled"))
                b = me.next_bank()
                tt(ksum, b[:, :], vx, ALU.mult)
                v.drain().then_inc(drained, 1)
                v.wait_ge(filled, me.next("filled"))
                bg = me.next_bank()
                v.tensor_copy(tb, bg[:, :])
                v.drain().then_inc(drained, 1)
                v.wait_ge(filled, me.next("filled"))
                b = me.next_bank()
                ts(ta, b[:, :], 1.0 / CH, ALU.mult, 64e-5, ALU.add)
                v.drain().then_inc(drained, 1)
                v.drain().then_inc(asked, me.add("asked"))
                v.wait_ge(answered, me.next("answered"))
                v.reciprocal(ta, ta)
                v.drain()
                tt(Y, Y, ta, ALU.mult)
                v.drain()
                ts(Y, Y, pp[:, 7:8], ALU.mult, pp[:, 8:9], ALU.add)
                v.drain()
                tt(Y, Y, ksum, ALU.add)
                v.drain()
                tt(rx, Y, tb, ALU.mult)
                v.drain()
            v.drain().then_inc(slab_used, 1)
            v.drain().then_inc(fed, me.add("fed"))
            me.first_bank()
            for f in range(KT):
                v.wait_ge(filled, me.next("filled"))
                b = me.next_bank()
                stt(resx[:, f, :], b[:, :], mod[:, 1, 2, f, 0:1], resx[:, f, :], ALU.mult, ALU.add)
                v.drain().then_inc(drained, 1)
            v.drain()
            moe(1, False)
            v.drain()
            norm([segx], [sqx], rstd, lambda k, j: (vec("final_g")[:, k:k + 1], None))
            v.drain()
            v.tensor_copy(resx[:, :, :], hx[:, :, :])

            v.drain().then_inc(asked, me.add("asked"))
            v.wait_ge(tables_loaded, 80)
            with me.loop("layer", 2) as l:
                v.tensor_copy(pv, layer2[:, bass.ds(l, 1), :].rearrange("p a b -> p (a b)"))
                v.drain().then_inc(asked, me.add("asked"))
                segs = [(resx, hx, NX, 0)]
                norm(segs, [sq2], rstd2, lambda k, j: (pv[:, k:k + 1], None))
                v.drain().then_inc(fed, me.add("fed"))
                me.first_bank()
                for f in range(F_TILES):
                    v.wait_ge(filled, me.next("filled"))
                    b = me.next_bank()
                    v.tensor_copy(Fm[:, f, :], b[:, :])
                    v.drain().then_inc(drained, 1)
                for c0, n in ((0, 256), (256, TM_W - 256)):
                    for i in range(4):
                        v.wait_ge(filled, me.next("filled"))
                        b = me.next_bank()
                        v.tensor_copy(VT[:, i, c0:c0 + n], b[:, 0:n])
                        v.drain().then_inc(drained, 1)
                v.drain()
                tt(S[:, 0:3, :], Fm[:, 0:3, :], Fm[:, 0:3, :], ALU.mult)
                v.drain().then_inc(fed, me.add("fed"))
                me.first_bank()
                inverse_roots([(NX, 256), (NX, 128)], S[:, 0:2, :].rearrange("p a b -> p (a b)"), 1e-6)
                for k in range(3):
                    stt(Fm[:, k, :], Fm[:, k, :], pv[:, 16 + k:17 + k], S[:, k // 2, :], ALU.mult, ALU.mult)
                tt(lf, VT[:, :, TM_W - 4:TM_W], bc(pv[:, 23:27].unsqueeze(1), 128, 4, 4), ALU.add)
                v.drain()
                stt(le, lf, -1.0, lf, ALU.mult, ALU.min)
                v.drain().then_inc(asked, me.add("asked"))
                v.wait_ge(answered, me.next("answered"))
                ts(le, le, 1.0, ALU.add)
                v.drain().then_inc(asked, me.add("asked"))
                v.wait_ge(answered, me.next("answered"))
                stt(lf, lf, 0.0, le, ALU.min, ALU.subtract)
                v.wait_ge(aux_loaded, l * 16 + 16)
                pass_on()
                v.drain().then_inc(fed, me.add("fed"))
                for dst, j in ((QN, 0), (QN, 1), (QR, None), (KN, 0), (KN, 1)):
                    v.wait_ge(filled, me.next("filled"))
                    b = me.next_bank()
                    v.tensor_copy(tile(dst, j), b[:, :])
                    v.drain().then_inc(drained, 1)
                for i in range(4):
                    v.wait_ge(filled, me.next("filled"))
                    b = me.next_bank()
                    v.tensor_copy(VA[:, i, :], b[:, 0:256])
                    v.drain().then_inc(drained, 1)
                v.drain().then_inc(fed, me.add("fed"))
                me.first_bank()
                for dst, j, d in ROPED:
                    x = tile(dst, j)
                    v.wait_ge(filled, me.next("filled"))
                    b = me.next_bank()
                    tt(S[:, 0, :], b[:, :], tab2(f"sin{d}"), ALU.mult)
                    v.drain().then_inc(drained, 1)
                    tt(x, x, tab2(f"cos{d}"), ALU.mult)
                    v.drain()
                    tt(x, x, S[:, 0, :], ALU.add)
                    v.drain()
                for h in range(HEADS):
                    v.tensor_copy(lfb, bc(lf[:, :, h:h + 1], 128, 4, 128))
                    v.drain().then_inc(fed, me.add("fed"))
                    v.wait_ge(filled, me.next("filled"))
                    b = me.next_bank()
                    v.tensor_copy(cumk[:, h, :], b[:, :])
                    v.drain().then_inc(drained, 1)
                for va in VARIANTS:
                    for i in range(4):
                        k0, k1 = span(va, i)
                        n = k1 - k0
                        v.drain().then_inc(fed, me.add("fed"))
                        me.first_bank()
                        causal = tab2("causal")[:, 384 - 128 * i + k0:384 - 128 * i + k1]
                        mask = causal
                        if va == "swa":
                            mask = tab2("window")[:, 384 - 128 * i + k0:384 - 128 * i + k1]
                        if va == "dsa" and i > 0:
                            sc, rs = score[:, 0:n], rest[:, 0:n]
                            for h in range(8):
                                v.wait_ge(filled, me.next("filled"))
                                b = me.next_bank()
                                wcol = VT[:, i, 640 + h:641 + h]
                                ts(rs if h else sc, b[:, 0:n], 0.0, ALU.max, wcol, ALU.mult)
                                v.drain().then_inc(drained, 1)
                                if h:
                                    tt(sc, sc, rs, ALU.add)
                                    v.drain()
                            tt(rs, sc, causal, ALU.add)
                            for _ in range(TOPK // 8):
                                v.drain()
                                v.max(t8, rs)
                                v.drain()
                                v.match_replace(rs, t8, rs, -3e38)
                            v.drain()
                            ts(keep[:, 0:n], rs, -2e38, ALU.is_gt, NEG, ALU.mult)
                            v.drain()
                            mask = keep[:, 0:n]
                        for h, (parts, _, _, _) in enumerate(heads(va)):
                            v.wait_ge(filled, me.next("filled"))
                            b = me.next_bank()
                            if va == "fox":
                                tt(PT[:, h, 0:n], causal, cumk[:, h, 0:n], ALU.subtract)
                                v.drain()
                                mask = PT[:, h, 0:n]
                            stt(S[:, h, 0:n], b[:, 0:n], SCALE[va], mask, ALU.mult, ALU.add)
                            v.drain().then_inc(drained, 1)
                            if len(parts) == 2:
                                v.wait_ge(filled, me.next("filled"))
                                b = me.next_bank()
                                stt(S[:, h, 0:n], b[:, 0:n], SCALE[va], S[:, h, 0:n], ALU.mult, ALU.add)
                                v.drain().then_inc(drained, 1)
                        v.tensor_reduce(mx, S[:, :, 0:n], AX, ALU.max)
                        v.drain()
                        if va == "swa":
                            tt(mx, mx, pv[:, 19:23], ALU.max)
                            v.drain()
                            tt(esink, pv[:, 19:23], mx, ALU.subtract)
                        ts(mxn, mx, -1.0, ALU.mult)
                        v.drain().then_inc(asked, me.add("asked"))
                        v.wait_ge(answered, me.next("answered"))
                        if va == "swa":
                            tt(sums, sums, esink, ALU.add)
                            v.drain()
                        v.reciprocal(sums, sums)
                        v.drain()
                        tt(S[:, :, 0:n], S[:, :, 0:n], bc(sums.unsqueeze(2), 128, HEADS, n), ALU.mult)
                        v.drain().then_inc(fed, me.add("fed"))
                        for h in range(HEADS):
                            v.wait_ge(filled, me.next("filled"))
                            b = me.next_bank()
                            v.tensor_copy(PT[:, h, 0:n], b[:, 0:n])
                            v.drain().then_inc(drained, 1)
                        v.drain().then_inc(fed, me.add("fed"))
                        for _, _, ot, rows in heads(va):
                            v.wait_ge(filled, me.next("filled"))
                            b = me.next_bank()
                            v.tensor_copy(OT[rows, ot, 128 * i:128 * i + 128], b[rows, 0:128])
                            v.drain().then_inc(drained, 1)
                v.drain().then_inc(fed, me.add("fed"))
                me.first_bank()
                for f in range(KT):
                    v.wait_ge(filled, me.next("filled"))
                    b = me.next_bank()
                    tt(resx[:, f, :], resx[:, f, :], b[:, :], ALU.add)
                    v.drain().then_inc(drained, 1)
                v.drain()
                norm(segs, [sq2], rstd2, lambda k, j: (pv[:, 8 + k:9 + k], None))
                v.drain().then_inc(fed, me.add("fed"))
                me.first_bank()
                for f in range(32):
                    v.wait_ge(filled, me.next("filled"))
                    b = me.next_bank()
                    ts(up[:, f, :], b[:, :], 0.0, ALU.max)
                    v.drain().then_inc(drained, 1)
                    tt(up[:, f, :], up[:, f, :], up[:, f, :], ALU.mult)
                v.drain().then_inc(fed, me.add("fed"))
                me.first_bank()
                for f in range(KT):
                    v.wait_ge(filled, me.next("filled"))
                    b = me.next_bank()
                    tt(resx[:, f, :], resx[:, f, :], b[:, :], ALU.add)
                    v.drain().then_inc(drained, 1)
                v.drain()
            norm([(resx, hx, NX, 0)], [sq2], rstd2, lambda k, j: (vec("final2")[:, k:k + 1], None))
            v.drain().then_inc(asked, me.add("asked"))

        if K.wrong:
            raise ValueError(f"counts of the loops: {sorted(K.wrong)}")


def shape_tables():
    f = np.float32
    p = np.arange(128)
    t1 = {}
    t1["ident"] = np.eye(128)
    t1["ones"] = np.ones((128, 128))
    t1["headones"] = (p[:, None] // 64 == p[None, :] // 64) * 1.0
    t1["iota_row"] = np.broadcast_to(np.arange(96), (128, 96))
    t1["iota_col"] = p[:, None]
    t1["chunk"] = np.broadcast_to((np.arange(256) % 64 != 0) * 1.0, (128, 256))
    same = p[:, None] // 64 == p[None, :] // 64
    s, t = p[:, None] % 64, p[None, :] % 64
    lev = []
    for d in range(2):
        a, b = (s, t) if d == 0 else (t, s)
        for l in range(6):
            n = 2 ** l
            lev.append(same & (a // (2 * n) == b // (2 * n)) & (a // n % 2 == 0) & (b // n % 2 == 1))
    t1["level"] = np.concatenate(lev, 1)
    t1["strict"] = np.concatenate([same & (s < t), same & (s > t)], 1)
    s, t = p[:, None] % 64, np.arange(64)[None, :]
    t1["incl"] = np.concatenate([s <= t, s >= t], 1)
    t2 = {}
    pos = np.arange(512, dtype=f)
    for d in (64, 32):
        half = d // 2
        inv = (1.0 / (f(10000.0) ** (np.arange(half, dtype=f) * f(2.0) / f(d)))).astype(f)
        ang = (inv[p % half][:, None] * pos[None, :]).astype(f)
        t2[f"cos{d}"], t2[f"sin{d}"] = np.cos(ang), np.sin(ang)
        rot = np.zeros((128, 128))
        for r in range(128):
            if r % d < half:
                rot[r + half, r] = -1.0
            else:
                rot[r - half, r] = 1.0
        t2[f"rot{d}"] = rot
    x = np.arange(896)[None, :] - 384
    q = p[:, None]
    t2["causal"] = np.where(x <= q, 0.0, NEG)
    t2["window"] = np.where((x <= q) & (q - x < 128), 0.0, NEG)
    t2["upto"] = (x >= q) * 1.0
    pack = lambda t, order: np.ascontiguousarray(np.concatenate([t[n] for n in order], 1).astype(f))
    n = np.arange(256)
    ang = 2 * np.pi * (np.outer(n, n) % 256) / 256
    feat = np.concatenate([np.cos(ang), np.sin(ang)], 1)
    fc = feat.reshape(2, 128, 512).transpose(1, 0, 2).reshape(128, 1024)

    def seq(T):
        m = np.arange(T)
        a = 2 * np.pi * (np.outer(m, m) % T) / T
        r = 1.0 / math.sqrt(T * 256)
        both = np.stack([np.cos(a) * r, -np.sin(a) * r])
        return both.reshape(2, T // 128, 128, T).transpose(2, 0, 1, 3).reshape(128, -1)

    first = np.zeros((128, 4096))
    first[:, 0:1024] = fc
    first[:, 1024:2048] = seq(256)
    return pack(t1, TAB1), pack(t2, TAB2), first.astype(f), seq(512).astype(f)


def lay_out(i):
    f = np.float32
    g = {k: np.asarray(a) for k, a in i.items()}
    tabs1, tabs2, fnet1, fnet2 = shape_tables()
    slabs = np.zeros((SLABS, 128, 4096), f)
    n = 0

    def add(w):
        nonlocal n
        k, cols = w.shape
        for c in range(0, cols, 512):
            part = w[:, c:c + 512]
            slabs[n].reshape(128, 8, 512)[:, 0:k // 128, 0:part.shape[1]] = part.reshape(k // 128, 128, -1).transpose(1, 0, 2)
            n += 1

    def moe(l):
        for e in range(NE):
            for h in range(2):
                add(g["moe_wg"][l, e][:, 512 * h:512 * h + 512])
                add(g["moe_wu"][l, e][:, 512 * h:512 * h + 512])
            add(g["moe_wd"][l, e])

    for l in range(2):
        add(g["ada_w"][l])
    slabs[n], slabs[n + 1] = fnet1, fnet2
    n += 2
    add(g["fnet_wo"][0])
    moe(0)
    add(np.concatenate([g["rw_w1"][0, 0], g["rw_w1"][0, 1], g["rw_a1"][0, 0], g["rw_a1"][0, 1], g["rw_g1"][0]], 1))
    for w in ("rw_wr", "rw_wk", "rw_wv"):
        add(g[w][0])
    slabs[n][:, 0:1024] = g["rw_w2"][0].reshape(128, D)
    slabs[n][:, 1024:2048] = g["rw_a2"][0].reshape(128, D)
    slabs[n][:, 2048:3072] = g["rw_g2"][0]
    n += 1
    add(g["rw_wo"][0])
    moe(1)
    sizes = [256, 128, 32, 256, 128, 128, 256, 256, 256, 256, 32, 8, 256, 256, 256, 4]
    ends = np.cumsum(sizes)
    cols = [np.arange(e - s, e) for s, e in zip(sizes, ends)]
    (acq, ackv, akr, bq, bk, bv, cq, ck, cv, cqi, cki, cw, dq, dk, dv, df) = cols
    swap = np.concatenate([np.arange(64 * h, 64 * h + 64) for h in (0, 2, 1, 3)])
    order = np.concatenate([acq, ackv, bq[swap], bk, cq, ck, cqi, dq, dk, np.tile(akr, 4), np.tile(cki, 4), bv, cv, dv, cw, df])
    mixed_rows = np.arange(D)
    mixed_rows[256:512] = 256 + swap
    aux = np.zeros((2, 128, 1280), f)
    nope = np.concatenate([np.arange(96 * h, 96 * h + 64) for h in range(4)] + [np.arange(96 * h + 64, 96 * h + 96) for h in range(4)])
    kv = np.concatenate([np.arange(128 * h, 128 * h + 64) for h in range(4)] + [np.arange(128 * h + 64, 128 * h + 128) for h in range(4)])
    for l in range(2):
        add(g["w_in_2"][l][:, order])
        add(g["w_out_2"][l][mixed_rows])
        add(g["w_up_2"][l])
        for h in range(2):
            for kg in range(4):
                add(g["w_down_2"][l][kg * D:(kg + 1) * D, 512 * h:512 * h + 512])
        aux[l][:, 0:768] = g["mla_w_uq_2"][l][:, nope].reshape(2, 128, 384).transpose(1, 0, 2).reshape(128, 768)
        aux[l][:, 768:] = g["mla_w_ukv_2"][l][:, kv]
    assert n == SLABS, n

    def tiles(v):
        return v.reshape(-1, 128).T

    def rows(v):
        return np.broadcast_to(v.reshape(1, -1), (128, v.size))

    parts = {
        "c": np.stack([tiles(g["c"][0]), tiles(g["c_ctx"])], 2).reshape(128, 16),
        "ada_b": tiles(g["ada_b"]), "norm_g": tiles(g["norm_g"]), "fnet_bo": tiles(g["fnet_bo"]),
        "final_g": tiles(g["final_g"]), "mix": tiles(g["rw_mix"][0]),
        "rwp": np.stack([tiles(z) for z in (g["rw_w0"][0, 0], g["rw_w0"][0, 1], g["rw_a0"][0, 0], g["rw_a0"][0, 1], g["rw_kk"][0],
                                            g["rw_ka"][0], g["rw_rk"][0].reshape(-1), g["rw_lnx_w"][0], g["rw_lnx_b"][0])], 2).reshape(128, 72),
        "router": g["moe_router"].reshape(2, 8, 128, 16).transpose(2, 0, 1, 3).reshape(128, 256),
        "layer2": np.concatenate([np.concatenate([
            tiles(g["norm1_2"][l]), tiles(g["norm2_2"][l]), tiles(g["mla_q_norm_2"][l]), tiles(g["mla_kv_norm_2"][l]),
            rows(g["swa_sinks_2"][l][[0, 2, 1, 3]]), rows(g["fox_b_f_2"][l])], 1) for l in range(2)], 1),
        "final2": tiles(g["final_norm_2"]),
    }
    vecs = np.ascontiguousarray(np.concatenate([parts[k] for k in VEC], 1))
    return {"slabs": slabs, "vecs": vecs, "tabs1": tabs1, "tabs2": tabs2, "aux": aux,
            "xT": np.ascontiguousarray(g["x"][0].T), "ctxT": np.ascontiguousarray(g["ctx"][0].T)}


def kernel(**inputs):
    import numpy as _np
    import concourse.bacc as _bacc
    from concourse import mybir as _mybir
    from concourse.bass_utils import run_bass_kernel_spmd as _run

    nc = _bacc.Bacc("TRN2", target_bir_lowering=False, num_devices=1)
    arrays = lay_out(inputs)
    args = [nc.dram_tensor(name, a.shape, _mybir.dt.from_np(a.dtype), kind="ExternalInput").ap() for name, a in arrays.items()]
    out = nc.dram_tensor("outT", (D, NX), _mybir.dt.float32, kind="ExternalOutput").ap()
    build(nc, *args, out)
    r = _run(nc, [arrays], core_ids=[0])
    return _np.ascontiguousarray(r.results[0]["outT"].T)[None]
```

```python
import concourse.bass as bass
from concourse import mybir
from contextlib import ExitStack, contextmanager
import math
import numpy as np

D = 1024
KT = D // 128
NX, NC = 512, 256
NE = 16
CAPX, CAPC = 2 * NX // NE, 2 * NC // NE
HALF = 512
RING = 3
ADA_SLABS, FNET_SLABS, EXPERT_SLABS, RWKV_SLABS, LAYER_SLABS = 24, 4, 6, 10, 24
SLABS = ADA_SLABS + FNET_SLABS + 2 * NE * EXPERT_SLABS + RWKV_SLABS + 2 * LAYER_SLABS
WORK = 24 * 1024 + 256
CH, GC = 64, 4
NCH, NCX = (NX + NC) // CH, NX // CH
HEADS = 4
TOPK = 128
NEG = -1e30
F_TILES = 18
TM_W = 652

VEC = {}
_n = 0
for _name, _w in [("c", 16), ("ada_b", 96), ("norm_g", 32), ("fnet_bo", 8), ("final_g", 8), ("mix", 48),
                  ("rwp", 72), ("router", 256), ("layer2", 54), ("final2", 8)]:
    VEC[_name] = (_n, _n + _w)
    _n += _w
NVEC = _n
TAB1 = {}
_n = 0
for _name, _w in [("ident", 128), ("ones", 128), ("headones", 128), ("iota_row", 96), ("iota_col", 1),
                  ("chunk", 768), ("level", 12 * CH), ("strict", 2 * CH), ("incl", 2 * CH),
                   ("eye2", CH)]:
    TAB1[_name] = (_n, _n + _w)
    _n += _w
NTAB1 = _n
TAB2 = {}
_n = 0
for _name, _w in [("cos64", 512), ("sin64", 512), ("cos32", 512), ("sin32", 512), ("rot64", 128), ("rot32", 128),
                  ("causal", 896), ("window", 896), ("upto", 896)]:
    TAB2[_name] = (_n, _n + _w)
    _n += _w
NTAB2 = _n

PER = {
    "expert_ctx": dict(slab=6, filled=26, fed=4, asked=2, answered=2),
    "expert": dict(slab=6, filled=18, fed=4, asked=2, answered=2),
    "pair": dict(slab=0, filled=95, fed=27, asked=4, answered=4, afilled=62, masked=36),
    "layer": dict(slab=24, filled=335, fed=61, asked=22, answered=21),
    "ada": dict(slab=3, filled=0, fed=0, asked=0, answered=0),
}


class Tally:

    def __init__(self):
        self.n = 0
        self.loops = []

    def at(self, more=0):
        v = self.n + more
        for i, per in self.loops:
            v = i * per + v
        return v


def place_in(order, name):
    return order.index(name) + 1


class Side:

    def __init__(self, eng, K):
        self.eng, self.K = eng, K
        self.t = {k: Tally() for k in ("slab", "filled", "fed", "asked", "answered", "afilled", "masked")}
        self.bank, self.abank, self.width = 0, 0, 8

    def add(self, name):
        self.t[name].n += 1
        return 1

    def next(self, name):
        self.t[name].n += 1
        return self.t[name].at()

    def first_bank(self):
        self.bank = 0
        return self.t["filled"].at()

    def reuses(self):
        return self.bank >= self.width

    def reused(self):
        return self.t["filled"].at(1 - self.width)

    def next_bank(self):
        self.bank += 1
        return self.K.banks[(self.bank - 1) % self.width]

    def split_banks(self):
        self.bank, self.abank, self.width = 0, 0, 4

    def next_act_bank(self):
        self.abank += 1
        return self.K.banks[4 + (self.abank - 1) % 4]

    def act_reuses(self):
        return self.abank >= 4

    def act_reused(self):
        return self.t["afilled"].at(-3)

    def mask_value(self, i, no):
        return i * PER["pair"]["masked"] + no

    def group(self, order, name):
        i, per = self.pair
        return i * per[order] + (self.K.first[order] + place_in(self.K.orders[order], name))

    def slot(self):
        return self.t["slab"].n % RING

    def landed(self):
        turn = self.t["slab"]
        v = 16 * (turn.n // RING + 1)
        for i, per in turn.loops:
            v = i * (16 * per // RING) + v
        return v

    def next_slab(self):
        self.t["slab"].n += 1
        return self.K.ring[(self.t["slab"].n - 1) % RING]

    @contextmanager
    def loop(self, name, turns):
        first = {k: t.n for k, t in self.t.items()}
        with self.eng.Fori(0, turns) as i:
            for k, t in self.t.items():
                t.loops.append((i, PER[name].get(k, 0)))
            yield i
            for k, t in self.t.items():
                t.loops.pop()
                got = t.n - first[k]
                if got and got != PER[name].get(k, 0):
                    self.K.wrong.add((name, k, got))
                if got:
                    t.n = first[k] + PER[name].get(k, 0) * turns


def build(nc, slabs_d, vecs_d, tabs1_d, tabs2_d, aux_d, x_d, ctx_d, out_d, spill_d):
    f32 = mybir.dt.float32
    ALU = mybir.AluOpType
    ACT = mybir.ActivationFunctionType
    AX = mybir.AxisListType.X
    stack = ExitStack()
    with stack:
        def sb(name, shape):
            return stack.enter_context(nc.sbuf_tensor(name, shape, f32))

        def sem(name):
            return stack.enter_context(nc.semaphore(name))

        ring = [sb(f"ring{s}", [128, KT, HALF]) for s in range(RING)]
        resx, resc = sb("resx", [128, KT, NX]), sb("resc", [128, KT, NC])
        hx, hc = sb("hx", [128, KT, NX]), sb("hc", [128, KT, NC])
        vecs, tabs1 = sb("vecs_sb", [128, NVEC]), sb("tabs1_sb", [128, NTAB1])
        mod = sb("mod", [128, 2, 6, KT, 2])
        cs = sb("cs", [128, KT, 2])
        cell = sb("cell", [1, 1])[:, :]
        work = sb("work", [128, WORK])
        ksum_t = sb("ksum_t", [128, NX])
        P = [stack.enter_context(nc.psum_tensor(f"bank{i}", [128, 512], f32)) for i in range(8)]

        slab_loaded = [sem(f"slab_loaded{s}") for s in range(RING)]
        filled_act, drained_act, masked, spilled, pe_steps = (sem(n) for n in ("filled_act", "drained_act", "masked", "spilled", "pe_steps"))
        slab_used, filled, drained, fed, mix_used = (sem(n) for n in ("slab_used", "filled", "drained", "fed", "mix_used"))
        asked, answered, tables_loaded, aux_loaded, stored = (sem(n) for n in ("asked", "answered", "tables_loaded", "aux_loaded", "stored"))

        class K:
            wrong = set()
            banks = P

        K.ring = ring

        def vec(name):
            return vecs[:, VEC[name][0]:VEC[name][1]]

        def tab(name):
            return tabs1[:, TAB1[name][0]:TAB1[name][1]]

        def cut(whole, at, *shape):
            n = math.prod(shape)
            v = whole[:, at:at + n]
            if len(shape) == 2:
                v = v.rearrange("p (a b) -> p a b", a=shape[0])
            if len(shape) == 3:
                v = v.rearrange("p (a b c) -> p a b c", a=shape[0], b=shape[1])
            return v

        def flat(t):
            return t[:, :, :].rearrange("p a b -> p (a b)")

        ident, ones, headones = tab("ident"), tab("ones"), tab("headones")
        levels = tab("level").rearrange("p (d l c) -> p d l c", d=2, l=6)
        strict = tab("strict").rearrange("p (d c) -> p d c", d=2)
        incl = tab("incl").rearrange("p (d c) -> p d c", d=2)
        norm_g = vec("norm_g").rearrange("p (l j k) -> p l j k", l=2, j=2)
        mixes = vec("mix").rearrange("p (j k) -> p j k", j=6)
        rwp = vec("rwp").rearrange("p (q j) -> p q j", q=KT)
        router = vec("router").rearrange("p (l k e) -> p l k e", l=2, k=KT)
        layer2 = vec("layer2").rearrange("p (l j) -> p l j", l=2)
        segx = (resx, hx, NX, 0)
        segc = (resc, hc, NC, 1)

        sqx, sqc = cut(work, 0, KT, NX), cut(work, KT * NX, KT, NC)
        rstd = cut(work, KT * (NX + NC), NX + NC)

        AB = cut(work, 0, 6, 4 * 512)

        htok = cut(work, 0, 6, D)
        o = 6 * D
        aff, o = cut(work, o, 6, NE), o + 6 * NE
        stok, o = cut(work, o, 6, NE), o + 6 * NE
        amax, o = cut(work, o, 6), o + 6
        affe, o = cut(work, o, 6), o + 6
        affT, o = cut(work, o, 768), o + 768
        left, o = cut(work, o, 768), o + 768
        slot, o = cut(work, o, 768), o + 768
        top8, o = cut(work, o, 8), o + 8
        pick, o = cut(work, o, 6, 96), o + 6 * 96
        esel, o = cut(work, o, 96), o + 96
        xsT, o = cut(work, o, KT, 96), o + KT * 96
        hid, o = cut(work, o, KT, 96), o + KT * 96
        gact, o = cut(work, o, 4, 96), o + 4 * 96
        put, o = cut(work, o, 768), o + 768
        gate, o = cut(work, o, 1), o + 1
        ys, o = cut(work, o, D), o + D
        ones768, o = cut(work, o, 768), o + 768

        Rx, o = cut(work, 0, KT, NX), KT * NX
        Kx, o = cut(work, o, KT, NX), o + KT * NX
        Vx, o = cut(work, o, KT, NX), o + KT * NX
        Kc, o = cut(work, o, KT, NC), o + KT * NC
        Vc, o = cut(work, o, KT, NC), o + KT * NC
        HW, o = cut(work, o, 768), o + 768
        HA, o = cut(work, o, 768), o + 768
        HG, o = cut(work, o, NX), o + NX
        rw0 = o
        diff = cut(work, o, 768)
        mixed = [cut(work, o + 768 * (j + 1), 768) for j in range(2)]
        NT, o = cut(work, o, NCH, CH), o + 768
        MT, o = cut(work, o, NCH, CH), o + 768
        QB, o = cut(work, o, NCX, CH), o + 512
        QK, o = cut(work, o, NCX, CH), o + 512
        BK, o = cut(work, o, NCH, 2 * CH), o + 1536
        Vt, o = cut(work, o, NCH, CH), o + 768
        AM, o = cut(work, o, NCH, 2 * CH), o + 1536
        assert o <= WORK, o
        kkv = work[:, rw0:rw0 + 768]
        ksq = work[:, rw0 + 768:rw0 + 1536]
        hxf, hcf, rcf, rxf = flat(hx), flat(hc), flat(resc), flat(resx)
        ar = hxf[:, 0:1536].rearrange("p (c n) -> p c n", c=NCH)
        bd, kd, kkn = (hxf[:, 1536 + j * 768:1536 + (j + 1) * 768] for j in range(3))
        w2p, a2p = (hxf[:, 3840 + j * 128:3968 + j * 128] for j in range(2))
        lw, Lc, E1, E3 = (rxf[:, j * 768:(j + 1) * 768] for j in range(4))
        XX = rxf[:, 0:1536].rearrange("p (x c n) -> p x c n", x=2, c=NCH)
        X, XT = (rxf[:, j * 768:(j + 1) * 768].rearrange("p (c n) -> p c n", c=NCH) for j in range(2))
        T, NL = (rxf[:, 1536 + j * 768:1536 + (j + 1) * 768].rearrange("p (c n) -> p c n", c=NCH) for j in range(2))
        WU = rxf[:, 1536:3072].rearrange("p (c n) -> p c n", c=NCH)
        vp = rxf[:, 0:768]
        ta, tb, tc = (rxf[:, j * 512:(j + 1) * 512] for j in range(3))
        Y, ksum = rxf[:, 3072:3584], ksum_t[:, :]
        g2p, Zs, ET, pp = rxf[:, 3584:3712], rxf[:, 3712:3840], rxf[:, 3840:3864], rxf[:, 3864:3874]
        Z = [Zs[:, d * CH:(d + 1) * CH] for d in range(2)]
        ETd = [ET[:, d * NCH:(d + 1) * NCH] for d in range(2)]
        At, Bc, Rt = [], [], []
        for z in (hcf, rcf):
            At.append(z[:, 0:768].rearrange("p (c n) -> p c n", c=NCH))
            Bc.append(z[:, 768:1536].rearrange("p (c n) -> p c n", c=NCH))
            Rt.append(z[:, 1536:2048].rearrange("p (c n) -> p c n", c=NCX))
        eye2 = tab("eye2")

        tabs2 = cut(work, 0, NTAB2)
        o = NTAB2
        o2 = o

        def tab2(name):
            return tabs2[:, TAB2[name][0]:TAB2[name][1]]

        Fm, o = cut(work, o, F_TILES, NX), o + F_TILES * NX
        VT, o = cut(work, o, 4, TM_W), o + 4 * TM_W
        QN, o = cut(work, o, 2, NX), o + 2 * NX
        QR, o = cut(work, o, NX), o + NX
        KN, o = cut(work, o, 2, NX), o + 2 * NX
        VA, o = cut(work, o, 4, 256), o + 4 * 256
        S, o = cut(work, o, HEADS, NX), o + HEADS * NX
        PT, o = cut(work, o, HEADS, NX), o + HEADS * NX
        assert o <= WORK, o
        up = cut(work, o2, 32, NX)
        sq2 = cut(work, o2, KT, NX)
        score, rest, keep = Fm[:, 0, :], Fm[:, 1, :], Fm[:, 2, :]
        cumk = rcf.rearrange("p (h n) -> p h n", h=HEADS)
        aux = hcf[:, 0:1280]
        pv = hcf[:, 1280:1307]
        lf = hcf[:, 1312:1328].rearrange("p (j h) -> p j h", j=4)
        le = hcf[:, 1328:1344].rearrange("p (j h) -> p j h", j=4)
        mx, mxn, sums, esink = (hcf[:, 1344 + 4 * j:1348 + 4 * j] for j in range(4))
        t8 = hcf[:, 1360:1368]
        lfb = hcf[:, 1408:1920].rearrange("p (j n) -> p j n", j=4)
        rstd2 = PT[:, 0, :]
        OT = hx

        def heads(v):
            out = []
            for h in range(HEADS):
                r, r32 = 64 * (h % 2), 32 * h
                rows, rows32 = slice(r, r + 64), slice(r32, r32 + 32)
                if v == "mla":
                    out.append(([(QN, h // 2, KN, h // 2, rows), (QR, None, Fm, 16, rows32)],
                                (VA, 128 * (h // 2)), h // 2, rows))
                elif v == "swa":
                    out.append(([(Fm, 3 + h // 2, Fm, 5, rows)], (VT, 0), 2 + h // 2, rows))
                elif v == "dsa":
                    out.append(([(Fm, 6 + h // 2, Fm, 8 + h // 2, rows)], (VT, 128 + 128 * (h // 2)), 4 + h // 2, rows))
                else:
                    out.append(([(Fm, 12 + h // 2, Fm, 14 + h // 2, rows)], (VT, 384 + 128 * (h // 2)), 6 + h // 2, rows))
            return out

        SCALE = {"mla": 96 ** -0.5, "swa": 64 ** -0.5, "dsa": 64 ** -0.5, "fox": 64 ** -0.5}
        VARIANTS = ("mla", "swa", "dsa", "fox")
        ROPED = [(Fm, 3, 64), (Fm, 4, 64), (Fm, 5, 64), (Fm, 6, 64), (Fm, 7, 64), (Fm, 8, 64), (Fm, 9, 64),
                 (QR, None, 32), (Fm, 10, 32), (Fm, 11, 32), (Fm, 16, 32), (Fm, 17, 32)]

        def tile(t, j):
            return t if j is None else t[:, j, :]

        def span(v, i):
            return (128 * max(0, i - 1) if v == "swa" else 0), 128 * (i + 1)

        CHAIN = [tuple(range(NCH)), (3, 2, 1, 0) + tuple(range(NCH - 1, 3, -1))]
        BATCHES = [slice(GC * b, GC * b + GC) for b in range(3)]
        PAIR_DVE = [("sum", 0), ("sum", 1)] + [("vt", b) for b in range(3)]
        PAIR_ACT = []
        for d_ in range(2):
            PAIR_DVE += [(n_, d_, b) for b in range(3) for n_ in ("NT", "MT")]
            PAIR_DVE += [("X0", d_, b) for b in range(3)]
            PAIR_DVE += [("XX", d_, l_, b) for l_ in range(1, 6) for b in range(3)]
            PAIR_DVE += [(n_, d_, b) for b in range(3) for n_ in ("AR", "Bc", "Y0") if b or n_ != "Y0"]
            PAIR_ACT += [("pre", d_, j) for j in range(4)]
            PAIR_ACT += [(n_, d_, b) for b in range(3) for n_ in ("BK", "At")]
            PAIR_ACT += [("MV", d_, b) for b in range(3)]
            PAIR_ACT += [("T", d_, l_, b) for l_ in range(1, 6) for b in range(3)]
            PAIR_ACT += [("WU", d_, b) for b in range(3)]

        def mask_no(d, l, b):
            return d * 18 + l * 3 + b + 1

        W_MIX = [(1, "w", 1, 1), (4, "a", 1, 1), (5, "g", 1, 1), (0, "r", 4, 2), (2, "k", 4, 2), (3, "v", 4, 2)]

        block = stack.enter_context(nc.Block())

        @block.sync
        def _(sp):
            sp.dma_start(vecs[:, :], vecs_d).then_inc(tables_loaded, 16)
            sp.dma_start(tabs1[:, :], tabs1_d).then_inc(tables_loaded, 16)
            sp.dma_start(resx[:, :, :], x_d.rearrange("(k p) t -> p k t", p=128)).then_inc(tables_loaded, 16)
            sp.dma_start(resc[:, :, :], ctx_d.rearrange("(k p) t -> p k t", p=128)).then_inc(tables_loaded, 16)
            for s in range(RING):
                sp.dma_start(flat(ring[s]), slabs_d[s]).then_inc(slab_loaded[s], 16)
            rounds = SLABS // RING
            with sp.Fori(1, rounds) as i:
                for s in range(RING):
                    sp.wait_ge(slab_used, i * RING + (s - RING + 1))
                    sp.dma_start(flat(ring[s]), slabs_d[i * RING + s]).then_inc(slab_loaded[s], 16)
            for n in range(rounds * RING, SLABS):
                sp.wait_ge(slab_used, n - RING + 1)
                sp.dma_start(flat(ring[n % RING]), slabs_d[n]).then_inc(slab_loaded[n % RING], 16)

        @block.tensor
        def _(pe):
            me = Side(pe, K)
            t = me.t

            def mm(out, lhsT, rhs, k, n):
                return pe.matmul(out, lhsT, rhs, start=(k == 0), stop=(k == n - 1))

            def square_sums(parts):
                pe.wait_ge(fed, me.next("fed"))
                pe.wait_ge(drained, me.first_bank())
                for sq, n, w in parts:
                    if me.reuses():
                        pe.wait_ge(drained, me.reused())
                    b = me.next_bank()
                    for k in range(n):
                        m = mm(b[:, 0:w], ones, sq[:, k, 0:w], k, n)
                    m.then_inc(filled, me.add("filled"))

            def transposed(parts):
                if me.reuses():
                    pe.wait_ge(drained, me.reused())
                b = me.next_bank()
                for in_, rows, at in parts:
                    m = pe.transpose(b[0:in_.shape[1], at:at + rows], in_, ident[0:rows, 0:rows])
                m.then_inc(filled, me.add("filled"))

            def dense(src, segs, then=None):
                pe.wait_ge(slab_loaded[me.slot()], me.landed())
                w = me.next_slab()
                for j in range(4):
                    for h, n in segs:
                        if me.reuses():
                            pe.wait_ge(drained, me.reused())
                        b = me.next_bank()
                        for k in range(KT):
                            m = mm(b[:, 0:n], w[:, k, j * 128:(j + 1) * 128], h[:, k, :], k, KT)
                        m.then_inc(filled, me.add("filled"))
                pe.drain().then_inc(slab_used, 1)

            pe.wait_ge(tables_loaded, 64)
            pe.wait_ge(answered, 1)
            with me.loop("ada", ADA_SLABS // RING) as i:
                for s in range(RING):
                    pe.wait_ge(slab_loaded[me.slot()], me.landed())
                    w = me.next_slab()
                    for j in range(4):
                        for k in range(KT):
                            m = mm(P[0][:, bass.ds(i * 8 * RING + 8 * s + 2 * j, 2)],
                                   w[:, k, j * 128:(j + 1) * 128], cs[:, k, :], k, KT)
                    m.then_inc(slab_used, 1)
            pe.drain().then_inc(filled, me.add("filled"))

            square_sums([(sqx, KT, NX), (sqc, KT, NC)])
            pe.wait_ge(fed, me.next("fed"))
            pe.wait_ge(drained, me.first_bank())
            pe.wait_ge(slab_loaded[me.slot()], me.landed())
            w = me.next_slab()
            wf = w[:, :, :].rearrange("p a b -> p (a b)")
            for tt in range(6):
                for g in range(4):
                    if me.reuses():
                        pe.wait_ge(drained, me.reused())
                    b = me.next_bank()
                    for k in range(2):
                        src = hx[:, 2 * g + k, tt * 128:(tt + 1) * 128] if tt < 4 else hc[:, 2 * g + k, (tt - 4) * 128:(tt - 3) * 128]
                        m = mm(b[:, :], src, wf[:, 512 * k:512 * k + 512], k, 2)
                    m.then_inc(filled, me.add("filled"))
            pe.wait_ge(fed, me.next("fed"))
            pe.wait_ge(drained, me.first_bank())
            pe.wait_ge(slab_loaded[me.slot()], me.landed())
            wx = me.next_slab()
            for f in range(KT):
                g, half = f // 2, f % 2
                for seg, tiles in ((0, range(0, 4)), (1, range(4, 6))):
                    if me.reuses():
                        pe.wait_ge(drained, me.reused())
                    b = me.next_bank()
                    n = 0
                    for part in range(2):
                        for j, tt in enumerate(tiles):
                            at = g * 512 + part * 256 + half * 128
                            if seg == 0:
                                rhs, wdt = wx[:, part * 4 + j, :], NX
                            else:
                                rhs, wdt = wf[:, 1024 + (part * 2 + j) * 256:1024 + (part * 2 + j + 1) * 256], NC
                            m = mm(b[:, 0:wdt], AB[:, tt, at:at + 128], rhs, n, 2 * len(tiles))
                            n += 1
                    m.then_inc(filled, me.add("filled"))
            pe.drain().then_inc(slab_used, 2)
            pe.wait_ge(fed, me.next("fed"))
            pe.wait_ge(drained, me.first_bank())
            for _ in range(2):
                dense(None, [(hx, NX), (hc, NC)])

            def moe(l, ctx):
                tiles = 6 if ctx else 4
                S_ = CAPX + CAPC if ctx else CAPX
                W = NX + NC * ctx
                square_sums([(sqx, KT, NX)] + [(sqc, KT, NC)] * ctx)
                pe.wait_ge(fed, me.next("fed"))
                pe.wait_ge(drained, me.first_bank())

                def htile(k, tt):
                    return hx[:, k, tt * 128:(tt + 1) * 128] if tt < 4 else hc[:, k, (tt - 4) * 128:(tt - 3) * 128]

                if me.reuses():
                    pe.wait_ge(drained, me.reused())
                b = me.next_bank()
                for tt in range(tiles):
                    for k in range(KT):
                        m = mm(b[:, tt * NE:(tt + 1) * NE], htile(k, tt), router[:, l, k, :], k, KT)
                m.then_inc(filled, me.add("filled"))
                for tt in range(tiles):
                    for half in range(2):
                        transposed([(htile(4 * half + j, tt), 128, 128 * j) for j in range(4)])
                pe.wait_ge(fed, me.next("fed"))
                transposed([(aff[:, tt, :], 128, 128 * tt) for tt in range(4)])
                if ctx:
                    transposed([(aff[:, tt, :], 128, 128 * (tt - 4)) for tt in range(4, 6)])
                pe.wait_ge(fed, me.next("fed"))
                if me.reuses():
                    pe.wait_ge(drained, me.reused())
                b = me.next_bank()
                for tt in range(tiles):
                    m = pe.transpose(b[:, tt * NE:(tt + 1) * NE], slot[0:NE, tt * 128:(tt + 1) * 128], ident[0:NE, 0:NE])
                m.then_inc(filled, me.add("filled"))
                with me.loop("expert_ctx" if ctx else "expert", NE):
                    pe.wait_ge(fed, me.next("fed"))
                    pe.wait_ge(drained, me.first_bank())
                    for half in range(2):
                        if me.reuses():
                            pe.wait_ge(drained, me.reused())
                        b = me.next_bank()
                        for j in range(4):
                            f = 4 * half + j
                            for tt in range(tiles):
                                m = mm(b[:, j * S_:(j + 1) * S_], htok[:, tt, f * 128:(f + 1) * 128], pick[:, tt, 0:S_], tt, tiles)
                        if half:
                            for tt in range(tiles):
                                m = mm(b[0:S_, 4 * S_:4 * S_ + 1], pick[:, tt, 0:S_], affe[:, tt:tt + 1], tt, tiles)
                        m.then_inc(filled, me.add("filled"))
                    if me.reuses():
                        pe.wait_ge(drained, me.reused())
                    b = me.next_bank()
                    mm(b[0:S_, 0:NX], esel[0:NE, 0:S_], slot[0:NE, 0:NX], 0, 1).then_inc(filled, me.add("filled"))
                    if me.reuses():
                        pe.wait_ge(drained, me.reused())
                    b = me.next_bank()
                    n = NC if ctx else 1
                    mm(b[0:S_, 0:n], esel[0:NE, 0:S_], slot[0:NE, W - n:W], 0, 1).then_inc(filled, me.add("filled"))
                    pe.wait_ge(fed, me.next("fed"))
                    for j in range(2):
                        for _ in range(2):
                            pe.wait_ge(slab_loaded[me.slot()], me.landed())
                            w = me.next_slab()
                            if me.reuses():
                                pe.wait_ge(drained, me.reused())
                            b = me.next_bank()
                            for m4 in range(4):
                                for k in range(KT):
                                    m = mm(b[:, m4 * S_:(m4 + 1) * S_], w[:, k, m4 * 128:(m4 + 1) * 128], xsT[:, k, 0:S_], k, KT)
                            m.then_inc(filled, me.add("filled"))
                            pe.drain().then_inc(slab_used, 1)
                    pe.wait_ge(fed, me.next("fed"))
                    for half in range(2):
                        pe.wait_ge(slab_loaded[me.slot()], me.landed())
                        w = me.next_slab()
                        if me.reuses():
                            pe.wait_ge(drained, me.reused())
                        b = me.next_bank()
                        for k in range(KT):
                            m = mm(b[0:S_, :], hid[:, k, 0:S_], w[:, k, :], k, KT)
                        m.then_inc(filled, me.add("filled"))
                        pe.drain().then_inc(slab_used, 1)
                    pe.wait_ge(fed, me.next("fed"))
                    for f in range(KT):
                        if me.reuses():
                            pe.wait_ge(drained, me.reused())
                        b = me.next_bank()
                        mm(b[:, 0:NX], ys[0:S_, f * 128:(f + 1) * 128], put[0:S_, 0:NX], 0, 1).then_inc(filled, me.add("filled"))
                        if ctx:
                            if me.reuses():
                                pe.wait_ge(drained, me.reused())
                            b = me.next_bank()
                            mm(b[:, 0:NC], ys[0:S_, f * 128:(f + 1) * 128], put[0:S_, NX:NX + NC], 0, 1).then_inc(filled, me.add("filled"))

            moe(0, True)

            square_sums([(sqx, KT, NX), (sqc, KT, NC)])
            pe.wait_ge(slab_loaded[me.slot()], me.landed())
            lora = me.next_slab()
            for j, what, mt, ns in W_MIX:
                segs = [(256, NX)] if what in "rg" else [(256, NX), (0, NC)]
                for half in range(ns):
                    if what in "wag":
                        w, first = lora, 128 * "wag".index(what)
                    else:
                        pe.wait_ge(slab_loaded[me.slot()], me.landed())
                        w, first = me.next_slab(), 0
                    pe.wait_ge(drained, me.first_bank())
                    banks = {(m4, at): me.next_bank() for m4 in range(mt) for at, _ in segs}
                    for k in range(KT):
                        pe.wait_ge(fed, me.next("fed"))
                        for m4 in range(mt):
                            for at, n in segs:
                                m = mm(banks[m4, at][:, 0:n], w[:, k, first + m4 * 128:first + (m4 + 1) * 128],
                                       mixed[k % 2][:, at:at + n], k, KT)
                                if k == KT - 1:
                                    m.then_inc(filled, me.add("filled"))
                        if k < KT - 1:
                            m.then_inc(mix_used, 1)
                    if what not in "wa":
                        pe.drain().then_inc(slab_used, 1)
            pe.wait_ge(slab_loaded[me.slot()], me.landed())
            me.next_slab()
            K.first = {"dve": t["filled"].n, "act": t["afilled"].n}
            K.orders = {"dve": PAIR_DVE, "act": PAIR_ACT}
            two = (slice(0, 64), slice(64, 128))


            def heads2(out, lhsT, rhs, k=0, n=1):
                for r in two:
                    m = pe.matmul(out[r], lhsT[r], rhs[r], start=(k == 0), stop=(k == n - 1))
                return m

            with me.loop("pair", KT) as i:
                me.pair = (i, {"dve": PER["pair"]["filled"], "act": PER["pair"]["afilled"]})
                pe.wait_ge(fed, me.next("fed"))
                pe.wait_ge(drained, me.first_bank())
                me.split_banks()
                for a, n in ((0, NC), (NC, NX)):
                    mm(me.next_bank()[:, 0:n], headones, ksq[:, a:a + n], 0, 1).then_inc(filled, me.add("filled"))
                for b in BATCHES:
                    if me.reuses():
                        pe.wait_ge(drained, me.reused())
                    p = me.next_bank()
                    pe.sem_inc(pe_steps)
                    for c in range(GC):
                        at = CH * (b.start + c)
                        m = heads2(p[:, c * CH:(c + 1) * CH], vp[:, at:at + CH], eye2)
                    m.then_inc(filled, me.add("filled"))
                for d in range(2):
                    rows = two[d]
                    for lhsT, rhs in ((w2p, HW), (a2p, HA)):
                        for a, n in ((0, NC), (NC, NX)):
                            if me.act_reuses() or d:
                                pe.wait_ge(drained_act, me.act_reused())
                            mm(me.next_act_bank()[:, 0:n], lhsT[rows, :], rhs[rows, a:a + n], 0, 1).then_inc(filled_act, me.add("afilled"))
                    pe.wait_ge(fed, me.next("fed"))
                    for bi, b in enumerate(BATCHES):
                        n = 2 * CH if bi else CH
                        for src in (bd, kd):
                            if me.reuses():
                                pe.wait_ge(drained, me.reused())
                            p = me.next_bank()
                            pe.sem_inc(pe_steps)
                            for c in range(GC):
                                at = CH * (b.start + c)
                                m = heads2(p[:, c * 128:c * 128 + n], src[:, at:at + CH], ar[:, b.start + c, 0:n])
                            m.then_inc(filled, me.add("filled"))
                        pe.wait_ge(drained_act, me.act_reused())
                        p = me.next_act_bank()
                        pe.sem_inc(pe_steps)
                        for c in range(GC):
                            at = CH * (b.start + c)
                            for q, src in enumerate((bd, kd)):
                                m = heads2(p[:, c * 128 + q * CH:c * 128 + (q + 1) * CH], src[:, at:at + CH], eye2)
                        m.then_inc(filled_act, me.add("afilled"))
                        pe.wait_ge(drained_act, me.act_reused())
                        p = me.next_act_bank()
                        pe.sem_inc(pe_steps)
                        for c in range(GC):
                            m = heads2(p[:, c * CH:(c + 1) * CH], ar[:, b.start + c, 0:CH], eye2)
                        m.then_inc(filled_act, me.add("afilled"))
                    for bi, b in enumerate(BATCHES):
                        pe.wait_ge(drained, me.group("dve", ("MT", d, bi)))
                        pe.wait_ge(drained_act, me.act_reused())
                        p = me.next_act_bank()
                        pe.sem_inc(pe_steps)
                        for c in range(GC):
                            m = heads2(p[:, c * CH:(c + 1) * CH], MT[:, b.start + c, :], Vt[:, b.start + c, :])
                        m.then_inc(filled_act, me.add("afilled"))
                    for bi, b in enumerate(BATCHES):
                        pe.wait_ge(masked, me.mask_value(i, mask_no(d, 0, bi)))
                        pe.wait_ge(drained, me.reused())
                        p = me.next_bank()
                        pe.sem_inc(pe_steps)
                        for c in range(GC):
                            m = heads2(p[:, c * CH:(c + 1) * CH], NL[:, b.start + c, :], eye2)
                        m.then_inc(filled, me.add("filled"))
                    for l in range(1, 6):
                        for bi, b in enumerate(BATCHES):
                            pe.wait_ge(masked, me.mask_value(i, mask_no(d, l, bi)))
                            pe.wait_ge(drained, me.group("dve", ("XX", d, l - 1, bi) if l > 1 else ("X0", d, bi)))
                            pe.wait_ge(drained_act, me.act_reused())
                            p = me.next_act_bank()
                            pe.sem_inc(pe_steps)
                            for c in range(GC):
                                m = heads2(p[:, c * CH:(c + 1) * CH], NL[:, b.start + c, :], X[:, b.start + c, :])
                            m.then_inc(filled_act, me.add("afilled"))
                        for bi, b in enumerate(BATCHES):
                            pe.wait_ge(drained_act, me.group("act", ("T", d, l, bi)))
                            pe.wait_ge(drained, me.reused())
                            p = me.next_bank()
                            pe.sem_inc(pe_steps)
                            for c in range(GC):
                                if l < 5:
                                    heads2(p[:, c * CH:(c + 1) * CH], XT[:, b.start + c, :], T[:, b.start + c, :])
                                m = heads2(p[:, 256 + c * CH:256 + (c + 1) * CH], T[:, b.start + c, :], XT[:, b.start + c, :])
                            m.then_inc(filled, me.add("filled"))
                    for bi, b in enumerate(BATCHES):
                        pe.wait_ge(drained, me.group("dve", ("XX", d, 5, bi)))
                        pe.wait_ge(drained_act, me.group("act", ("MV", d, bi)))
                        pe.wait_ge(drained_act, me.act_reused())
                        p = me.next_act_bank()
                        pe.sem_inc(pe_steps)
                        for c in range(GC):
                            m = heads2(p[:, c * 128:(c + 1) * 128], XT[:, b.start + c, :], AM[:, b.start + c, :])
                        m.then_inc(filled_act, me.add("afilled"))
                    for bi, b in enumerate(BATCHES):
                        pe.wait_ge(drained_act, me.group("act", ("WU", d, bi)))
                        pe.wait_ge(drained, me.reused())
                        p = me.next_bank()
                        pe.sem_inc(pe_steps)
                        for c in range(GC):
                            cc = b.start + c
                            m = heads2(p[:, c * 128:c * 128 + CH], WU[:, cc, 0:CH], BK[:, cc, 0:CH])
                            if bi:
                                m = heads2(p[:, c * 128 + CH:(c + 1) * 128], WU[:, cc, 0:CH], QB[:, cc - GC, :])
                        m.then_inc(filled, me.add("filled"))
                        pe.wait_ge(drained, me.reused())
                        p = me.next_bank()
                        pe.sem_inc(pe_steps)
                        for c in range(GC):
                            cc = b.start + c
                            for r in two:
                                pe.matmul(p[r, c * CH:(c + 1) * CH], BK[r, cc, 0:CH], WU[r, cc, CH:128], start=True, stop=False)
                                m = pe.matmul(p[r, c * CH:(c + 1) * CH], BK[r, cc, CH:128], Vt[r, cc, :], start=False, stop=True)
                        m.then_inc(filled, me.add("filled"))
                        if bi:
                            pe.wait_ge(drained, me.reused())
                            p = me.next_bank()
                            pe.sem_inc(pe_steps)
                            for c in range(GC):
                                cc = b.start + c
                                for r in two:
                                    pe.matmul(p[r, c * CH:(c + 1) * CH], WU[r, cc, CH:128], QB[r, cc - GC, :], start=True, stop=False)
                                    m = pe.matmul(p[r, c * CH:(c + 1) * CH], Vt[r, cc, :], QK[r, cc - GC, :], start=False, stop=True)
                            m.then_inc(filled, me.add("filled"))
                for j in range(1, NCH):
                    for d in range(2):
                        c = CHAIN[d][j]
                        pe.wait_ge(fed, me.next("fed"))
                        pe.sem_inc(pe_steps)
                        if c >= GC:
                            m = heads2(P[4 + d][:, CH * (c - GC):CH * (c - GC + 1)], Z[d], Rt[d][:, c - GC, :])
                        if j < NCH - 1:
                            pe.wait_ge(drained, me.reused())
                            pe.sem_inc(pe_steps)
                            m = heads2(me.next_bank()[:, 0:CH], At[d][:, c, :], Z[d])
                        m.then_inc(filled, me.add("filled"))
                        if j == NCH - 1:
                            me.next_bank()
                pe.wait_ge(fed, me.next("fed"))
                pe.wait_ge(drained, me.first_bank())
                mm(me.next_bank()[:, :], headones, Y, 0, 1).then_inc(filled, me.add("filled"))
                mm(me.next_bank()[:, :], headones, tb, 0, 1).then_inc(filled, me.add("filled"))
                mm(me.next_bank()[:, :], g2p, HG, 0, 1).then_inc(filled, me.add("filled"))
                pe.wait_ge(fed, me.next("fed"))
                mm(me.next_bank()[:, :], headones, tc, 0, 1).then_inc(filled, me.add("filled"))
            me.width = 8
            pe.wait_ge(fed, me.next("fed"))
            pe.wait_ge(drained, me.first_bank())
            for _ in range(2):
                dense(None, [(Rx, NX)])
            moe(1, False)
            square_sums([(sqx, KT, NX)])

            with me.loop("layer", 2):
                square_sums([(sq2, KT, NX)])
                pe.wait_ge(fed, me.next("fed"))
                pe.wait_ge(drained, me.first_bank())
                for sl in range(5):
                    pe.wait_ge(slab_loaded[me.slot()], me.landed())
                    w = me.next_slab()
                    for j in range(4 if sl < 4 else 2):
                        if me.reuses():
                            pe.wait_ge(drained, me.reused())
                        b = me.next_bank()
                        for k in range(KT):
                            m = mm(b[:, :], w[:, k, j * 128:(j + 1) * 128], hx[:, k, :], k, KT)
                        m.then_inc(filled, me.add("filled"))
                    if sl < 4:
                        pe.drain().then_inc(slab_used, 1)
                pe.wait_ge(slab_loaded[me.slot()], me.landed())
                w5 = me.next_slab()
                for ww, c0, n in ((w, 256, 256), (w5, 0, TM_W - 256)):
                    for tt in range(4):
                        if me.reuses():
                            pe.wait_ge(drained, me.reused())
                        b = me.next_bank()
                        for k in range(KT):
                            m = mm(b[:, 0:n], hx[:, k, tt * 128:(tt + 1) * 128], ww[:, k, c0:c0 + n], k, KT)
                        m.then_inc(filled, me.add("filled"))
                pe.drain().then_inc(slab_used, 2)
                pe.wait_ge(fed, me.next("fed"))
                pe.wait_ge(drained, me.first_bank())
                for tiles in ((0, 1), (2,)):
                    if me.reuses():
                        pe.wait_ge(drained, me.reused())
                    b = me.next_bank()
                    for k, j in enumerate(tiles):
                        m = mm(b[:, :], ones, S[:, j, :], k, len(tiles))
                    m.then_inc(filled, me.add("filled"))
                pe.wait_ge(fed, me.next("fed"))
                uq = aux[:, 0:768].rearrange("p (k n) -> p k n", k=2)
                ukv = aux[:, 768:1280]
                for j in range(3):
                    if me.reuses():
                        pe.wait_ge(drained, me.reused())
                    b = me.next_bank()
                    for k in range(2):
                        m = mm(b[:, :], uq[:, k, j * 128:(j + 1) * 128], Fm[:, k, :], k, 2)
                    m.then_inc(filled, me.add("filled"))
                for j in range(2):
                    if me.reuses():
                        pe.wait_ge(drained, me.reused())
                    b = me.next_bank()
                    mm(b[:, :], ukv[:, j * 128:(j + 1) * 128], Fm[:, 2, :], 0, 1).then_inc(filled, me.add("filled"))
                for tt in range(4):
                    if me.reuses():
                        pe.wait_ge(drained, me.reused())
                    b = me.next_bank()
                    mm(b[:, 0:256], Fm[:, 2, tt * 128:(tt + 1) * 128], ukv[:, 256:512], 0, 1).then_inc(filled, me.add("filled"))
                pe.wait_ge(fed, me.next("fed"))
                pe.wait_ge(drained, me.first_bank())
                for tl, j, d in ROPED:
                    if me.reuses():
                        pe.wait_ge(drained, me.reused())
                    b = me.next_bank()
                    mm(b[:, :], tab2(f"rot{d}"), tile(tl, j), 0, 1).then_inc(filled, me.add("filled"))
                for h in range(HEADS):
                    pe.wait_ge(fed, me.next("fed"))
                    if me.reuses():
                        pe.wait_ge(drained, me.reused())
                    b = me.next_bank()
                    for j in range(4):
                        at = 384 - 128 * j
                        m = mm(b[:, :], lfb[:, j, :], tab2("upto")[:, at:at + NX], j, 4)
                    m.then_inc(filled, me.add("filled"))
                for v in VARIANTS:
                    for i in range(4):
                        k0, k1 = span(v, i)
                        q = slice(128 * i, 128 * i + 128)
                        pe.wait_ge(fed, me.next("fed"))
                        pe.wait_ge(drained, me.first_bank())
                        if v == "dsa" and i > 0:
                            for h in range(8):
                                rows = slice(32 * (h % 4), 32 * (h % 4) + 32)
                                if me.reuses():
                                    pe.wait_ge(drained, me.reused())
                                b = me.next_bank()
                                mm(b[:, 0:k1], Fm[rows, 10 + h // 4, q], Fm[rows, 17, 0:k1], 0, 1).then_inc(filled, me.add("filled"))
                        for parts, _, _, _ in heads(v):
                            for qt, qj, kt_, kj, rows in parts:
                                if me.reuses():
                                    pe.wait_ge(drained, me.reused())
                                b = me.next_bank()
                                mm(b[:, 0:k1 - k0], tile(qt, qj)[rows, q], tile(kt_, kj)[rows, k0:k1], 0, 1).then_inc(filled, me.add("filled"))
                        pe.wait_ge(fed, me.next("fed"))
                        for h in range(HEADS):
                            transposed([(S[:, h, a:a + 128], 128, a) for a in range(0, k1 - k0, 128)])
                        pe.wait_ge(fed, me.next("fed"))
                        for h, (_, (vt, vc), _, _) in enumerate(heads(v)):
                            if me.reuses():
                                pe.wait_ge(drained, me.reused())
                            b = me.next_bank()
                            nk = (k1 - k0) // 128
                            for kk in range(nk):
                                m = mm(b[:, 0:128], vt[:, k0 // 128 + kk, vc:vc + 128], PT[:, h, kk * 128:(kk + 1) * 128], kk, nk)
                            m.then_inc(filled, me.add("filled"))
                pe.wait_ge(fed, me.next("fed"))
                pe.wait_ge(drained, me.first_bank())
                for _ in range(2):
                    dense(None, [(OT, NX)])
                square_sums([(sq2, KT, NX)])
                pe.wait_ge(fed, me.next("fed"))
                pe.wait_ge(drained, me.first_bank())
                for _ in range(8):
                    dense(None, [(hx, NX)])
                pe.wait_ge(fed, me.next("fed"))
                pe.wait_ge(drained, me.first_bank())
                for half in range(2):
                    banks = [me.next_bank() for _ in range(4)]
                    for kg in range(4):
                        pe.wait_ge(slab_loaded[me.slot()], me.landed())
                        w = me.next_slab()
                        for j in range(4):
                            for k in range(KT):
                                m = mm(banks[j][:, :], w[:, k, j * 128:(j + 1) * 128], up[:, kg * KT + k, :], kg * KT + k, 32)
                            if kg == 3:
                                m.then_inc(filled, me.add("filled"))
                        pe.drain().then_inc(slab_used, 1)
            square_sums([(sq2, KT, NX)])

        @block.scalar
        def _(act):
            me = Side(act, K)
            t = me.t

            def root(x):
                act.wait_ge(asked, me.next("asked"))
                act.activation(x, x, ACT.Sqrt)
                act.drain().then_inc(answered, me.add("answered"))

            act.wait_ge(tables_loaded, 64)
            act.activation(cs[:, :, :], vec("c").rearrange("p (k j) -> p k j", j=2), ACT.Silu)
            act.drain().then_inc(answered, me.add("answered"))
            root(rstd)

            def moe(l, ctx):
                tiles = 6 if ctx else 4
                S_ = CAPX + CAPC if ctx else CAPX
                root(rstd[:, 0:NX + NC * ctx])
                act.wait_ge(asked, me.next("asked"))
                act.activation(aff[:, 0:tiles, :], aff[:, 0:tiles, :], ACT.Exp)
                act.drain().then_inc(answered, me.add("answered"))
                with me.loop("expert_ctx" if ctx else "expert", NE):
                    for j in range(2):
                        act.wait_ge(asked, me.next("asked"))
                        act.activation(gact[:, :, 0:S_], P[4 + 2 * j][:, 0:4 * S_].rearrange("p (a b) -> p a b", a=4), ACT.Silu)
                        act.drain().then_inc(answered, me.add("answered"))

            moe(0, True)
            root(rstd)
            act.wait_ge(asked, me.next("asked"))
            act.dma_start(spill_d, rxf).then_inc(spilled, 16)
            for what, dst in (("w", HW), ("g", HG)):
                act.wait_ge(asked, me.next("asked"))
                if what == "w":
                    act.activation(HW[:, NC:NC + NX], P[0][:, :], ACT.Tanh)
                    act.activation(HW[:, 0:NC], P[1][:, 0:NC], ACT.Tanh)
                else:
                    act.activation(HG, P[0][:, :], ACT.Sigmoid)
                act.drain().then_inc(answered, me.add("answered"))
            with me.loop("pair", KT):
                me.split_banks()
                root(ksq)
                for d in range(2):
                    for q, dst in ((0, lw), (1, bd)):
                        for a, n in ((0, NC), (NC, NX)):
                            act.wait_ge(filled_act, me.next("afilled"))
                            act.activation(dst[:, a:a + n], me.next_act_bank()[:, 0:n], ACT.Sigmoid, bias=pp[:, 2 * q + d:2 * q + d + 1])
                            act.drain().then_inc(drained_act, 1)
                    act.wait_ge(asked, me.next("asked"))
                    act.activation(E1, E1, ACT.Exp)
                    act.activation(E3, Lc, ACT.Exp, scale=-1.0)
                    act.activation(ETd[d], ETd[d], ACT.Exp)
                    act.drain()
                    act.activation(Lc[:, NC:NC + NX], Lc[:, NC:NC + NX], ACT.Exp)
                    act.drain().then_inc(answered, me.add("answered"))
                    for b in BATCHES:
                        act.wait_ge(filled_act, me.next("afilled"))
                        act.activation(BK[:, b, :], me.next_act_bank()[:, :].rearrange("p (c n) -> p c n", c=GC), ACT.Copy)
                        act.drain().then_inc(drained_act, 1)
                        act.wait_ge(filled_act, me.next("afilled"))
                        act.activation(AM[:, b, 0:CH], me.next_act_bank()[:, 0:256].rearrange("p (c n) -> p c n", c=GC), ACT.Copy)
                        act.drain().then_inc(drained_act, 1)
                    for b in BATCHES:
                        act.wait_ge(filled_act, me.next("afilled"))
                        act.activation(AM[:, b, CH:128], me.next_act_bank()[:, 0:256].rearrange("p (c n) -> p c n", c=GC), ACT.Copy)
                        act.drain().then_inc(drained_act, 1)
                    for l in range(1, 6):
                        for b in BATCHES:
                            act.wait_ge(filled_act, me.next("afilled"))
                            act.activation(T[:, b, :], me.next_act_bank()[:, 0:256].rearrange("p (c n) -> p c n", c=GC), ACT.Copy)
                            act.drain().then_inc(drained_act, 1)
                    for b in BATCHES:
                        act.wait_ge(filled_act, me.next("afilled"))
                        act.activation(WU[:, b, :], me.next_act_bank()[:, :].rearrange("p (c n) -> p c n", c=GC), ACT.Copy)
                        act.drain().then_inc(drained_act, 1)
                root(ta)
            act.wait_ge(asked, me.next("asked"))
            act.dma_start(rxf, spill_d).then_inc(spilled, 16)
            moe(1, False)
            root(rstd[:, 0:NX])

            act.wait_ge(asked, me.next("asked"))
            act.dma_start(tabs2, tabs2_d).then_inc(tables_loaded, 16)
            with me.loop("layer", 2) as l:
                act.wait_ge(asked, me.next("asked"))
                act.dma_start(aux, aux_d[l]).then_inc(aux_loaded, 16)
                root(rstd2)
                root(S[:, 0:2, :])
                act.wait_ge(asked, me.next("asked"))
                act.activation(le, le, ACT.Exp)
                act.drain().then_inc(answered, me.add("answered"))
                act.wait_ge(asked, me.next("asked"))
                act.activation(le, le, ACT.Ln)
                act.drain().then_inc(answered, me.add("answered"))
                for v in VARIANTS:
                    for i in range(4):
                        n = span(v, i)[1] - span(v, i)[0]
                        act.wait_ge(asked, me.next("asked"))
                        for h in range(HEADS):
                            act.activation(S[:, h, 0:n], S[:, h, 0:n], ACT.Exp, bias=mxn[:, h:h + 1], accum_out=sums[:, h:h + 1])
                        if v == "swa":
                            act.activation(esink, esink, ACT.Exp)
                        act.drain().then_inc(answered, me.add("answered"))
                root(rstd2)
            root(rstd2)
            act.wait_ge(asked, me.next("asked"))
            act.dma_start(out_d.rearrange("(k p) t -> p k t", p=128), hx[:, :, :]).then_inc(stored, 16)
            act.wait_ge(stored, 16)

        @block.vector
        def _(v):
            me = Side(v, K)
            t = me.t

            def pass_on():
                v.memset(cell, 0.0)

            def tt(out, a, b, op):
                v.tensor_tensor(out, a, b, op)

            def ts(out, a, s1, op0, s2=None, op1=None):
                if op1 is None:
                    v.tensor_scalar(out, a, s1, None, op0)
                else:
                    v.tensor_scalar(out, a, s1, s2, op0, op1)

            def stt(out, a, s, b, op0, op1):
                v.scalar_tensor_tensor(out, a, s, b, op0, op1)

            def bc(x, *shape):
                return x.to_broadcast(list(shape))

            def inverse_roots(parts, root, eps):
                at = 0
                for w, n in parts:
                    v.wait_ge(filled, me.next("filled"))
                    b = me.next_bank()
                    ts(root[:, at:at + w], b[:, 0:w], 1.0 / n, ALU.mult, eps, ALU.add)
                    v.drain().then_inc(drained, 1)
                    at += w
                v.drain().then_inc(asked, me.add("asked"))
                v.wait_ge(answered, me.next("answered"))
                v.reciprocal(root[:, 0:at], root[:, 0:at])
                v.drain()

            def norm(segs, sqs, root, gains):
                for (res, h, n, j), sq in zip(segs, sqs):
                    tt(sq, res[:, :, :], res[:, :, :], ALU.mult)
                v.drain().then_inc(fed, me.add("fed"))
                me.first_bank()
                inverse_roots([(s[2], D) for s in segs], root, 1e-6)
                at = 0
                for res, h, n, j in segs:
                    tt(h[:, :, :], res[:, :, :], bc(root[:, at:at + n].unsqueeze(1), 128, KT, n), ALU.mult)
                    at += n
                v.drain()
                for res, h, n, j in segs:
                    for k in range(KT):
                        gain, shift = gains(k, j)
                        if shift is None:
                            ts(h[:, k, :], h[:, k, :], gain, ALU.mult)
                        else:
                            ts(h[:, k, :], h[:, k, :], gain, ALU.mult, shift, ALU.add)

            def modulated(l, which):
                return lambda k, j: (mod[:, l, 3 * which + 1, k, j:j + 1], mod[:, l, 3 * which, k, j:j + 1])

            v.wait_ge(tables_loaded, 64)
            t["answered"].n += 1
            v.wait_ge(filled, me.next("filled"))
            b = me.next_bank()
            mods = mod[:, :, :, :, :].rearrange("p l j k c -> p (l j k) c")
            tt(mods, b[:, 0:192].rearrange("p (q c) -> p q c", c=2), bc(vec("ada_b").unsqueeze(2), 128, 96, 2), ALU.add)
            v.drain().then_inc(drained, 1)
            for l in range(2):
                for j in range(2):
                    m = mod[:, l, 3 * j + 1, :, :]
                    stt(m, m, 1.0, bc(norm_g[:, l, j, :].unsqueeze(2), 128, KT, 2), ALU.add, ALU.mult)
            v.drain()

            norm([segx, segc], [sqx, sqc], rstd, modulated(0, 0))
            v.drain().then_inc(fed, me.add("fed"))
            me.first_bank()
            for tile_ in range(6):
                for g in range(4):
                    v.wait_ge(filled, me.next("filled"))
                    b = me.next_bank()
                    v.tensor_copy(AB[:, tile_, g * 512:(g + 1) * 512], b[:, :])
                    v.drain().then_inc(drained, 1)
            v.drain().then_inc(fed, me.add("fed"))
            me.first_bank()
            for f in range(KT):
                for h, n in ((hx, NX), (hc, NC)):
                    v.wait_ge(filled, me.next("filled"))
                    b = me.next_bank()
                    v.tensor_copy(h[:, f, :], b[:, 0:n])
                    v.drain().then_inc(drained, 1)
            v.drain().then_inc(fed, me.add("fed"))
            me.first_bank()
            tmp = cut(work, 0, NX)
            for f in range(KT):
                for res, h, n, j in (segx, segc):
                    v.wait_ge(filled, me.next("filled"))
                    b = me.next_bank()
                    ts(tmp[:, 0:n], b[:, 0:n], vec("fnet_bo")[:, f:f + 1], ALU.add, mod[:, 0, 2, f, j:j + 1], ALU.mult)
                    v.drain().then_inc(drained, 1)
                    tt(res[:, f, :], res[:, f, :], tmp[:, 0:n], ALU.add)
                    v.drain()

            def moe(l, ctx):
                tiles = 6 if ctx else 4
                S_ = CAPX + CAPC if ctx else CAPX
                W = NX + NC * ctx
                segs = [segx, segc] if ctx else [segx]
                norm(segs, [sqx, sqc], rstd, modulated(l, 1))
                v.drain().then_inc(fed, me.add("fed"))
                me.first_bank()
                v.wait_ge(filled, me.next("filled"))
                b = me.next_bank()
                lg = b[:, 0:tiles * NE].rearrange("p (t e) -> p t e", e=NE)
                af, am = aff[:, 0:tiles, :], amax[:, 0:tiles]
                v.tensor_reduce(am, lg, AX, ALU.max)
                v.drain()
                tt(af, lg, bc(am.unsqueeze(2), 128, tiles, NE), ALU.subtract)
                v.drain().then_inc(drained, 1)
                v.drain().then_inc(asked, me.add("asked"))
                v.wait_ge(answered, me.next("answered"))
                v.tensor_reduce(am, af, AX, ALU.add)
                v.drain()
                v.reciprocal(am, am)
                v.drain()
                tt(af, af, bc(am.unsqueeze(2), 128, tiles, NE), ALU.mult)
                v.drain().then_inc(fed, me.add("fed"))
                for tile_ in range(tiles):
                    for half in range(2):
                        v.wait_ge(filled, me.next("filled"))
                        b = me.next_bank()
                        v.tensor_copy(htok[:, tile_, half * 512:(half + 1) * 512], b[:, :])
                        v.drain().then_inc(drained, 1)
                v.wait_ge(filled, me.next("filled"))
                b = me.next_bank()
                v.tensor_copy(affT[0:NE, 0:NX], b[0:NE, :])
                v.drain().then_inc(drained, 1)
                if ctx:
                    v.wait_ge(filled, me.next("filled"))
                    b = me.next_bank()
                    v.tensor_copy(affT[0:NE, NX:W], b[0:NE, 0:NC])
                    v.drain().then_inc(drained, 1)
                v.memset(ones768[0:NE, 0:W], 1.0)
                v.tensor_copy(left[0:NE, 0:W], affT[0:NE, 0:W])
                for a, n, cap, first in ((0, NX, CAPX, 0.0), (NX, NC, CAPC, float(CAPX)))[:1 + ctx]:
                    part = left[0:NE, a:a + n]
                    for _ in range(cap // 8):
                        v.drain()
                        v.max(top8[0:NE, :], part)
                        v.drain()
                        v.match_replace(part, top8[0:NE, :], part, -1.0)
                v.drain()
                ts(left[0:NE, 0:W], left[0:NE, 0:W], -1.0, ALU.is_equal)
                v.drain()
                for a, n, first in ((0, NX, 0.0), (NX, NC, float(CAPX)))[:1 + ctx]:
                    v.tensor_tensor_scan(slot[0:NE, a:a + n], ones768[0:NE, a:a + n], left[0:NE, a:a + n], first, ALU.mult, ALU.add)
                v.drain()
                tt(slot[0:NE, 0:W], slot[0:NE, 0:W], left[0:NE, 0:W], ALU.mult)
                v.drain()
                ts(slot[0:NE, 0:W], slot[0:NE, 0:W], -1.0, ALU.add)
                v.drain().then_inc(fed, me.add("fed"))
                v.wait_ge(filled, me.next("filled"))
                b = me.next_bank()
                v.tensor_copy(stok[:, 0:tiles, :], b[:, 0:tiles * NE].rearrange("p (t e) -> p t e", e=NE))
                v.drain().then_inc(drained, 1)
                with me.loop("expert_ctx" if ctx else "expert", NE) as e:
                    me.first_bank()
                    tt(pick[:, 0:tiles, 0:S_], bc(tab("iota_row")[:, 0:S_].unsqueeze(1), 128, tiles, S_),
                       bc(stok[:, 0:tiles, bass.ds(e, 1)], 128, tiles, S_), ALU.is_equal)
                    v.tensor_copy(esel[0:NE, 0:S_], bc(ident[0:NE, bass.ds(e, 1)], NE, S_))
                    v.tensor_copy(affe[:, 0:tiles].unsqueeze(2), aff[:, 0:tiles, bass.ds(e, 1)])
                    v.drain().then_inc(fed, me.add("fed"))
                    for half in range(2):
                        v.wait_ge(filled, me.next("filled"))
                        b = me.next_bank()
                        v.tensor_copy(xsT[:, 4 * half:4 * half + 4, 0:S_], b[:, 0:4 * S_].rearrange("p (a b) -> p a b", a=4))
                        if half:
                            v.tensor_copy(gate[0:S_, :], b[0:S_, 4 * S_:4 * S_ + 1])
                        v.drain().then_inc(drained, 1)
                    v.drain().then_inc(fed, me.add("fed"))
                    v.wait_ge(filled, me.next("filled"))
                    b = me.next_bank()
                    ts(put[0:S_, 0:NX], b[0:S_, :], tab("iota_col")[0:S_, :], ALU.is_equal)
                    v.drain().then_inc(drained, 1)
                    v.wait_ge(filled, me.next("filled"))
                    b = me.next_bank()
                    if ctx:
                        ts(put[0:S_, NX:W], b[0:S_, 0:NC], tab("iota_col")[0:S_, :], ALU.is_equal)
                    else:
                        pass_on()
                    v.drain().then_inc(drained, 1)
                    for j in range(2):
                        v.wait_ge(filled, me.next("filled"))
                        me.next_bank()
                        v.wait_ge(filled, me.next("filled"))
                        bu = me.next_bank()
                        pass_on()
                        v.drain().then_inc(asked, me.add("asked"))
                        v.wait_ge(answered, me.next("answered"))
                        tt(hid[:, 4 * j:4 * j + 4, 0:S_], gact[:, :, 0:S_], bu[:, 0:4 * S_].rearrange("p (a b) -> p a b", a=4), ALU.mult)
                        v.drain().then_inc(drained, 2)
                    v.drain().then_inc(fed, me.add("fed"))
                    for half in range(2):
                        v.wait_ge(filled, me.next("filled"))
                        b = me.next_bank()
                        ts(ys[0:S_, half * 512:(half + 1) * 512], b[0:S_, :], gate[0:S_, :], ALU.mult)
                        v.drain().then_inc(drained, 1)
                    v.drain().then_inc(fed, me.add("fed"))
                    for f in range(KT):
                        for res, h, n, j in segs:
                            v.wait_ge(filled, me.next("filled"))
                            b = me.next_bank()
                            stt(res[:, f, :], b[:, 0:n], mod[:, l, 5, f, j:j + 1], res[:, f, :], ALU.mult, ALU.add)
                            v.drain().then_inc(drained, 1)

            moe(0, True)

            norm([segx, segc], [sqx, sqc], rstd, modulated(1, 0))
            v.drain()
            hxg = hx[:, :, :].rearrange("p k (r c) -> p k r c", c=64)
            dx, dxg = diff[:, NC:NC + NX], diff[:, NC:NC + NX].rearrange("p (r c) -> p r c", c=64)
            dc = diff[:, 0:NC]

            def shifted(k):
                g = hxg[:, k, :, :]
                src, dst, edge = [
                    ((slice(None), slice(0, 63)), (slice(None), slice(1, 64)), (slice(None), slice(0, 1))),
                    ((slice(None), slice(1, 64)), (slice(None), slice(0, 63)), (slice(None), slice(63, 64))),
                    ((slice(0, 7), slice(None)), (slice(1, 8), slice(None)), (slice(0, 1), slice(None))),
                    ((slice(1, 8), slice(None)), (slice(0, 7), slice(None)), (slice(7, 8), slice(None)))][k // 2]
                tt(dxg[:, dst[0], dst[1]], g[:, src[0], src[1]], g[:, dst[0], dst[1]], ALU.subtract)
                ts(dxg[:, edge[0], edge[1]], g[:, edge[0], edge[1]], -1.0, ALU.mult)
                c = hc[:, k, :]
                s, d, e = ((slice(0, NC - 1), slice(1, NC), slice(0, 1)) if k < KT // 2 else
                           (slice(1, NC), slice(0, NC - 1), slice(NC - 1, NC)))
                tt(dc[:, d], c[:, s], c[:, d], ALU.subtract)
                ts(dc[:, e], c[:, e], -1.0, ALU.mult)

            stream = 0
            v.drain().then_inc(asked, me.add("asked"))
            for j, what, mt, ns in W_MIX:
                for half in range(ns):
                    me.first_bank()
                    for k in range(KT):
                        shifted(k)
                        v.drain()
                        if k >= 2:
                            v.wait_ge(mix_used, stream * (KT - 1) + k - 1)
                        m = mixed[k % 2]
                        stt(m[:, NC:NC + NX], dx, mixes[:, j, k:k + 1], hx[:, k, :], ALU.mult, ALU.add)
                        stt(m[:, 0:NC], dc, mixes[:, j, k:k + 1], hc[:, k, :], ALU.mult, ALU.add)
                        v.drain().then_inc(fed, me.add("fed"))
                    stream += 1
                    if what in "wg":
                        v.wait_ge(filled, me.next("filled"))
                        me.next_bank()
                        if what == "w":
                            v.wait_ge(filled, me.next("filled"))
                            me.next_bank()
                        v.drain().then_inc(asked, me.add("asked"))
                        v.wait_ge(answered, me.next("answered"))
                        v.drain().then_inc(drained, 2 if what == "w" else 1)
                        continue
                    if what == "a":
                        v.wait_ge(filled, me.next("filled"))
                        b = me.next_bank()
                        v.tensor_copy(HA[:, NC:NC + NX], b[:, :])
                        v.drain().then_inc(drained, 1)
                        v.wait_ge(filled, me.next("filled"))
                        b = me.next_bank()
                        v.tensor_copy(HA[:, 0:NC], b[:, 0:NC])
                        v.drain().then_inc(drained, 1)
                        continue
                    for m4 in range(mt):
                        f = half * 4 + m4
                        v.wait_ge(filled, me.next("filled"))
                        b = me.next_bank()
                        v.tensor_copy({"r": Rx, "k": Kx, "v": Vx}[what][:, f, :], b[:, :])
                        v.drain().then_inc(drained, 1)
                        if what != "r":
                            v.wait_ge(filled, me.next("filled"))
                            b = me.next_bank()
                            v.tensor_copy({"k": Kc, "v": Vc}[what][:, f, :], b[:, 0:NC])
                            v.drain().then_inc(drained, 1)

            s = t["slab"]
            s.n = ADA_SLABS + FNET_SLABS + NE * EXPERT_SLABS + 7
            lora = ring[s.n % RING]
            v.wait_ge(slab_loaded[s.n % RING], 16 * (s.n // RING + 1))
            lora2 = lora[:, :, :].rearrange("p a b -> p (a b)")
            v.wait_ge(spilled, 16)
            with me.loop("pair", KT) as p:
                me.pair = (p, {"dve": PER["pair"]["filled"], "act": PER["pair"]["afilled"]})
                v.tensor_copy(pp[:, 0:9], rwp[:, bass.ds(p, 1), :].rearrange("p a b -> p (a b)"))
                for q, dst in enumerate((w2p, a2p, g2p)):
                    v.tensor_copy(dst, lora2[:, bass.ds(p * 128 + 1024 * q, 128)])
                kx, kc, vx, vc, rx = (z[:, bass.ds(p, 1), :].rearrange("p a b -> p (a b)") for z in (Kx, Kc, Vx, Vc, Rx))
                v.tensor_copy(vp[:, 0:NC], vc)
                v.tensor_copy(vp[:, NC:768], vx)
                v.drain()
                ts(pp[:, 9:10], pp[:, 5:6], -1.0, ALU.mult, 1.0, ALU.add)
                ts(kkv[:, 0:NC], kc, pp[:, 4:5], ALU.mult)
                ts(kkv[:, NC:768], kx, pp[:, 4:5], ALU.mult)
                v.drain()
                tt(ksq, kkv, kkv, ALU.mult)
                v.drain().then_inc(fed, me.add("fed"))
                me.split_banks()
                for a, n in ((0, NC), (NC, NX)):
                    v.wait_ge(filled, me.next("filled"))
                    b = me.next_bank()
                    ts(ksq[:, a:a + n], b[:, 0:n], 1e-12, ALU.add)
                    v.drain().then_inc(drained, 1)
                v.drain().then_inc(asked, me.add("asked"))
                for b in BATCHES:
                    v.wait_ge(filled, me.next("filled"))
                    v.tensor_copy(Vt[:, b, :], me.next_bank()[:, 0:256].rearrange("p (c n) -> p c n", c=GC))
                    v.drain().then_inc(drained, 1)
                v.wait_ge(answered, me.next("answered"))
                v.reciprocal(ksq, ksq)
                v.drain()
                tt(kkn, kkv, ksq, ALU.mult)
                chunked = "p (c n) -> p c n"
                for d in range(2):
                    v.wait_ge(drained_act, me.group("act", ("pre", d, 3)))
                    ts(lw, lw, -math.exp(-0.5), ALU.mult)
                    ts(kd, bd, pp[:, 5:6], ALU.mult, pp[:, 9:10], ALU.add)
                    v.drain()
                    v.tensor_tensor_scan(Lc, tab("chunk"), lw, 0.0, ALU.mult, ALU.add)
                    tt(kd[:, 0:NC], kd[:, 0:NC], kc, ALU.mult)
                    tt(kd[:, NC:768], kd[:, NC:768], kx, ALU.mult)
                    tt(bd, bd, kkn, ALU.mult)
                    v.drain()
                    L3 = Lc.rearrange(chunked, c=NCH)
                    ET3 = ETd[d].unsqueeze(2)
                    v.tensor_copy(ET3, L3[:, :, CH - 1:CH])
                    v.drain()
                    if d == 1:
                        tt(L3, bc(ET3, 128, NCH, CH), L3, ALU.subtract)
                        v.drain()
                        tt(Lc, Lc, lw, ALU.add)
                        v.drain()
                    tt(E1, Lc, lw, ALU.subtract)
                    v.drain().then_inc(asked, me.add("asked"))
                    if d == 0:
                        v.tensor_copy(ksum, kd[:, NC:768])
                    else:
                        tt(ksum, ksum, kd[:, NC:768], ALU.add)
                    v.drain()
                    v.wait_ge(answered, me.next("answered"))
                    stt(ar[:, :, 0:CH], kkn.rearrange(chunked, c=NCH), -1.0, E1.rearrange(chunked, c=NCH), ALU.mult, ALU.mult)
                    tt(ar[:, GC:NCH, CH:128], rx.rearrange(chunked, c=NCX), L3[:, GC:NCH, :], ALU.mult)
                    tt(bd, bd, E3, ALU.mult)
                    tt(kd, kd, E3, ALU.mult)
                    v.drain().then_inc(fed, me.add("fed"))
                    for bi, b in enumerate(BATCHES):
                        xb = slice(b.start - GC, b.stop - GC)
                        for dst, mask, q in ((NT, None, QB), (MT, tab("strict")[:, d * CH:(d + 1) * CH], QK)):
                            v.wait_ge(filled, me.next("filled"))
                            p3 = me.next_bank()[:, :].rearrange(chunked, c=GC)
                            if mask is None:
                                v.tensor_copy(dst[:, b, :], p3[:, :, 0:CH])
                            else:
                                tt(dst[:, b, :], p3[:, :, 0:CH], bc(mask.unsqueeze(1), 128, GC, CH), ALU.mult)
                            if bi:
                                tt(q[:, xb, :], p3[:, :, CH:128], bc(tab("incl")[:, d * CH:(d + 1) * CH].unsqueeze(1), 128, GC, CH), ALU.mult)
                            v.drain().then_inc(drained, 1)
                    for b in BATCHES:
                        v.wait_ge(filled, me.next("filled"))
                        tt(X[:, b, :], me.next_bank()[:, 0:256].rearrange(chunked, c=GC), bc(eye2.unsqueeze(1), 128, GC, CH), ALU.add)
                        v.drain().then_inc(drained, 1)
                    for l in range(1, 6):
                        for b in BATCHES:
                            v.wait_ge(filled, me.next("filled"))
                            p4 = me.next_bank()[:, :].rearrange("p (x c n) -> p x c n", x=2, c=GC)
                            if l < 5:
                                tt(XX[:, :, b, :], XX[:, :, b, :], p4, ALU.add)
                            else:
                                tt(XT[:, b, :], XT[:, b, :], p4[:, 1, :, :], ALU.add)
                            v.drain().then_inc(drained, 1)
                    for bi, b in enumerate(BATCHES):
                        xb = slice(b.start - GC, b.stop - GC)
                        v.wait_ge(filled, me.next("filled"))
                        p3 = me.next_bank()[:, :].rearrange(chunked, c=GC)
                        tt(At[d][:, b, :], p3[:, :, 0:CH], bc(eye2.unsqueeze(1), 128, GC, CH), ALU.add)
                        if bi:
                            tt(Rt[d][:, xb, :], p3[:, :, CH:128], ar[:, b, CH:128], ALU.add)
                        v.drain().then_inc(drained, 1)
                        v.wait_ge(filled, me.next("filled"))
                        p3 = me.next_bank()[:, 0:256].rearrange(chunked, c=GC)
                        tt(Bc[d][:, b, :], p3, bc(ETd[d][:, b].unsqueeze(2), 128, GC, CH), ALU.mult)
                        v.drain().then_inc(drained, 1)
                        if bi:
                            v.wait_ge(filled, me.next("filled"))
                            p2 = me.next_bank()[:, 0:256]
                            y = Y[:, 256 * (bi - 1):256 * bi]
                            if d == 0:
                                v.tensor_copy(y, p2)
                            else:
                                tt(y, y, p2, ALU.add)
                            v.drain().then_inc(drained, 1)
                for d in range(2):
                    v.tensor_copy(Z[d], Bc[d][:, CHAIN[d][0], :])
                    v.drain().then_inc(fed, me.add("fed"))
                for j in range(1, NCH):
                    for d in range(2):
                        c = CHAIN[d][j]
                        v.wait_ge(filled, me.next("filled"))
                        p2 = me.next_bank()
                        if j < NCH - 1:
                            stt(Z[d], p2[:, 0:CH], ETd[d][:, c:c + 1], Bc[d][:, c, :], ALU.mult, ALU.add)
                            v.drain().then_inc(drained, 1)
                            v.drain().then_inc(fed, me.add("fed"))
                        else:
                            tt(Y, Y, P[4 + d][:, :], ALU.add)
                            v.drain().then_inc(drained, 1)
                tt(tb, rx, ksum, ALU.mult)
                v.drain()
                ts(tb, tb, pp[:, 6:7], ALU.mult)
                v.drain().then_inc(fed, me.add("fed"))
                me.first_bank()
                v.wait_ge(filled, me.next("filled"))
                b = me.next_bank()
                stt(Y, b[:, :], -1.0 / CH, Y, ALU.mult, ALU.add)
                v.drain().then_inc(drained, 1)
                tt(tc, Y, Y, ALU.mult)
                v.drain().then_inc(fed, me.add("fed"))
                v.wait_ge(filled, me.next("filled"))
                b = me.next_bank()
                tt(ksum, b[:, :], vx, ALU.mult)
                v.drain().then_inc(drained, 1)
                v.wait_ge(filled, me.next("filled"))
                b = me.next_bank()
                v.tensor_copy(tb, b[:, :])
                v.drain().then_inc(drained, 1)
                v.wait_ge(filled, me.next("filled"))
                b = me.next_bank()
                ts(ta, b[:, :], 1.0 / CH, ALU.mult, 64e-5, ALU.add)
                v.drain().then_inc(drained, 1)
                v.drain().then_inc(asked, me.add("asked"))
                v.wait_ge(answered, me.next("answered"))
                v.reciprocal(ta, ta)
                v.drain()
                tt(Y, Y, ta, ALU.mult)
                v.drain()
                ts(Y, Y, pp[:, 7:8], ALU.mult, pp[:, 8:9], ALU.add)
                v.drain()
                tt(Y, Y, ksum, ALU.add)
                v.drain()
                tt(rx, Y, tb, ALU.mult)
                v.drain()
            me.width = 8
            v.drain().then_inc(asked, me.add("asked"))
            v.wait_ge(spilled, 32)
            v.drain().then_inc(slab_used, 1)
            v.drain().then_inc(fed, me.add("fed"))
            me.first_bank()
            for f in range(KT):
                v.wait_ge(filled, me.next("filled"))
                b = me.next_bank()
                stt(resx[:, f, :], b[:, :], mod[:, 1, 2, f, 0:1], resx[:, f, :], ALU.mult, ALU.add)
                v.drain().then_inc(drained, 1)
            v.drain()
            moe(1, False)
            v.drain()
            norm([segx], [sqx], rstd, lambda k, j: (vec("final_g")[:, k:k + 1], None))
            v.drain()
            v.tensor_copy(resx[:, :, :], hx[:, :, :])

            v.drain().then_inc(asked, me.add("asked"))
            v.wait_ge(tables_loaded, 80)
            with me.loop("layer", 2) as l:
                v.tensor_copy(pv, layer2[:, bass.ds(l, 1), :].rearrange("p a b -> p (a b)"))
                v.drain().then_inc(asked, me.add("asked"))
                segs = [(resx, hx, NX, 0)]
                norm(segs, [sq2], rstd2, lambda k, j: (pv[:, k:k + 1], None))
                v.drain().then_inc(fed, me.add("fed"))
                me.first_bank()
                for f in range(F_TILES):
                    v.wait_ge(filled, me.next("filled"))
                    b = me.next_bank()
                    v.tensor_copy(Fm[:, f, :], b[:, :])
                    v.drain().then_inc(drained, 1)
                for c0, n in ((0, 256), (256, TM_W - 256)):
                    for i in range(4):
                        v.wait_ge(filled, me.next("filled"))
                        b = me.next_bank()
                        v.tensor_copy(VT[:, i, c0:c0 + n], b[:, 0:n])
                        v.drain().then_inc(drained, 1)
                v.drain()
                tt(S[:, 0:3, :], Fm[:, 0:3, :], Fm[:, 0:3, :], ALU.mult)
                v.drain().then_inc(fed, me.add("fed"))
                me.first_bank()
                inverse_roots([(NX, 256), (NX, 128)], S[:, 0:2, :].rearrange("p a b -> p (a b)"), 1e-6)
                for k in range(3):
                    stt(Fm[:, k, :], Fm[:, k, :], pv[:, 16 + k:17 + k], S[:, k // 2, :], ALU.mult, ALU.mult)
                tt(lf, VT[:, :, TM_W - 4:TM_W], bc(pv[:, 23:27].unsqueeze(1), 128, 4, 4), ALU.add)
                v.drain()
                stt(le, lf, -1.0, lf, ALU.mult, ALU.min)
                v.drain().then_inc(asked, me.add("asked"))
                v.wait_ge(answered, me.next("answered"))
                ts(le, le, 1.0, ALU.add)
                v.drain().then_inc(asked, me.add("asked"))
                v.wait_ge(answered, me.next("answered"))
                stt(lf, lf, 0.0, le, ALU.min, ALU.subtract)
                v.wait_ge(aux_loaded, l * 16 + 16)
                pass_on()
                v.drain().then_inc(fed, me.add("fed"))
                for dst, j in ((QN, 0), (QN, 1), (QR, None), (KN, 0), (KN, 1)):
                    v.wait_ge(filled, me.next("filled"))
                    b = me.next_bank()
                    v.tensor_copy(tile(dst, j), b[:, :])
                    v.drain().then_inc(drained, 1)
                for i in range(4):
                    v.wait_ge(filled, me.next("filled"))
                    b = me.next_bank()
                    v.tensor_copy(VA[:, i, :], b[:, 0:256])
                    v.drain().then_inc(drained, 1)
                v.drain().then_inc(fed, me.add("fed"))
                me.first_bank()
                for dst, j, d in ROPED:
                    x = tile(dst, j)
                    v.wait_ge(filled, me.next("filled"))
                    b = me.next_bank()
                    tt(S[:, 0, :], b[:, :], tab2(f"sin{d}"), ALU.mult)
                    v.drain().then_inc(drained, 1)
                    tt(x, x, tab2(f"cos{d}"), ALU.mult)
                    v.drain()
                    tt(x, x, S[:, 0, :], ALU.add)
                    v.drain()
                for h in range(HEADS):
                    v.tensor_copy(lfb, bc(lf[:, :, h:h + 1], 128, 4, 128))
                    v.drain().then_inc(fed, me.add("fed"))
                    v.wait_ge(filled, me.next("filled"))
                    b = me.next_bank()
                    v.tensor_copy(cumk[:, h, :], b[:, :])
                    v.drain().then_inc(drained, 1)
                for va in VARIANTS:
                    for i in range(4):
                        k0, k1 = span(va, i)
                        n = k1 - k0
                        v.drain().then_inc(fed, me.add("fed"))
                        me.first_bank()
                        causal = tab2("causal")[:, 384 - 128 * i + k0:384 - 128 * i + k1]
                        mask = causal
                        if va == "swa":
                            mask = tab2("window")[:, 384 - 128 * i + k0:384 - 128 * i + k1]
                        if va == "dsa" and i > 0:
                            sc, rs = score[:, 0:n], rest[:, 0:n]
                            for h in range(8):
                                v.wait_ge(filled, me.next("filled"))
                                b = me.next_bank()
                                wcol = VT[:, i, 640 + h:641 + h]
                                ts(rs if h else sc, b[:, 0:n], 0.0, ALU.max, wcol, ALU.mult)
                                v.drain().then_inc(drained, 1)
                                if h:
                                    tt(sc, sc, rs, ALU.add)
                                    v.drain()
                            tt(rs, sc, causal, ALU.add)
                            for _ in range(TOPK // 8):
                                v.drain()
                                v.max(t8, rs)
                                v.drain()
                                v.match_replace(rs, t8, rs, -3e38)
                            v.drain()
                            ts(keep[:, 0:n], rs, -2e38, ALU.is_gt, NEG, ALU.mult)
                            v.drain()
                            mask = keep[:, 0:n]
                        for h, (parts, _, _, _) in enumerate(heads(va)):
                            v.wait_ge(filled, me.next("filled"))
                            b = me.next_bank()
                            if va == "fox":
                                tt(PT[:, h, 0:n], causal, cumk[:, h, 0:n], ALU.subtract)
                                v.drain()
                                mask = PT[:, h, 0:n]
                            stt(S[:, h, 0:n], b[:, 0:n], SCALE[va], mask, ALU.mult, ALU.add)
                            v.drain().then_inc(drained, 1)
                            if len(parts) == 2:
                                v.wait_ge(filled, me.next("filled"))
                                b = me.next_bank()
                                stt(S[:, h, 0:n], b[:, 0:n], SCALE[va], S[:, h, 0:n], ALU.mult, ALU.add)
                                v.drain().then_inc(drained, 1)
                        v.tensor_reduce(mx, S[:, :, 0:n], AX, ALU.max)
                        v.drain()
                        if va == "swa":
                            tt(mx, mx, pv[:, 19:23], ALU.max)
                            v.drain()
                            tt(esink, pv[:, 19:23], mx, ALU.subtract)
                        ts(mxn, mx, -1.0, ALU.mult)
                        v.drain().then_inc(asked, me.add("asked"))
                        v.wait_ge(answered, me.next("answered"))
                        if va == "swa":
                            tt(sums, sums, esink, ALU.add)
                            v.drain()
                        v.reciprocal(sums, sums)
                        v.drain()
                        tt(S[:, :, 0:n], S[:, :, 0:n], bc(sums.unsqueeze(2), 128, HEADS, n), ALU.mult)
                        v.drain().then_inc(fed, me.add("fed"))
                        for h in range(HEADS):
                            v.wait_ge(filled, me.next("filled"))
                            b = me.next_bank()
                            v.tensor_copy(PT[:, h, 0:n], b[:, 0:n])
                            v.drain().then_inc(drained, 1)
                        v.drain().then_inc(fed, me.add("fed"))
                        for _, _, ot, rows in heads(va):
                            v.wait_ge(filled, me.next("filled"))
                            b = me.next_bank()
                            v.tensor_copy(OT[rows, ot, 128 * i:128 * i + 128], b[rows, 0:128])
                            v.drain().then_inc(drained, 1)
                v.drain().then_inc(fed, me.add("fed"))
                me.first_bank()
                for f in range(KT):
                    v.wait_ge(filled, me.next("filled"))
                    b = me.next_bank()
                    tt(resx[:, f, :], resx[:, f, :], b[:, :], ALU.add)
                    v.drain().then_inc(drained, 1)
                v.drain()
                norm(segs, [sq2], rstd2, lambda k, j: (pv[:, 8 + k:9 + k], None))
                v.drain().then_inc(fed, me.add("fed"))
                me.first_bank()
                for f in range(32):
                    v.wait_ge(filled, me.next("filled"))
                    b = me.next_bank()
                    ts(up[:, f, :], b[:, :], 0.0, ALU.max)
                    v.drain().then_inc(drained, 1)
                    tt(up[:, f, :], up[:, f, :], up[:, f, :], ALU.mult)
                v.drain().then_inc(fed, me.add("fed"))
                me.first_bank()
                for f in range(KT):
                    v.wait_ge(filled, me.next("filled"))
                    b = me.next_bank()
                    tt(resx[:, f, :], resx[:, f, :], b[:, :], ALU.add)
                    v.drain().then_inc(drained, 1)
                v.drain()
            norm([(resx, hx, NX, 0)], [sq2], rstd2, lambda k, j: (vec("final2")[:, k:k + 1], None))
            v.drain().then_inc(asked, me.add("asked"))

        @block.gpsimd
        def _(pool):
            me = Side(pool, K)
            with me.loop("pair", KT) as i:
                me.pair = (i, {"dve": PER["pair"]["filled"], "act": PER["pair"]["afilled"]})
                for d in range(2):
                    for l in range(6):
                        for bi, b in enumerate(BATCHES):
                            if l == 0:
                                pool.wait_ge(drained, me.group("dve", ("NT", d, bi)))
                            elif l == 1:
                                pool.wait_ge(drained, me.group("dve", ("X0", d, bi)))
                            else:
                                pool.wait_ge(drained_act, me.group("act", ("T", d, l - 1, bi)))
                            m = levels[:, d, l, :].unsqueeze(1).to_broadcast([128, GC, CH])
                            pool.tensor_tensor(NL[:, b, :], NT[:, b, :], m, ALU.mult)
                            if l == 0:
                                pool.drain()
                                pool.tensor_tensor(XT[:, b, :], NL[:, b, :], eye2.unsqueeze(1).to_broadcast([128, GC, CH]), ALU.add)
                            pool.drain().then_inc(masked, me.add("masked"))

        if K.wrong:
            raise ValueError(f"counts of the loops: {sorted(K.wrong)}")


def shape_tables():
    f = np.float32
    p = np.arange(128)
    t1 = {}
    t1["ident"] = np.eye(128)
    t1["ones"] = np.ones((128, 128))
    t1["headones"] = (p[:, None] // 64 == p[None, :] // 64) * 1.0
    t1["iota_row"] = np.broadcast_to(np.arange(96), (128, 96))
    t1["iota_col"] = p[:, None]
    t1["chunk"] = np.broadcast_to((np.arange(768) % CH != 0) * 1.0, (128, 768))
    s, t = p[:, None] % CH, np.arange(CH)[None, :]
    lev = []
    for d in range(2):
        a, b = (s, t) if d == 0 else (t, s)
        for l in range(6):
            n = 2 ** l
            lev.append((a // (2 * n) == b // (2 * n)) & (a // n % 2 == 0) & (b // n % 2 == 1))
    t1["level"] = np.concatenate(lev, 1)
    t1["strict"] = np.concatenate([s < t, s > t], 1)
    t1["incl"] = np.concatenate([s <= t, s >= t], 1)
    t1["eye2"] = (s == t) * 1.0
    t2 = {}
    pos = np.arange(512, dtype=f)
    for d in (64, 32):
        half = d // 2
        inv = (1.0 / (f(10000.0) ** (np.arange(half, dtype=f) * f(2.0) / f(d)))).astype(f)
        ang = (inv[p % half][:, None] * pos[None, :]).astype(f)
        t2[f"cos{d}"], t2[f"sin{d}"] = np.cos(ang), np.sin(ang)
        rot = np.zeros((128, 128))
        for r in range(128):
            if r % d < half:
                rot[r + half, r] = -1.0
            else:
                rot[r - half, r] = 1.0
        t2[f"rot{d}"] = rot
    x = np.arange(896)[None, :] - 384
    q = p[:, None]
    t2["causal"] = np.where(x <= q, 0.0, NEG)
    t2["window"] = np.where((x <= q) & (q - x < 128), 0.0, NEG)
    t2["upto"] = (x >= q) * 1.0
    pack = lambda t, order: np.ascontiguousarray(np.concatenate([t[n] for n in order], 1).astype(f))
    n = np.arange(256)
    ang = 2 * np.pi * (np.outer(n, n) % 256) / 256
    feat = np.concatenate([np.cos(ang), np.sin(ang)], 1)
    fc = feat.reshape(2, 128, 512).transpose(1, 0, 2).reshape(128, 1024)

    def seq(T):
        m = np.arange(T)
        a = 2 * np.pi * (np.outer(m, m) % T) / T
        r = 1.0 / math.sqrt(T * 256)
        both = np.stack([np.cos(a) * r, -np.sin(a) * r])
        return both.reshape(2, T // 128, 128, T).transpose(2, 0, 1, 3).reshape(128, -1)

    first = np.zeros((128, 4096))
    first[:, 0:1024] = fc
    first[:, 1024:2048] = seq(256)
    return pack(t1, TAB1), pack(t2, TAB2), first.astype(f), seq(512).astype(f)


def lay_out(i):
    f = np.float32
    g = {k: np.asarray(a) for k, a in i.items()}
    tabs1, tabs2, fnet1, fnet2 = shape_tables()
    slabs = np.zeros((SLABS, 128, 4096), f)
    n = 0

    def add(w):
        nonlocal n
        k, cols = w.shape
        for c in range(0, cols, 512):
            part = w[:, c:c + 512]
            slabs[n].reshape(128, 8, 512)[:, 0:k // 128, 0:part.shape[1]] = part.reshape(k // 128, 128, -1).transpose(1, 0, 2)
            n += 1

    def moe(l):
        for e in range(NE):
            for h in range(2):
                add(g["moe_wg"][l, e][:, 512 * h:512 * h + 512])
                add(g["moe_wu"][l, e][:, 512 * h:512 * h + 512])
            add(g["moe_wd"][l, e])

    for l in range(2):
        add(g["ada_w"][l])
    slabs[n], slabs[n + 1] = fnet1, fnet2
    n += 2
    add(g["fnet_wo"][0])
    moe(0)
    add(np.concatenate([g["rw_w1"][0, 0], g["rw_w1"][0, 1], g["rw_a1"][0, 0], g["rw_a1"][0, 1], g["rw_g1"][0]], 1))
    for w in ("rw_wr", "rw_wk", "rw_wv"):
        add(g[w][0])
    slabs[n][:, 0:1024] = g["rw_w2"][0].reshape(128, D)
    slabs[n][:, 1024:2048] = g["rw_a2"][0].reshape(128, D)
    slabs[n][:, 2048:3072] = g["rw_g2"][0]
    n += 1
    add(g["rw_wo"][0])
    moe(1)
    sizes = [256, 128, 32, 256, 128, 128, 256, 256, 256, 256, 32, 8, 256, 256, 256, 4]
    ends = np.cumsum(sizes)
    cols = [np.arange(e - s, e) for s, e in zip(sizes, ends)]
    (acq, ackv, akr, bq, bk, bv, cq, ck, cv, cqi, cki, cw, dq, dk, dv, df) = cols
    swap = np.concatenate([np.arange(64 * h, 64 * h + 64) for h in (0, 2, 1, 3)])
    order = np.concatenate([acq, ackv, bq[swap], bk, cq, ck, cqi, dq, dk, np.tile(akr, 4), np.tile(cki, 4), bv, cv, dv, cw, df])
    mixed_rows = np.arange(D)
    mixed_rows[256:512] = 256 + swap
    aux = np.zeros((2, 128, 1280), f)
    nope = np.concatenate([np.arange(96 * h, 96 * h + 64) for h in range(4)] + [np.arange(96 * h + 64, 96 * h + 96) for h in range(4)])
    kv = np.concatenate([np.arange(128 * h, 128 * h + 64) for h in range(4)] + [np.arange(128 * h + 64, 128 * h + 128) for h in range(4)])
    for l in range(2):
        add(g["w_in_2"][l][:, order])
        add(g["w_out_2"][l][mixed_rows])
        add(g["w_up_2"][l])
        for h in range(2):
            for kg in range(4):
                add(g["w_down_2"][l][kg * D:(kg + 1) * D, 512 * h:512 * h + 512])
        aux[l][:, 0:768] = g["mla_w_uq_2"][l][:, nope].reshape(2, 128, 384).transpose(1, 0, 2).reshape(128, 768)
        aux[l][:, 768:] = g["mla_w_ukv_2"][l][:, kv]
    assert n == SLABS, n

    def tiles(v):
        return v.reshape(-1, 128).T

    def rows(v):
        return np.broadcast_to(v.reshape(1, -1), (128, v.size))

    parts = {
        "c": np.stack([tiles(g["c"][0]), tiles(g["c_ctx"])], 2).reshape(128, 16),
        "ada_b": tiles(g["ada_b"]), "norm_g": tiles(g["norm_g"]), "fnet_bo": tiles(g["fnet_bo"]),
        "final_g": tiles(g["final_g"]), "mix": tiles(g["rw_mix"][0]),
        "rwp": np.stack([tiles(z) for z in (g["rw_w0"][0, 0], g["rw_w0"][0, 1], g["rw_a0"][0, 0], g["rw_a0"][0, 1], g["rw_kk"][0],
                                            g["rw_ka"][0], g["rw_rk"][0].reshape(-1), g["rw_lnx_w"][0], g["rw_lnx_b"][0])], 2).reshape(128, 72),
        "router": g["moe_router"].reshape(2, 8, 128, 16).transpose(2, 0, 1, 3).reshape(128, 256),
        "layer2": np.concatenate([np.concatenate([
            tiles(g["norm1_2"][l]), tiles(g["norm2_2"][l]), tiles(g["mla_q_norm_2"][l]), tiles(g["mla_kv_norm_2"][l]),
            rows(g["swa_sinks_2"][l][[0, 2, 1, 3]]), rows(g["fox_b_f_2"][l])], 1) for l in range(2)], 1),
        "final2": tiles(g["final_norm_2"]),
    }
    vecs = np.ascontiguousarray(np.concatenate([parts[k] for k in VEC], 1))
    return {"slabs": slabs, "vecs": vecs, "tabs1": tabs1, "tabs2": tabs2, "aux": aux,
            "xT": np.ascontiguousarray(g["x"][0].T), "ctxT": np.ascontiguousarray(g["ctx"][0].T)}


def kernel(**inputs):
    import numpy as _np
    import concourse.bacc as _bacc
    from concourse import mybir as _mybir
    from concourse.bass_utils import run_bass_kernel_spmd as _run

    nc = _bacc.Bacc("TRN2", target_bir_lowering=False, num_devices=1)
    arrays = lay_out(inputs)
    args = [nc.dram_tensor(name, a.shape, _mybir.dt.from_np(a.dtype), kind="ExternalInput").ap() for name, a in arrays.items()]
    out = nc.dram_tensor("outT", (D, NX), _mybir.dt.float32, kind="ExternalOutput").ap()
    spill = nc.dram_tensor("spill", (128, KT * NX), _mybir.dt.float32, kind="Internal").ap()
    build(nc, *args, out, spill)
    r = _run(nc, [arrays], core_ids=[0])
    return _np.ascontiguousarray(r.results[0]["outT"].T)[None]
```

```python
import concourse.bass as bass
from concourse import mybir
from contextlib import ExitStack, contextmanager
import math
import numpy as np

D = 1024
KT = D // 128
NX, NC = 512, 256
NE = 16
CAPX, CAPC = 2 * NX // NE, 2 * NC // NE
FILL = CAPX + CAPC
HALF = 512
RING = 3
ADA_SLABS, FNET_SLABS, EXPERT_SLABS, RWKV_SLABS, LAYER_SLABS = 24, 4, 6, 10, 24
SLABS = ADA_SLABS + FNET_SLABS + 2 * NE * EXPERT_SLABS + RWKV_SLABS + 2 * LAYER_SLABS
WORK = 24 * 1024 + 256 + NX
LORA_SLAB = ADA_SLABS + FNET_SLABS + NE * EXPERT_SLABS + 7
CH, GC = 64, 4
NCH, NCX = (NX + NC) // CH, NX // CH
HEADS = 4
TOPK = 128
NEG = -1e30
F_TILES = 18
TM_W = 652

VEC = {}
_n = 0
for _name, _w in [("c", 16), ("ada_b", 96), ("norm_g", 32), ("fnet_bo", 8), ("final_g", 8), ("mix", 48),
                  ("rwp", 72), ("router", 256), ("layer2", 54), ("final2", 8)]:
    VEC[_name] = (_n, _n + _w)
    _n += _w
NVEC = _n
TAB1 = {}
_n = 0
for _name, _w in [("ident", 128), ("ones", 128), ("headones", 128), ("iota_row", CAPX + CAPC), ("iota_col", 2),
                  ("chunk", 768), ("level", 12 * CH), ("strict", 2 * CH), ("incl", 2 * CH),
                   ("eye2", CH)]:
    TAB1[_name] = (_n, _n + _w)
    _n += _w
NTAB1 = _n
TAB2 = {}
_n = 0
for _name, _w in [("cos64", 512), ("sin64", 512), ("cos32", 512), ("sin32", 512), ("rot64", 128), ("rot32", 128),
                  ("causal", 896), ("window", 896), ("upto", 896)]:
    TAB2[_name] = (_n, _n + _w)
    _n += _w
NTAB2 = _n

PER = {
    "expert_ctx": dict(slab=12, filled=32, fed=7, asked=4, answered=4),
    "expert": dict(slab=12, filled=24, fed=7, asked=4, answered=4),
    "pair": dict(slab=0, filled=95, fed=27, asked=4, answered=4, afilled=62, masked=36),
    "layer": dict(slab=24, filled=271, fed=10, asked=22, answered=21, afilled=64, weighted=16, normalised=16),
    "ada": dict(slab=3, filled=3, fed=0, asked=0, answered=0),
}


class Tally:

    def __init__(self):
        self.n = 0
        self.loops = []

    def at(self, more=0):
        v = self.n + more
        for i, per in self.loops:
            v = i * per + v
        return v


def place_in(order, name):
    return order.index(name) + 1


class Side:

    def __init__(self, eng, K):
        self.eng, self.K = eng, K
        self.t = {k: Tally() for k in ("slab", "filled", "fed", "asked", "answered", "afilled", "masked", "weighted", "normalised")}
        self.bank, self.abank, self.width = 0, 0, 8

    def add(self, name):
        self.t[name].n += 1
        return 1

    def next(self, name):
        self.t[name].n += 1
        return self.t[name].at()

    def first_bank(self):
        self.bank = 0
        return self.t["filled"].at()

    def reuses(self):
        return self.bank >= self.width

    def reused(self):
        return self.t["filled"].at(1 - self.width)

    def next_bank(self):
        self.bank += 1
        return self.K.banks[(self.bank - 1) % self.width]

    def split_banks(self):
        self.bank, self.abank, self.width = 0, 0, 4

    def next_act_bank(self):
        self.abank += 1
        return self.K.banks[4 + (self.abank - 1) % 4]

    def act_reuses(self):
        return self.abank >= 4

    def act_reused(self):
        return self.t["afilled"].at(-3)

    def mask_value(self, i, no):
        return i * PER["pair"]["masked"] + no

    def group(self, order, name):
        i, per = self.pair
        return i * per[order] + (self.K.first[order] + place_in(self.K.orders[order], name))

    def slot(self):
        return self.t["slab"].n % RING

    def landed(self):
        turn = self.t["slab"]
        v = 16 * (turn.n // RING + 1)
        for i, per in turn.loops:
            v = i * (16 * per // RING) + v
        return v

    def next_slab(self):
        self.t["slab"].n += 1
        return self.K.ring[(self.t["slab"].n - 1) % RING]

    @contextmanager
    def loop(self, name, turns):
        first = {k: t.n for k, t in self.t.items()}
        with self.eng.Fori(0, turns) as i:
            for k, t in self.t.items():
                t.loops.append((i, PER[name].get(k, 0)))
            yield i
            for k, t in self.t.items():
                t.loops.pop()
                got = t.n - first[k]
                if got and got != PER[name].get(k, 0):
                    self.K.wrong.add((name, k, got))
                if got:
                    t.n = first[k] + PER[name].get(k, 0) * turns


def build(nc, slabs_d, vecs_d, tabs1_d, tabs2_d, aux_d, x_d, ctx_d, out_d, spill_d):
    f32 = mybir.dt.float32
    ALU = mybir.AluOpType
    ACT = mybir.ActivationFunctionType
    AX = mybir.AxisListType.X
    stack = ExitStack()
    with stack:
        def sb(name, shape):
            return stack.enter_context(nc.sbuf_tensor(name, shape, f32))

        def sem(name):
            return stack.enter_context(nc.semaphore(name))

        ring = [sb(f"ring{s}", [128, KT, HALF]) for s in range(RING)]
        resx, resc = sb("resx", [128, KT, NX]), sb("resc", [128, KT, NC])
        hx, hc = sb("hx", [128, KT, NX]), sb("hc", [128, KT, NC])
        vecs, tabs1 = sb("vecs_sb", [128, NVEC]), sb("tabs1_sb", [128, NTAB1])
        mod = sb("mod", [128, 2, 6, KT, 2])
        cs = sb("cs", [128, KT, 2])
        cell = sb("cell", [1, 1])[:, :]
        work = sb("work", [128, WORK])
        P = [stack.enter_context(nc.psum_tensor(f"bank{i}", [128, 512], f32)) for i in range(8)]

        slab_loaded = [sem(f"slab_loaded{s}") for s in range(RING)]
        filled_act, drained_act, masked, spilled, pe_steps, weighted, normalised = (sem(n) for n in ("filled_act", "drained_act", "masked", "spilled", "pe_steps", "weighted", "normalised"))
        slab_used, filled, drained, fed, mix_used = (sem(n) for n in ("slab_used", "filled", "drained", "fed", "mix_used"))
        asked, answered, tables_loaded, aux_loaded, stored = (sem(n) for n in ("asked", "answered", "tables_loaded", "aux_loaded", "stored"))

        class K:
            wrong = set()
            banks = P

        K.ring = ring

        def vec(name):
            return vecs[:, VEC[name][0]:VEC[name][1]]

        def tab(name):
            return tabs1[:, TAB1[name][0]:TAB1[name][1]]

        def cut(whole, at, *shape):
            n = math.prod(shape)
            v = whole[:, at:at + n]
            if len(shape) == 2:
                v = v.rearrange("p (a b) -> p a b", a=shape[0])
            if len(shape) == 3:
                v = v.rearrange("p (a b c) -> p a b c", a=shape[0], b=shape[1])
            return v

        def flat(t):
            return t[:, :, :].rearrange("p a b -> p (a b)")

        ident, ones, headones = tab("ident"), tab("ones"), tab("headones")
        levels = tab("level").rearrange("p (d l c) -> p d l c", d=2, l=6)
        strict = tab("strict").rearrange("p (d c) -> p d c", d=2)
        incl = tab("incl").rearrange("p (d c) -> p d c", d=2)
        norm_g = vec("norm_g").rearrange("p (l j k) -> p l j k", l=2, j=2)
        mixes = vec("mix").rearrange("p (j k) -> p j k", j=6)
        rwp = vec("rwp").rearrange("p (q j) -> p q j", q=KT)
        router = vec("router").rearrange("p (l k e) -> p l k e", l=2, k=KT)
        layer2 = vec("layer2").rearrange("p (l j) -> p l j", l=2)
        segx = (resx, hx, NX, 0)
        segc = (resc, hc, NC, 1)

        sqx, sqc = cut(work, 0, KT, NX), cut(work, KT * NX, KT, NC)
        rstd = cut(work, KT * (NX + NC), NX + NC)

        adarow = work[:, 0:ADA_SLABS * HALF]
        AB = cut(work, 0, 6, 4 * 512)

        htok = cut(work, 0, 6, D)
        o = 6 * D
        aff_wide, o = cut(work, o, 6, NE + 2), o + 6 * (NE + 2)
        stok, o = cut(work, o, 6, NE + 2), o + 6 * (NE + 2)
        aff = aff_wide[:, :, 0:NE]
        amax, o = cut(work, o, 6), o + 6
        affe, o = cut(work, o, 2, 6), o + 12
        affT, o = cut(work, o, 768), o + 768
        left, o = cut(work, o, 768), o + 768
        slot, o = cut(work, o, 768), o + 768
        top8, o = cut(work, o, 8), o + 8
        pickx, o = cut(work, o, 4, 2 * CAPX), o + 8 * CAPX
        pickc, o = cut(work, o, 2, 2 * CAPC), o + 4 * CAPC
        xtok, o = cut(work, o, D), o + D
        ctok, o = cut(work, o, D // 2), o + D // 2
        eselx, o = cut(work, o, 2 * CAPX), o + 2 * CAPX
        eselc, o = cut(work, o, 2 * CAPC), o + 2 * CAPC
        xsT, o = [cut(work, o + j * KT * 96, KT, 96) for j in range(2)], o + 2 * KT * 96
        hid, o = [cut(work, o + j * KT * 96, KT, 96) for j in range(2)], o + 2 * KT * 96
        gact, o = cut(work, o, 4, 96), o + 4 * 96
        putx, o = cut(work, o, NX), o + NX
        putc, o = cut(work, o, NC), o + NC
        gate, o = cut(work, o, 2), o + 2
        ysx, o = cut(work, o, D), o + D
        ysc, o = cut(work, o, D), o + D
        ones768, o = cut(work, o, 768), o + 768

        Rx, o = cut(work, 0, KT + 1, NX), (KT + 1) * NX
        Kx, o = cut(work, o, KT, NX), o + KT * NX
        Vx, o = cut(work, o, KT, NX), o + KT * NX
        Kc, o = cut(work, o, KT, NC), o + KT * NC
        Vc, o = cut(work, o, KT, NC), o + KT * NC
        HW, o = cut(work, o, 768), o + 768
        HA, o = cut(work, o, 768), o + 768
        HG, o = cut(work, o, NX), o + NX
        rw0 = o
        diff = cut(work, o, 768)
        mixed = [cut(work, o + 768 * (j + 1), 768) for j in range(2)]
        NT, MT, QB, QK, BK, AM = ([] for _ in range(6))
        for names, *shape in ((NT, NCH, CH), (MT, NCH, CH), (QB, NCX, CH), (QK, NCX, CH), (BK, NCH, 2 * CH), (AM, NCH, 2 * CH)):
            names.append(cut(work, o, *shape))
            o += math.prod(shape)
        Vt, o = cut(work, o, NCH, CH), o + 768
        assert o <= WORK, o
        kkv = work[:, rw0:rw0 + 768]
        ksq = work[:, rw0 + 768:rw0 + 1536]
        hxf, hcf, rcf, rxf = flat(hx), flat(hc), flat(resc), flat(resx)
        ring_v0, ring_v1, ring_lora = (flat(ring[(LORA_SLAB + q) % RING]) for q in (-2, -1, 0))
        o = 0
        for names, *shape in ((BK, NCH, 2 * CH), (AM, NCH, 2 * CH), (QB, NCX, CH), (QK, NCX, CH)):
            names.append(cut(ring_v0, o, *shape))
            o += math.prod(shape)
        NT.append(cut(ring_v1, 3072, NCH, CH))
        MT.append(cut(ring_lora, 3 * D, NCH, CH))
        ar = [cut(z, at, NCH, 2 * CH) for z, at in ((hxf, 0), (ring_v1, 0))]
        scaled = [z[:, 1536:3072] for z in (hxf, ring_v1)]
        bd, kd = ([z[:, j:j + 768] for z in scaled] for j in (0, 768))
        kkn = hxf[:, 3072:3840]
        w2p, a2p = (hxf[:, 3840 + j * 128:3968 + j * 128] for j in range(2))
        lw, Lc, E1, E3 = ([z[:, j * 768:(j + 1) * 768] for z in (rxf, ring_v0)] for j in range(4))
        XX = [z.rearrange("p (x c n) -> p x c n", x=2, c=NCH) for z in (rxf[:, 0:1536], scaled[0])]
        X, XT = ([z[:, j, :, :] for z in XX] for j in range(2))
        T = MT
        NL = [rxf[:, 1536 + j * 768:1536 + (j + 1) * 768].rearrange("p (c n) -> p c n", c=NCH) for j in range(2)]
        WU = [z.rearrange("p (c n) -> p c n", c=NCH) for z in (rxf[:, 1536:3072], scaled[1])]
        Y = rxf[:, 3072:3584]
        vp, ksum, squares = hcf[:, 0:768], rcf[:, 1536:2048], hcf[:, 1536:2048]
        g2p, Zs, ET, pp, lnx = rxf[:, 3584:3712], rxf[:, 3712:3840], rxf[:, 3840:3864], rxf[:, 3864:3874], rxf[:, 3874:3876]
        Z = [Zs[:, d * CH:(d + 1) * CH] for d in range(2)]
        ETd = [ET[:, d * NCH:(d + 1) * NCH] for d in range(2)]
        At, Bc, Rt = [], [], []
        for z in (hcf, rcf):
            At.append(z[:, 0:768].rearrange("p (c n) -> p c n", c=NCH))
            Bc.append(z[:, 768:1536].rearrange("p (c n) -> p c n", c=NCH))
            Rt.append(z[:, 1536:2048].rearrange("p (c n) -> p c n", c=NCX))
        eye2 = tab("eye2")

        tabs2 = cut(work, 0, NTAB2)
        o = NTAB2
        o2 = o

        def tab2(name):
            return tabs2[:, TAB2[name][0]:TAB2[name][1]]

        Fm, o = cut(work, o, F_TILES, NX), o + F_TILES * NX
        VT, o = cut(work, o, 4, TM_W), o + 4 * TM_W
        QN, o = cut(work, o, 2, NX), o + 2 * NX
        QR, o = cut(work, o, NX), o + NX
        KN, o = cut(work, o, 2, NX), o + 2 * NX
        VA, o = cut(work, o, 4, 256), o + 4 * 256
        S, o = cut(work, o, HEADS, NX), o + HEADS * NX
        PT, o = cut(work, o, HEADS, NX), o + HEADS * NX
        assert o <= WORK, o
        up = cut(work, o2, 32, NX)
        sq2 = cut(work, o2, KT, NX)
        ring_in = flat(ring[(SLABS - 2 * LAYER_SLABS + 5) % RING])
        SS, PTs = ([z, cut(ring_in, j * HEADS * NX, HEADS, NX)] for j, z in enumerate((S, PT)))
        score, rest, keep = Fm[:, 0, :], Fm[:, 1, :], Fm[:, 2, :]
        cumk = rcf.rearrange("p (h n) -> p h n", h=HEADS)
        aux = hcf[:, 0:1280]
        pv = hcf[:, 1280:1307]
        lf = hcf[:, 1312:1328].rearrange("p (j h) -> p j h", j=4)
        le = hcf[:, 1328:1344].rearrange("p (j h) -> p j h", j=4)
        mx, mxn, sums, esink = ([hcf[:, at + 4 * j:at + 4 * j + 4] for at in (1344, 1920)] for j in range(4))
        t8 = hcf[:, 1360:1368]
        lfb = PT.rearrange("p h (j n) -> p h j n", j=4)
        rstd2 = PT[:, 0, :]
        OT = hx

        def heads(v):
            out = []
            for h in range(HEADS):
                r, r32 = 64 * (h % 2), 32 * h
                rows, rows32 = slice(r, r + 64), slice(r32, r32 + 32)
                if v == "mla":
                    out.append(([(QN, h // 2, KN, h // 2, rows), (QR, None, Fm, 16, rows32)],
                                (VA, 128 * (h // 2)), h // 2, rows))
                elif v == "swa":
                    out.append(([(Fm, 3 + h // 2, Fm, 5, rows)], (VT, 0), 2 + h // 2, rows))
                elif v == "dsa":
                    out.append(([(Fm, 6 + h // 2, Fm, 8 + h // 2, rows)], (VT, 128 + 128 * (h // 2)), 4 + h // 2, rows))
                else:
                    out.append(([(Fm, 12 + h // 2, Fm, 14 + h // 2, rows)], (VT, 384 + 128 * (h // 2)), 6 + h // 2, rows))
            return out

        SCALE = {"mla": 96 ** -0.5, "swa": 64 ** -0.5, "dsa": 64 ** -0.5, "fox": 64 ** -0.5}
        VARIANTS = ("mla", "swa", "dsa", "fox")
        ROPED = [(Fm, 3, 64), (Fm, 4, 64), (Fm, 5, 64), (Fm, 6, 64), (Fm, 7, 64), (Fm, 8, 64), (Fm, 9, 64),
                 (QR, None, 32), (Fm, 10, 32), (Fm, 11, 32), (Fm, 16, 32), (Fm, 17, 32)]
        FORGETS = {3 * h + 2: h for h in range(HEADS)}

        def tile(t, j):
            return t if j is None else t[:, j, :]

        def span(v, i):
            return (128 * max(0, i - 1) if v == "swa" else 0), 128 * (i + 1)

        ATTENTION = [(v, i) for v in VARIANTS for i in range(4)]

        CHAIN = [tuple(range(NCH)), (3, 2, 1, 0) + tuple(range(NCH - 1, 3, -1))]
        BATCHES = [slice(GC * b, GC * b + GC) for b in range(3)]
        UNITS = [(d_, bi_, b_) for d_ in range(2) for bi_, b_ in enumerate(BATCHES)]
        PAIR_DVE = [("sum", 0), ("sum", 1)]
        PAIR_DVE += [(n_, d_, b_) for d_, b_, _ in UNITS for n_ in ("NT", "MT")]
        PAIR_DVE += [("vt", b_) for b_ in range(3)] + [("bonus",)]
        PAIR_DVE += [("X0", d_, b_) for d_, b_, _ in UNITS] + [("mean",)]
        for l_ in range(1, 6):
            PAIR_DVE += [("XX", d_, l_, b_) for d_, b_, _ in UNITS]
            PAIR_DVE += {1: [("var",)], 2: [("gate",)]}.get(l_, [])
        PAIR_DVE += [(n_, d_, b_) for d_, b_, _ in UNITS for n_ in ("AR", "Bc", "Y0") if b_ or n_ != "Y0"]
        PAIR_ACT = [("pre", d_, j_) for d_ in range(2) for j_ in range(4)]
        PAIR_ACT += [(n_, d_, b_) for d_, b_, _ in UNITS for n_ in ("BK", "At")]
        PAIR_ACT += [("MV", d_, b_) for d_, b_, _ in UNITS]
        PAIR_ACT += [("T", d_, l_, b_) for l_ in range(1, 6) for d_, b_, _ in UNITS]
        PAIR_ACT += [("WU", d_, b_) for d_, b_, _ in UNITS]

        def mask_no(d, l, b):
            return 6 * l + 3 * d + b + 1

        W_MIX = [(1, "w", 1, 1), (4, "a", 1, 1), (5, "g", 1, 1), (0, "r", 4, 2), (2, "k", 4, 2), (3, "v", 4, 2)]

        block = stack.enter_context(nc.Block())

        @block.sync
        def _(sp):
            sp.dma_start(vecs[:, :], vecs_d).then_inc(tables_loaded, 16)
            sp.dma_start(tabs1[:, :], tabs1_d).then_inc(tables_loaded, 16)
            sp.dma_start(resx[:, :, :], x_d.rearrange("(k p) t -> p k t", p=128)).then_inc(tables_loaded, 16)
            sp.dma_start(resc[:, :, :], ctx_d.rearrange("(k p) t -> p k t", p=128)).then_inc(tables_loaded, 16)
            for s in range(RING):
                sp.dma_start(flat(ring[s]), slabs_d[s]).then_inc(slab_loaded[s], 16)
            rounds = SLABS // RING
            with sp.Fori(1, rounds) as i:
                for s in range(RING):
                    sp.wait_ge(slab_used, i * RING + (s - RING + 1))
                    sp.dma_start(flat(ring[s]), slabs_d[i * RING + s]).then_inc(slab_loaded[s], 16)
            for n in range(rounds * RING, SLABS):
                sp.wait_ge(slab_used, n - RING + 1)
                sp.dma_start(flat(ring[n % RING]), slabs_d[n]).then_inc(slab_loaded[n % RING], 16)

        @block.tensor
        def _(pe):
            me = Side(pe, K)
            t = me.t

            def mm(out, lhsT, rhs, k, n):
                return pe.matmul(out, lhsT, rhs, start=(k == 0), stop=(k == n - 1))

            def square_sums(parts):
                pe.wait_ge(fed, me.next("fed"))
                pe.wait_ge(drained, me.first_bank())
                for sq, n, w in parts:
                    if me.reuses():
                        pe.wait_ge(drained, me.reused())
                    b = me.next_bank()
                    for k in range(n):
                        m = mm(b[:, 0:w], ones, sq[:, k, 0:w], k, n)
                    m.then_inc(filled, me.add("filled"))

            def transposed(parts):
                if me.reuses():
                    pe.wait_ge(drained, me.reused())
                b = me.next_bank()
                for in_, rows, at in parts:
                    m = pe.transpose(b[0:in_.shape[1], at:at + rows], in_, ident[0:rows, 0:rows])
                m.then_inc(filled, me.add("filled"))

            def dense(src, segs, then=None):
                pe.wait_ge(slab_loaded[me.slot()], me.landed())
                w = me.next_slab()
                for j in range(4):
                    for h, n in segs:
                        if me.reuses():
                            pe.wait_ge(drained, me.reused())
                        b = me.next_bank()
                        for k in range(KT):
                            m = mm(b[:, 0:n], w[:, k, j * 128:(j + 1) * 128], h[:, k, :], k, KT)
                        m.then_inc(filled, me.add("filled"))
                pe.drain().then_inc(slab_used, 1)

            pe.wait_ge(tables_loaded, 64)
            pe.wait_ge(answered, 1)

            def ada_slab(n):
                pe.wait_ge(slab_loaded[me.slot()], me.landed())
                w = me.next_slab()
                for k in range(KT):
                    m = mm(P[n][0:2, :], cs[:, k, :], w[:, k, :], k, KT)
                m.then_inc(filled, me.add("filled"))
                pe.drain().then_inc(slab_used, 1)

            for n in range(RING):
                ada_slab(n)
            with me.loop("ada", ADA_SLABS // RING - 1):
                for n in range(RING):
                    pe.wait_ge(drained, me.t["filled"].at(1 - RING))
                    ada_slab(n)
            pe.wait_ge(fed, me.next("fed"))
            pe.wait_ge(drained, me.first_bank())
            b = me.next_bank()
            for q in range(ADA_SLABS * HALF // 128):
                m = pe.transpose(b[:, 2 * q:2 * q + 2], adarow[0:2, q * 128:(q + 1) * 128], ident[0:2, 0:2])
            m.then_inc(filled, me.add("filled"))

            square_sums([(sqx, KT, NX), (sqc, KT, NC)])
            pe.wait_ge(fed, me.next("fed"))
            pe.wait_ge(drained, me.first_bank())
            pe.wait_ge(slab_loaded[me.slot()], me.landed())
            w = me.next_slab()
            wf = w[:, :, :].rearrange("p a b -> p (a b)")
            for tt in range(6):
                for g in range(4):
                    if me.reuses():
                        pe.wait_ge(drained, me.reused())
                    b = me.next_bank()
                    for k in range(2):
                        src = hx[:, 2 * g + k, tt * 128:(tt + 1) * 128] if tt < 4 else hc[:, 2 * g + k, (tt - 4) * 128:(tt - 3) * 128]
                        m = mm(b[:, :], src, wf[:, 512 * k:512 * k + 512], k, 2)
                    m.then_inc(filled, me.add("filled"))
            pe.wait_ge(fed, me.next("fed"))
            pe.wait_ge(drained, me.first_bank())
            pe.wait_ge(slab_loaded[me.slot()], me.landed())
            wx = me.next_slab()
            for f in range(KT):
                g, half = f // 2, f % 2
                for seg, tiles in ((0, range(0, 4)), (1, range(4, 6))):
                    if me.reuses():
                        pe.wait_ge(drained, me.reused())
                    b = me.next_bank()
                    n = 0
                    for part in range(2):
                        for j, tt in enumerate(tiles):
                            at = g * 512 + part * 256 + half * 128
                            if seg == 0:
                                rhs, wdt = wx[:, part * 4 + j, :], NX
                            else:
                                rhs, wdt = wf[:, 1024 + (part * 2 + j) * 256:1024 + (part * 2 + j + 1) * 256], NC
                            m = mm(b[:, 0:wdt], AB[:, tt, at:at + 128], rhs, n, 2 * len(tiles))
                            n += 1
                    m.then_inc(filled, me.add("filled"))
            pe.drain().then_inc(slab_used, 2)
            pe.wait_ge(fed, me.next("fed"))
            pe.wait_ge(drained, me.first_bank())
            for _ in range(2):
                dense(None, [(hx, NX), (hc, NC)])

            def moe(l, ctx):
                tiles = 6 if ctx else 4
                S_ = CAPX + CAPC if ctx else CAPX
                W = NX + NC * ctx
                square_sums([(sqx, KT, NX)] + [(sqc, KT, NC)] * ctx)
                pe.wait_ge(fed, me.next("fed"))
                pe.wait_ge(drained, me.first_bank())

                def htile(k, tt):
                    return hx[:, k, tt * 128:(tt + 1) * 128] if tt < 4 else hc[:, k, (tt - 4) * 128:(tt - 3) * 128]

                if me.reuses():
                    pe.wait_ge(drained, me.reused())
                b = me.next_bank()
                for tt in range(tiles):
                    for k in range(KT):
                        m = mm(b[:, tt * NE:(tt + 1) * NE], htile(k, tt), router[:, l, k, :], k, KT)
                m.then_inc(filled, me.add("filled"))
                for tt in range(tiles):
                    for half in range(2):
                        transposed([(htile(4 * half + j, tt), 128, 128 * j) for j in range(4)])
                pe.wait_ge(fed, me.next("fed"))
                transposed([(aff[:, tt, :], 128, 128 * tt) for tt in range(4)])
                if ctx:
                    transposed([(aff[:, tt, :], 128, 128 * (tt - 4)) for tt in range(4, 6)])
                pe.wait_ge(fed, me.next("fed"))
                if me.reuses():
                    pe.wait_ge(drained, me.reused())
                b = me.next_bank()
                for tt in range(tiles):
                    m = pe.transpose(b[:, tt * NE:(tt + 1) * NE], slot[0:NE, tt * 128:(tt + 1) * 128], ident[0:NE, 0:NE])
                m.then_inc(filled, me.add("filled"))
                pe.wait_ge(fed, me.next("fed"))
                pe.wait_ge(drained, me.first_bank())

                def bank():
                    pe.wait_ge(drained, me.reused())
                    return me.next_bank()

                def slab():
                    pe.wait_ge(slab_loaded[me.slot()], me.landed())
                    return me.next_slab()

                with me.loop("expert_ctx" if ctx else "expert", NE // 2):
                    for half in range(2):
                        b = bank()
                        for tt in range(4):
                            m = mm(b[:, :], pickx[:, tt, :], htok[:, tt, half * 512:(half + 1) * 512], tt, 4)
                        m.then_inc(filled, me.add("filled"))
                    if ctx:
                        b = bank()
                        for half in range(2):
                            for tt in range(2):
                                m = mm(b[half * 64:half * 64 + 64, :], pickc[:, tt, :], htok[:, 4 + tt, half * 512:(half + 1) * 512], tt, 2)
                        m.then_inc(filled, me.add("filled"))
                    b = bank()
                    for j in range(2):
                        for tt in range(4):
                            out = b[0:CAPX, j:j + 1] if ctx else b[j * CAPX:(j + 1) * CAPX, 0:1]
                            m = mm(out, pickx[:, tt, j * CAPX:(j + 1) * CAPX], affe[:, j, tt:tt + 1], tt, 4)
                        if ctx:
                            for tt in range(2):
                                m = mm(b[CAPX:S_, j:j + 1], pickc[:, tt, j * CAPC:(j + 1) * CAPC], affe[:, j, 4 + tt:5 + tt], tt, 2)
                    if ctx:
                        m = mm(b[0:2 * CAPC, NC:2 * NC], eselc[0:NE, :], slot[0:NE, NX:W], 0, 1)
                    m.then_inc(filled, me.add("filled"))
                    mm(bank()[:, 0:NX], eselx[0:NE, :], slot[0:NE, 0:NX], 0, 1).then_inc(filled, me.add("filled"))
                    pe.wait_ge(fed, me.next("fed"))
                    for half in range(2):
                        b = bank()
                        for q in range(4):
                            m = pe.transpose(b[:, q * 128:(q + 1) * 128], xtok[:, half * 512 + q * 128:half * 512 + (q + 1) * 128], ident)
                        m.then_inc(filled, me.add("filled"))
                    if ctx:
                        b = bank()
                        pe.sem_inc(pe_steps)
                        for f in range(KT):
                            if f == 4:
                                pe.drain()
                            rows = slice(f // 4 * 64, f // 4 * 64 + 64)
                            m = pe.transpose(b[:, f * 64:(f + 1) * 64], ctok[rows, f % 4 * 128:(f % 4 + 1) * 128], ident[rows, rows])
                        m.then_inc(filled, me.add("filled"))
                    pe.wait_ge(fed, me.next("fed"))
                    for j in range(2):
                        for _ in range(4):
                            w = slab()
                            b = bank()
                            for m4 in range(4):
                                for k in range(KT):
                                    m = mm(b[:, m4 * FILL:(m4 + 1) * FILL], w[:, k, m4 * 128:(m4 + 1) * 128], xsT[j][:, k, :], k, KT)
                            m.then_inc(filled, me.add("filled"))
                            pe.drain().then_inc(slab_used, 1)
                    me.add("fed")
                    for half in range(2):
                        for j in range(2):
                            if half == 0:
                                pe.wait_ge(fed, me.next("fed"))
                            w = slab()
                            if ctx or j == 0:
                                b = bank()
                            rows = slice(0, S_) if ctx else slice(j * CAPX, (j + 1) * CAPX)
                            for k in range(KT):
                                m = mm(b[rows, :], hid[j][:, k, 0:S_], w[:, k, :], k, KT)
                            if ctx or j:
                                m.then_inc(filled, me.add("filled"))
                            pe.drain().then_inc(slab_used, 1)
                    for half in range(2):
                        pe.wait_ge(fed, me.next("fed"))
                        for f in range(4 * half, 4 * half + 4):
                            mm(bank()[:, :], ysx[:, f * 128:(f + 1) * 128], putx, 0, 1).then_inc(filled, me.add("filled"))
                            if ctx and f % 2:
                                b = bank()
                                for q in range(2):
                                    m = mm(b[:, q * NC:(q + 1) * NC], ysc[0:2 * CAPC, (f - 1 + q) * 128:(f + q) * 128], putc[0:2 * CAPC, :], 0, 1)
                                m.then_inc(filled, me.add("filled"))
                pe.wait_ge(drained, me.first_bank())

            moe(0, True)

            square_sums([(sqx, KT, NX), (sqc, KT, NC)])
            pe.wait_ge(slab_loaded[me.slot()], me.landed())
            lora = me.next_slab()
            for j, what, mt, ns in W_MIX:
                segs = [(256, NX)] if what in "rg" else [(256, NX), (0, NC)]
                for half in range(ns):
                    if what in "wag":
                        w, first = lora, 128 * "wag".index(what)
                    else:
                        pe.wait_ge(slab_loaded[me.slot()], me.landed())
                        w, first = me.next_slab(), 0
                    pe.wait_ge(drained, me.first_bank())
                    banks = {(m4, at): me.next_bank() for m4 in range(mt) for at, _ in segs}
                    for k in range(KT):
                        pe.wait_ge(fed, me.next("fed"))
                        for m4 in range(mt):
                            for at, n in segs:
                                m = mm(banks[m4, at][:, 0:n], w[:, k, first + m4 * 128:first + (m4 + 1) * 128],
                                       mixed[k % 2][:, at:at + n], k, KT)
                                if k == KT - 1:
                                    m.then_inc(filled, me.add("filled"))
                        if k < KT - 1:
                            m.then_inc(mix_used, 1)
                    if what not in "wav":
                        pe.drain().then_inc(slab_used, 1)
            pe.wait_ge(slab_loaded[me.slot()], me.landed())
            me.next_slab()
            K.first = {"dve": t["filled"].n, "act": t["afilled"].n}
            K.orders = {"dve": PAIR_DVE, "act": PAIR_ACT}
            two = (slice(0, 64), slice(64, 128))

            def heads2(out, lhsT, rhs, k=0, n=1):
                for r in two:
                    m = pe.matmul(out[r], lhsT[r], rhs[r], start=(k == 0), stop=(k == n - 1))
                return m

            def turn2(out, in_):
                lower, upper = two
                pe.transpose(out[lower], in_[lower], eye2[lower])
                return pe.matmul(out[upper], in_[upper], eye2[upper], start=True, stop=True)

            def keep_warm(n):
                if me.reuses():
                    pe.wait_ge(drained, me.reused())
                for _ in range(n):
                    mm(K.banks[me.bank % me.width][:, :], headones, HG, 0, 1)

            def head_sums(x):
                pe.wait_ge(drained, me.reused())
                mm(me.next_bank()[:, :], headones, x, 0, 1).then_inc(filled, me.add("filled"))

            with me.loop("pair", KT) as i:
                me.pair = (i, {"dve": PER["pair"]["filled"], "act": PER["pair"]["afilled"]})
                pe.wait_ge(fed, me.next("fed"))
                pe.wait_ge(drained, me.first_bank())
                me.split_banks()
                for a, n in ((0, NC), (NC, NX)):
                    mm(me.next_bank()[:, 0:n], headones, ksq[:, a:a + n], 0, 1).then_inc(filled, me.add("filled"))
                for d in range(2):
                    rows = two[d]
                    for lhsT, rhs in ((w2p, HW), (a2p, HA)):
                        for a, n in ((0, NC), (NC, NX)):
                            if me.act_reuses():
                                pe.wait_ge(drained_act, me.act_reused())
                            mm(me.next_act_bank()[:, 0:n], lhsT[rows, :], rhs[rows, a:a + n], 0, 1).then_inc(filled_act, me.add("afilled"))
                for d in range(2):
                    keep_warm((8, 4)[d])
                    pe.wait_ge(fed, me.next("fed"))
                    for bi, b in enumerate(BATCHES):
                        n = 2 * CH if bi else CH
                        for src in (bd[d], kd[d]):
                            if me.reuses():
                                pe.wait_ge(drained, me.reused())
                            p = me.next_bank()
                            pe.sem_inc(pe_steps)
                            for c in range(GC):
                                at = CH * (b.start + c)
                                m = heads2(p[:, c * 128:c * 128 + n], src[:, at:at + CH], ar[d][:, b.start + c, 0:n])
                            m.then_inc(filled, me.add("filled"))
                        pe.wait_ge(drained_act, me.act_reused())
                        p = me.next_act_bank()
                        pe.sem_inc(pe_steps)
                        for c in range(GC):
                            at = CH * (b.start + c)
                            for q, src in enumerate((bd[d], kd[d])):
                                m = turn2(p[:, c * 128 + q * CH:c * 128 + (q + 1) * CH], src[:, at:at + CH])
                        m.then_inc(filled_act, me.add("afilled"))
                        pe.wait_ge(drained_act, me.act_reused())
                        p = me.next_act_bank()
                        pe.sem_inc(pe_steps)
                        for c in range(GC):
                            m = turn2(p[:, c * CH:(c + 1) * CH], ar[d][:, b.start + c, 0:CH])
                        m.then_inc(filled_act, me.add("afilled"))
                for b in BATCHES:
                    pe.wait_ge(drained, me.reused())
                    p = me.next_bank()
                    pe.sem_inc(pe_steps)
                    for c in range(GC):
                        at = CH * (b.start + c)
                        m = turn2(p[:, c * CH:(c + 1) * CH], vp[:, at:at + CH])
                    m.then_inc(filled, me.add("filled"))
                pe.wait_ge(fed, me.next("fed"))
                head_sums(ksum)
                for u, (d, bi, b) in enumerate(UNITS):
                    if u in (0,3,):
                        keep_warm(1)
                    pe.wait_ge(drained, me.group("dve", ("vt", 2)))
                    pe.wait_ge(drained_act, me.act_reused())
                    p = me.next_act_bank()
                    pe.sem_inc(pe_steps)
                    for c in range(GC):
                        m = heads2(p[:, c * CH:(c + 1) * CH], MT[d][:, b.start + c, :], Vt[:, b.start + c, :])
                    m.then_inc(filled_act, me.add("afilled"))
                for d, bi, b in UNITS:
                    pe.wait_ge(masked, me.mask_value(i, mask_no(d, 0, bi)))
                    pe.wait_ge(drained, me.reused())
                    p = me.next_bank()
                    pe.sem_inc(pe_steps)
                    for c in range(GC):
                        m = turn2(p[:, c * CH:(c + 1) * CH], NL[d][:, b.start + c, :])
                    m.then_inc(filled, me.add("filled"))
                keep_warm(3)
                head_sums(Y)
                for l in range(1, 6):
                    if l == 2:
                        pe.wait_ge(fed, me.next("fed"))
                        head_sums(squares)
                    if l == 3:
                        pe.wait_ge(drained, me.reused())
                        mm(me.next_bank()[:, :], g2p, HG, 0, 1).then_inc(filled, me.add("filled"))
                    for u, (d, bi, b) in enumerate(UNITS):
                        if u in (0,3,):
                            keep_warm(1)
                        pe.wait_ge(masked, me.mask_value(i, mask_no(d, l, bi)))
                        pe.wait_ge(drained, me.group("dve", ("XX", d, l - 1, bi) if l > 1 else ("X0", d, bi)))
                        pe.wait_ge(drained_act, me.act_reused())
                        p = me.next_act_bank()
                        pe.sem_inc(pe_steps)
                        for c in range(GC):
                            m = heads2(p[:, c * CH:(c + 1) * CH], NL[d][:, b.start + c, :], X[d][:, b.start + c, :])
                        m.then_inc(filled_act, me.add("afilled"))
                    for u, (d, bi, b) in enumerate(UNITS):
                        if u in (0,2,4,):
                            keep_warm(1)
                        pe.wait_ge(drained_act, me.group("act", ("T", d, l, bi)))
                        pe.wait_ge(drained, me.reused())
                        p = me.next_bank()
                        pe.sem_inc(pe_steps)
                        for c in range(GC):
                            if l < 5:
                                heads2(p[:, c * CH:(c + 1) * CH], XT[d][:, b.start + c, :], T[d][:, b.start + c, :])
                            m = heads2(p[:, 256 + c * CH:256 + (c + 1) * CH], T[d][:, b.start + c, :], XT[d][:, b.start + c, :])
                        m.then_inc(filled, me.add("filled"))
                for u, (d, bi, b) in enumerate(UNITS):
                    if u in (0,2,4,):
                        keep_warm(1 if u else 2)
                    pe.wait_ge(drained, me.group("dve", ("XX", d, 5, bi)))
                    pe.wait_ge(drained_act, me.group("act", ("MV", d, bi)))
                    pe.wait_ge(drained_act, me.act_reused())
                    p = me.next_act_bank()
                    pe.sem_inc(pe_steps)
                    for c in range(GC):
                        m = heads2(p[:, c * 128:(c + 1) * 128], XT[d][:, b.start + c, :], AM[d][:, b.start + c, :])
                    m.then_inc(filled_act, me.add("afilled"))
                for d, bi, b in UNITS:
                    keep_warm(1)
                    pe.wait_ge(drained_act, me.group("act", ("WU", d, bi)))
                    pe.wait_ge(drained, me.reused())
                    p = me.next_bank()
                    pe.sem_inc(pe_steps)
                    for c in range(GC):
                        cc = b.start + c
                        m = heads2(p[:, c * 128:c * 128 + CH], WU[d][:, cc, 0:CH], BK[d][:, cc, 0:CH])
                        if bi:
                            m = heads2(p[:, c * 128 + CH:(c + 1) * 128], WU[d][:, cc, 0:CH], QB[d][:, cc - GC, :])
                    m.then_inc(filled, me.add("filled"))
                    pe.wait_ge(drained, me.reused())
                    p = me.next_bank()
                    pe.sem_inc(pe_steps)
                    for c in range(GC):
                        cc = b.start + c
                        for r in two:
                            pe.matmul(p[r, c * CH:(c + 1) * CH], BK[d][r, cc, 0:CH], WU[d][r, cc, CH:128], start=True, stop=False)
                            m = pe.matmul(p[r, c * CH:(c + 1) * CH], BK[d][r, cc, CH:128], Vt[r, cc, :], start=False, stop=True)
                    m.then_inc(filled, me.add("filled"))
                    if bi:
                        keep_warm(1)
                        pe.wait_ge(drained, me.reused())
                        p = me.next_bank()
                        pe.sem_inc(pe_steps)
                        for c in range(GC):
                            cc = b.start + c
                            for r in two:
                                pe.matmul(p[r, c * CH:(c + 1) * CH], WU[d][r, cc, CH:128], QB[d][r, cc - GC, :], start=True, stop=False)
                                m = pe.matmul(p[r, c * CH:(c + 1) * CH], Vt[r, cc, :], QK[d][r, cc - GC, :], start=False, stop=True)
                        m.then_inc(filled, me.add("filled"))
                for j in range(1, NCH):
                    for d in range(2):
                        c = CHAIN[d][j]
                        pe.wait_ge(fed, me.next("fed"))
                        pe.sem_inc(pe_steps)
                        if c >= GC:
                            m = heads2(P[4 + d][:, CH * (c - GC):CH * (c - GC + 1)], Z[d], Rt[d][:, c - GC, :])
                        if j < NCH - 1:
                            pe.wait_ge(drained, me.reused())
                            pe.sem_inc(pe_steps)
                            m = heads2(me.next_bank()[:, 0:CH], At[d][:, c, :], Z[d])
                        m.then_inc(filled, me.add("filled"))
                        if j == NCH - 1:
                            me.next_bank()
            pe.wait_ge(fed, me.next("fed"))
            pe.wait_ge(drained, me.first_bank())
            mm(me.next_bank()[:, :], headones, Y, 0, 1).then_inc(filled, me.add("filled"))
            pe.wait_ge(fed, me.next("fed"))
            mm(me.next_bank()[:, :], headones, squares, 0, 1).then_inc(filled, me.add("filled"))
            mm(me.next_bank()[:, :], g2p, HG, 0, 1).then_inc(filled, me.add("filled"))
            me.width = 8
            pe.wait_ge(fed, me.next("fed"))
            pe.wait_ge(drained, me.first_bank())
            for _ in range(2):
                dense(None, [(Rx[:, 1:KT + 1, :], NX)])
            moe(1, False)
            square_sums([(sqx, KT, NX)])

            with me.loop("layer", 2):
                square_sums([(sq2, KT, NX)])
                pe.wait_ge(fed, me.next("fed"))
                pe.wait_ge(drained, me.first_bank())
                for sl in range(5):
                    pe.wait_ge(slab_loaded[me.slot()], me.landed())
                    w = me.next_slab()
                    for j in range(4 if sl < 4 else 2):
                        if me.reuses():
                            pe.wait_ge(drained, me.reused())
                        b = me.next_bank()
                        for k in range(KT):
                            m = mm(b[:, :], w[:, k, j * 128:(j + 1) * 128], hx[:, k, :], k, KT)
                        m.then_inc(filled, me.add("filled"))
                    if sl < 4:
                        pe.drain().then_inc(slab_used, 1)
                pe.wait_ge(slab_loaded[me.slot()], me.landed())
                w5 = me.next_slab()
                for ww, c0, n in ((w, 256, 256), (w5, 0, TM_W - 256)):
                    for tt in range(4):
                        if me.reuses():
                            pe.wait_ge(drained, me.reused())
                        b = me.next_bank()
                        for k in range(KT):
                            m = mm(b[:, 0:n], hx[:, k, tt * 128:(tt + 1) * 128], ww[:, k, c0:c0 + n], k, KT)
                        m.then_inc(filled, me.add("filled"))
                pe.drain().then_inc(slab_used, 1)
                pe.wait_ge(fed, me.next("fed"))
                pe.wait_ge(drained, me.first_bank())
                for tiles in ((0, 1), (2,)):
                    if me.reuses():
                        pe.wait_ge(drained, me.reused())
                    b = me.next_bank()
                    for k, j in enumerate(tiles):
                        m = mm(b[:, :], ones, S[:, j, :], k, len(tiles))
                    m.then_inc(filled, me.add("filled"))
                pe.wait_ge(fed, me.next("fed"))
                uq = aux[:, 0:768].rearrange("p (k n) -> p k n", k=2)
                ukv = aux[:, 768:1280]
                for j in range(3):
                    if me.reuses():
                        pe.wait_ge(drained, me.reused())
                    b = me.next_bank()
                    for k in range(2):
                        m = mm(b[:, :], uq[:, k, j * 128:(j + 1) * 128], Fm[:, k, :], k, 2)
                    m.then_inc(filled, me.add("filled"))
                for j in range(2):
                    if me.reuses():
                        pe.wait_ge(drained, me.reused())
                    b = me.next_bank()
                    mm(b[:, :], ukv[:, j * 128:(j + 1) * 128], Fm[:, 2, :], 0, 1).then_inc(filled, me.add("filled"))
                for tt in range(4):
                    if me.reuses():
                        pe.wait_ge(drained, me.reused())
                    b = me.next_bank()
                    mm(b[:, 0:256], Fm[:, 2, tt * 128:(tt + 1) * 128], ukv[:, 256:512], 0, 1).then_inc(filled, me.add("filled"))
                pe.wait_ge(fed, me.next("fed"))
                pe.wait_ge(drained, me.first_bank())
                for r, (tl, j, d) in enumerate(ROPED):
                    if me.reuses():
                        pe.wait_ge(drained, me.reused())
                    b = me.next_bank()
                    mm(b[:, :], tab2(f"rot{d}"), tile(tl, j), 0, 1).then_inc(filled, me.add("filled"))
                    if r in FORGETS:
                        if me.reuses():
                            pe.wait_ge(drained, me.reused())
                        b = me.next_bank()
                        for j in range(4):
                            m = mm(b[:, 128 * j:NX], lfb[:, FORGETS[r], j, :], tab2("upto")[:, 384:896 - 128 * j], j, 4)
                        m.then_inc(filled, me.add("filled"))
                pe.wait_ge(fed, me.next("fed"))
                pe.wait_ge(drained, me.first_bank())
                me.split_banks()

                def scores(v, i):
                    k0, k1 = span(v, i)
                    q = slice(128 * i, 128 * i + 128)
                    if v == "dsa" and i > 0:
                        for h in range(8):
                            rows = slice(32 * (h % 4), 32 * (h % 4) + 32)
                            pe.wait_ge(drained, me.reused())
                            mm(me.next_bank()[:, 0:k1], Fm[rows, 10 + h // 4, q], Fm[rows, 17, 0:k1], 0, 1).then_inc(filled, me.add("filled"))
                    for parts, _, _, _ in heads(v):
                        for qt, qj, kt_, kj, rows in parts:
                            if me.reuses():
                                pe.wait_ge(drained, me.reused())
                            b = me.next_bank()
                            mm(b[:, 0:k1 - k0], tile(qt, qj)[rows, q], tile(kt_, kj)[rows, k0:k1], 0, 1).then_inc(filled, me.add("filled"))

                scores(*ATTENTION[0])
                scores(*ATTENTION[1])
                for u, (v, i) in enumerate(ATTENTION):
                    k0, k1 = span(v, i)
                    pe.wait_ge(normalised, me.next("normalised"))
                    for h in range(HEADS):
                        if me.act_reuses():
                            pe.wait_ge(drained_act, me.act_reused())
                        b = me.next_act_bank()
                        for a in range(0, k1 - k0, 128):
                            m = pe.transpose(b[:, a:a + 128], SS[u % 2][:, h, a:a + 128], ident)
                        m.then_inc(filled_act, me.add("afilled"))
                    if u + 2 < len(ATTENTION):
                        scores(*ATTENTION[u + 2])
                    for h, (_, (vt, vc), _, _) in enumerate(heads(v)):
                        pe.wait_ge(drained_act, me.t["afilled"].at(h + 1 - HEADS))
                        pe.wait_ge(drained, me.reused())
                        b = me.next_bank()
                        nk = (k1 - k0) // 128
                        for kk in range(nk):
                            m = mm(b[:, 0:128], vt[:, k0 // 128 + kk, vc:vc + 128], PTs[u % 2][:, h, kk * 128:(kk + 1) * 128], kk, nk)
                        m.then_inc(filled, me.add("filled"))
                me.width = 8
                pe.wait_ge(fed, me.next("fed"))
                pe.wait_ge(drained, me.first_bank())
                for _ in range(2):
                    dense(None, [(OT, NX)])
                square_sums([(sq2, KT, NX)])
                pe.wait_ge(fed, me.next("fed"))
                pe.wait_ge(drained, me.first_bank())
                for _ in range(8):
                    dense(None, [(hx, NX)])
                pe.wait_ge(fed, me.next("fed"))
                pe.wait_ge(drained, me.first_bank())
                for half in range(2):
                    banks = [me.next_bank() for _ in range(4)]
                    for kg in range(4):
                        pe.wait_ge(slab_loaded[me.slot()], me.landed())
                        w = me.next_slab()
                        for j in range(4):
                            for k in range(KT):
                                m = mm(banks[j][:, :], w[:, k, j * 128:(j + 1) * 128], up[:, kg * KT + k, :], kg * KT + k, 32)
                            if kg == 3:
                                m.then_inc(filled, me.add("filled"))
                        pe.drain().then_inc(slab_used, 1)
            square_sums([(sq2, KT, NX)])

        @block.scalar
        def _(act):
            me = Side(act, K)
            t = me.t

            def root(x):
                act.wait_ge(asked, me.next("asked"))
                act.activation(x, x, ACT.Sqrt)
                act.drain().then_inc(answered, me.add("answered"))

            act.wait_ge(tables_loaded, 64)
            act.activation(cs[:, :, :], vec("c").rearrange("p (k j) -> p k j", j=2), ACT.Silu)
            act.drain().then_inc(answered, me.add("answered"))
            root(rstd)

            def moe(l, ctx):
                tiles = 6 if ctx else 4
                S_ = CAPX + CAPC if ctx else CAPX
                root(rstd[:, 0:NX + NC * ctx])
                act.wait_ge(asked, me.next("asked"))
                act.activation(aff[:, 0:tiles, :], aff[:, 0:tiles, :], ACT.Exp)
                act.drain().then_inc(answered, me.add("answered"))
                me.first_bank()
                with me.loop("expert_ctx" if ctx else "expert", NE // 2):
                    me.bank += 8 if ctx else 6
                    for _ in range(4):
                        b, _ = me.next_bank(), me.next_bank()
                        act.wait_ge(asked, me.next("asked"))
                        act.activation(gact[:, :, 0:S_], b[:, 0:4 * FILL].rearrange("p (a b) -> p a b", a=4)[:, :, 0:S_], ACT.Silu)
                        act.drain().then_inc(answered, me.add("answered"))

            moe(0, True)
            root(rstd)
            act.wait_ge(asked, me.next("asked"))
            act.dma_start(spill_d, rxf).then_inc(spilled, 16)
            for what, dst in (("w", HW), ("g", HG)):
                act.wait_ge(asked, me.next("asked"))
                if what == "w":
                    act.activation(HW[:, NC:NC + NX], P[0][:, :], ACT.Tanh)
                    act.activation(HW[:, 0:NC], P[1][:, 0:NC], ACT.Tanh)
                else:
                    act.activation(HG, P[0][:, :], ACT.Sigmoid)
                act.drain().then_inc(answered, me.add("answered"))
            with me.loop("pair", KT):
                me.split_banks()
                root(ksq)
                for d in range(2):
                    for q, dst in ((0, lw[d]), (1, bd[d])):
                        for a, n in ((0, NC), (NC, NX)):
                            act.wait_ge(filled_act, me.next("afilled"))
                            act.activation(dst[:, a:a + n], me.next_act_bank()[:, 0:n], ACT.Sigmoid, bias=pp[:, 2 * q + d:2 * q + d + 1])
                            act.drain().then_inc(drained_act, 1)
                for d in range(2):
                    act.wait_ge(asked, me.next("asked"))
                    act.activation(E1[d], E1[d], ACT.Exp)
                    act.activation(E3[d], Lc[d], ACT.Exp, scale=-1.0)
                    act.activation(ETd[d], ETd[d], ACT.Exp)
                    act.drain()
                    act.activation(Lc[d][:, NC:NC + NX], Lc[d][:, NC:NC + NX], ACT.Exp)
                    act.drain().then_inc(answered, me.add("answered"))
                for d, bi, b in UNITS:
                    act.wait_ge(filled_act, me.next("afilled"))
                    act.activation(BK[d][:, b, :], me.next_act_bank()[:, :].rearrange("p (c n) -> p c n", c=GC), ACT.Copy)
                    act.drain().then_inc(drained_act, 1)
                    act.wait_ge(filled_act, me.next("afilled"))
                    act.activation(AM[d][:, b, 0:CH], me.next_act_bank()[:, 0:256].rearrange("p (c n) -> p c n", c=GC), ACT.Copy)
                    act.drain().then_inc(drained_act, 1)
                for d, bi, b in UNITS:
                    act.wait_ge(filled_act, me.next("afilled"))
                    act.activation(AM[d][:, b, CH:128], me.next_act_bank()[:, 0:256].rearrange("p (c n) -> p c n", c=GC), ACT.Copy)
                    act.drain().then_inc(drained_act, 1)
                for l in range(1, 6):
                    for d, bi, b in UNITS:
                        act.wait_ge(filled_act, me.next("afilled"))
                        act.activation(T[d][:, b, :], me.next_act_bank()[:, 0:256].rearrange("p (c n) -> p c n", c=GC), ACT.Copy)
                        act.drain().then_inc(drained_act, 1)
                    if l == 2:
                        root(squares)
                for d, bi, b in UNITS:
                    act.wait_ge(filled_act, me.next("afilled"))
                    act.activation(WU[d][:, b, :], me.next_act_bank()[:, :].rearrange("p (c n) -> p c n", c=GC), ACT.Copy)
                    act.drain().then_inc(drained_act, 1)
            me.width = 8
            root(squares)
            act.wait_ge(asked, me.next("asked"))
            act.dma_start(rxf, spill_d).then_inc(spilled, 16)
            moe(1, False)
            root(rstd[:, 0:NX])

            act.wait_ge(asked, me.next("asked"))
            act.dma_start(tabs2, tabs2_d).then_inc(tables_loaded, 16)
            with me.loop("layer", 2) as l:
                act.wait_ge(asked, me.next("asked"))
                act.dma_start(aux, aux_d[l]).then_inc(aux_loaded, 16)
                root(rstd2)
                root(S[:, 0:2, :])
                act.wait_ge(asked, me.next("asked"))
                act.activation(le, le, ACT.Exp)
                act.drain().then_inc(answered, me.add("answered"))
                act.wait_ge(asked, me.next("asked"))
                act.activation(le, le, ACT.Ln)
                act.drain().then_inc(answered, me.add("answered"))
                me.split_banks()

                def exponentials(u):
                    v, i = ATTENTION[u]
                    n = span(v, i)[1] - span(v, i)[0]
                    act.wait_ge(asked, me.next("asked"))
                    for h in range(HEADS):
                        act.activation(SS[u % 2][:, h, 0:n], SS[u % 2][:, h, 0:n], ACT.Exp, bias=mxn[u % 2][:, h:h + 1], accum_out=sums[u % 2][:, h:h + 1])
                    if v == "swa":
                        act.activation(esink[u % 2], esink[u % 2], ACT.Exp)
                    act.drain().then_inc(answered, me.add("answered"))

                exponentials(0)
                exponentials(1)
                for u, (v, i) in enumerate(ATTENTION):
                    n = span(v, i)[1] - span(v, i)[0]
                    for h in range(HEADS):
                        act.wait_ge(filled_act, me.next("afilled"))
                        act.activation(PTs[u % 2][:, h, 0:n], me.next_act_bank()[:, 0:n], ACT.Copy)
                        act.drain().then_inc(drained_act, 1)
                    if u + 2 < len(ATTENTION):
                        exponentials(u + 2)
                me.width = 8
                root(rstd2)
            root(rstd2)
            act.wait_ge(asked, me.next("asked"))
            act.dma_start(out_d.rearrange("(k p) t -> p k t", p=128), hx[:, :, :]).then_inc(stored, 16)
            act.wait_ge(stored, 16)

        @block.vector
        def _(v):
            me = Side(v, K)
            t = me.t

            def pass_on():
                v.memset(cell, 0.0)

            def tt(out, a, b, op):
                v.tensor_tensor(out, a, b, op)

            def ts(out, a, s1, op0, s2=None, op1=None):
                if op1 is None:
                    v.tensor_scalar(out, a, s1, None, op0)
                else:
                    v.tensor_scalar(out, a, s1, s2, op0, op1)

            def stt(out, a, s, b, op0, op1):
                v.scalar_tensor_tensor(out, a, s, b, op0, op1)

            def bc(x, *shape):
                return x.to_broadcast(list(shape))

            def inverse_roots(parts, root, eps):
                at = 0
                for w, n in parts:
                    v.wait_ge(filled, me.next("filled"))
                    b = me.next_bank()
                    ts(root[:, at:at + w], b[:, 0:w], 1.0 / n, ALU.mult, eps, ALU.add)
                    v.drain().then_inc(drained, 1)
                    at += w
                v.drain().then_inc(asked, me.add("asked"))
                v.wait_ge(answered, me.next("answered"))
                v.reciprocal(root[:, 0:at], root[:, 0:at])
                v.drain()

            def norm(segs, sqs, root, gains):
                for (res, h, n, j), sq in zip(segs, sqs):
                    tt(sq, res[:, :, :], res[:, :, :], ALU.mult)
                v.drain().then_inc(fed, me.add("fed"))
                me.first_bank()
                inverse_roots([(s[2], D) for s in segs], root, 1e-6)
                at = 0
                for res, h, n, j in segs:
                    if gains(0, j)[1] is None:
                        for k in range(KT):
                            stt(h[:, k, :], res[:, k, :], gains(k, j)[0], root[:, at:at + n], ALU.mult, ALU.mult)
                    else:
                        tt(h[:, :, :], res[:, :, :], bc(root[:, at:at + n].unsqueeze(1), 128, KT, n), ALU.mult)
                        v.drain()
                        for k in range(KT):
                            gain, shift = gains(k, j)
                            ts(h[:, k, :], h[:, k, :], gain, ALU.mult, shift, ALU.add)
                    at += n

            def modulated(l, which):
                return lambda k, j: (mod[:, l, 3 * which + 1, k, j:j + 1], mod[:, l, 3 * which, k, j:j + 1])

            v.wait_ge(tables_loaded, 64)
            t["answered"].n += 1
            for n in range(RING):
                v.wait_ge(filled, me.next("filled"))
                v.tensor_copy(adarow[0:2, n * HALF:(n + 1) * HALF], P[n][0:2, :])
                v.drain().then_inc(drained, 1)
            with me.loop("ada", ADA_SLABS // RING - 1) as i:
                for n in range(RING):
                    v.wait_ge(filled, me.next("filled"))
                    pass_on()
                    v.tensor_copy(adarow[0:2, bass.ds((i + 1) * (RING * HALF) + n * HALF, HALF)], P[n][0:2, :])
                    v.drain().then_inc(drained, 1)
            v.drain().then_inc(fed, me.add("fed"))
            me.first_bank()
            v.wait_ge(filled, me.next("filled"))
            b = me.next_bank()
            mods = mod[:, :, :, :, :].rearrange("p l j k c -> p (l j k) c")
            tt(mods, b[:, 0:192].rearrange("p (q c) -> p q c", c=2), bc(vec("ada_b").unsqueeze(2), 128, 96, 2), ALU.add)
            v.drain().then_inc(drained, 1)
            for l in range(2):
                for j in range(2):
                    m = mod[:, l, 3 * j + 1, :, :]
                    stt(m, m, 1.0, bc(norm_g[:, l, j, :].unsqueeze(2), 128, KT, 2), ALU.add, ALU.mult)
            v.drain()

            norm([segx, segc], [sqx, sqc], rstd, modulated(0, 0))
            v.drain().then_inc(fed, me.add("fed"))
            me.first_bank()
            for tile_ in range(6):
                for g in range(4):
                    v.wait_ge(filled, me.next("filled"))
                    b = me.next_bank()
                    v.tensor_copy(AB[:, tile_, g * 512:(g + 1) * 512], b[:, :])
                    v.drain().then_inc(drained, 1)
            v.drain().then_inc(fed, me.add("fed"))
            me.first_bank()
            for f in range(KT):
                for h, n in ((hx, NX), (hc, NC)):
                    v.wait_ge(filled, me.next("filled"))
                    b = me.next_bank()
                    v.tensor_copy(h[:, f, :], b[:, 0:n])
                    v.drain().then_inc(drained, 1)
            v.drain().then_inc(fed, me.add("fed"))
            me.first_bank()
            tmp = cut(work, 0, NX)
            for f in range(KT):
                for res, h, n, j in (segx, segc):
                    v.wait_ge(filled, me.next("filled"))
                    b = me.next_bank()
                    ts(tmp[:, 0:n], b[:, 0:n], vec("fnet_bo")[:, f:f + 1], ALU.add, mod[:, 0, 2, f, j:j + 1], ALU.mult)
                    v.drain().then_inc(drained, 1)
                    tt(res[:, f, :], res[:, f, :], tmp[:, 0:n], ALU.add)
                    v.drain()

            def moe(l, ctx):
                tiles = 6 if ctx else 4
                S_ = CAPX + CAPC if ctx else CAPX
                W = NX + NC * ctx
                segs = [segx, segc] if ctx else [segx]
                norm(segs, [sqx, sqc], rstd, modulated(l, 1))
                v.drain().then_inc(fed, me.add("fed"))
                me.first_bank()
                v.wait_ge(filled, me.next("filled"))
                b = me.next_bank()
                lg = b[:, 0:tiles * NE].rearrange("p (t e) -> p t e", e=NE)
                af, am = aff[:, 0:tiles, :], amax[:, 0:tiles]
                v.tensor_reduce(am, lg, AX, ALU.max)
                v.drain()
                tt(af, lg, bc(am.unsqueeze(2), 128, tiles, NE), ALU.subtract)
                v.drain().then_inc(drained, 1)
                v.drain().then_inc(asked, me.add("asked"))
                v.wait_ge(answered, me.next("answered"))
                v.tensor_reduce(am, af, AX, ALU.add)
                v.drain()
                v.reciprocal(am, am)
                v.drain()
                tt(af, af, bc(am.unsqueeze(2), 128, tiles, NE), ALU.mult)
                v.drain().then_inc(fed, me.add("fed"))
                for tile_ in range(tiles):
                    for half in range(2):
                        v.wait_ge(filled, me.next("filled"))
                        b = me.next_bank()
                        v.tensor_copy(htok[:, tile_, half * 512:(half + 1) * 512], b[:, :])
                        v.drain().then_inc(drained, 1)
                v.wait_ge(filled, me.next("filled"))
                b = me.next_bank()
                v.tensor_copy(affT[0:NE, 0:NX], b[0:NE, :])
                v.drain().then_inc(drained, 1)
                if ctx:
                    v.wait_ge(filled, me.next("filled"))
                    b = me.next_bank()
                    v.tensor_copy(affT[0:NE, NX:W], b[0:NE, 0:NC])
                    v.drain().then_inc(drained, 1)
                v.memset(ones768[0:NE, 0:W], 1.0)
                v.tensor_copy(left[0:NE, 0:W], affT[0:NE, 0:W])
                for a, n, cap, first in ((0, NX, CAPX, 0.0), (NX, NC, CAPC, float(CAPX)))[:1 + ctx]:
                    part = left[0:NE, a:a + n]
                    for _ in range(cap // 8):
                        v.drain()
                        v.max(top8[0:NE, :], part)
                        v.drain()
                        v.match_replace(part, top8[0:NE, :], part, -1.0)
                v.drain()
                ts(left[0:NE, 0:W], left[0:NE, 0:W], -1.0, ALU.is_equal)
                v.drain()
                for a, n, first in ((0, NX, 0.0), (NX, NC, float(CAPX)))[:1 + ctx]:
                    v.tensor_tensor_scan(slot[0:NE, a:a + n], ones768[0:NE, a:a + n], left[0:NE, a:a + n], first, ALU.mult, ALU.add)
                v.drain()
                tt(slot[0:NE, 0:W], slot[0:NE, 0:W], left[0:NE, 0:W], ALU.mult)
                v.drain()
                ts(slot[0:NE, 0:W], slot[0:NE, 0:W], -1.0, ALU.add)
                v.drain().then_inc(fed, me.add("fed"))
                v.wait_ge(filled, me.next("filled"))
                b = me.next_bank()
                v.tensor_copy(stok[:, 0:tiles, 0:NE], b[:, 0:tiles * NE].rearrange("p (t e) -> p t e", e=NE))
                v.drain().then_inc(drained, 1)
                v.memset(aff_wide[:, :, NE:NE + 2], 0.0)
                v.memset(stok[:, :, NE:NE + 2], -1.0)
                v.drain()

                def picks(first):
                    for j in range(2):
                        tt(pickx[:, :, j * CAPX:(j + 1) * CAPX], bc(tab("iota_row")[:, 0:CAPX].unsqueeze(1), 128, 4, CAPX),
                           bc(stok[:, 0:4, bass.ds(first + j, 1)], 128, 4, CAPX), ALU.is_equal)
                        if ctx:
                            tt(pickc[:, :, j * CAPC:(j + 1) * CAPC], bc(tab("iota_row")[:, CAPX:CAPX + CAPC].unsqueeze(1), 128, 2, CAPC),
                               bc(stok[:, 4:6, bass.ds(first + j, 1)], 128, 2, CAPC), ALU.is_equal)
                            v.tensor_copy(eselc[0:NE, j * CAPC:(j + 1) * CAPC], bc(ident[0:NE, bass.ds(first + j, 1)], NE, CAPC))
                        v.tensor_copy(eselx[0:NE, j * CAPX:(j + 1) * CAPX], bc(ident[0:NE, bass.ds(first + j, 1)], NE, CAPX))
                        v.tensor_copy(affe[:, j, 0:tiles].unsqueeze(2), aff_wide[:, 0:tiles, bass.ds(first + j, 1)])
                    v.drain().then_inc(fed, me.add("fed"))

                if not ctx:
                    for j in range(2):
                        v.memset(xsT[j][:, :, CAPX:FILL], 0.0)
                picks(0)
                me.first_bank()
                with me.loop("expert_ctx" if ctx else "expert", NE // 2) as e:
                    for half in range(2):
                        v.wait_ge(filled, me.next("filled"))
                        v.tensor_copy(xtok[:, half * 512:(half + 1) * 512], me.next_bank()[:, :])
                        v.drain().then_inc(drained, 1)
                    if ctx:
                        v.wait_ge(filled, me.next("filled"))
                        v.tensor_copy(ctok, me.next_bank()[:, :])
                        v.drain().then_inc(drained, 1)
                    v.drain().then_inc(fed, me.add("fed"))
                    v.wait_ge(filled, me.next("filled"))
                    b = me.next_bank()
                    if ctx:
                        v.tensor_copy(gate[0:S_, :], b[0:S_, 0:2])
                        ts(putc[0:2 * CAPC, :], b[0:2 * CAPC, NC:2 * NC], tab("iota_col")[0:2 * CAPC, 1:2], ALU.is_equal)
                    else:
                        v.tensor_copy(gate[:, 0:1], b[:, 0:1])
                    v.drain().then_inc(drained, 1)
                    v.wait_ge(filled, me.next("filled"))
                    ts(putx, me.next_bank()[:, 0:NX], tab("iota_col")[:, 0:1], ALU.is_equal)
                    v.drain().then_inc(drained, 1)
                    for half in range(2):
                        v.wait_ge(filled, me.next("filled"))
                        b = me.next_bank()[:, :].rearrange("p (f s) -> p f s", f=4)
                        for j in range(2):
                            v.tensor_copy(xsT[j][:, 4 * half:4 * half + 4, 0:CAPX], b[:, :, j * CAPX:(j + 1) * CAPX])
                        v.drain().then_inc(drained, 1)
                    if ctx:
                        v.wait_ge(filled, me.next("filled"))
                        b = me.next_bank()[:, :].rearrange("p (f s) -> p f s", f=KT)
                        for j in range(2):
                            v.tensor_copy(xsT[j][:, :, CAPX:S_], b[:, :, j * CAPC:(j + 1) * CAPC])
                        v.drain().then_inc(drained, 1)
                    v.drain().then_inc(fed, me.add("fed"))
                    picks(e * 2 + 2)
                    for j in range(2):
                        for half in range(2):
                            v.wait_ge(filled, me.next("filled"))
                            me.next_bank()
                            v.wait_ge(filled, me.next("filled"))
                            bu = me.next_bank()
                            pass_on()
                            v.drain().then_inc(asked, me.add("asked"))
                            v.wait_ge(answered, me.next("answered"))
                            tt(hid[j][:, 4 * half:4 * half + 4, 0:S_], gact[:, :, 0:S_], bu[:, 0:4 * FILL].rearrange("p (a b) -> p a b", a=4)[:, :, 0:S_], ALU.mult)
                            v.drain().then_inc(drained, 2)
                        v.drain().then_inc(fed, me.add("fed"))
                    for half in range(2):
                        cols = slice(half * 512, (half + 1) * 512)
                        if not ctx:
                            v.wait_ge(filled, me.next("filled"))
                            ts(ysx[:, cols], me.next_bank()[:, :], gate[:, 0:1], ALU.mult)
                            v.drain().then_inc(drained, 1)
                        for j in range(2 * ctx):
                            v.wait_ge(filled, me.next("filled"))
                            b = me.next_bank()
                            ts(ysx[j * CAPX:(j + 1) * CAPX, cols], b[0:CAPX, :], gate[0:CAPX, j:j + 1], ALU.mult)
                            ts(ysc[j * CAPC:(j + 1) * CAPC, cols], b[CAPX:S_, :], gate[CAPX:S_, j:j + 1], ALU.mult)
                            v.drain().then_inc(drained, 1)
                        v.drain().then_inc(fed, me.add("fed"))
                    for f in range(KT):
                        v.wait_ge(filled, me.next("filled"))
                        b = me.next_bank()
                        stt(resx[:, f, :], b[:, :], mod[:, l, 5, f, 0:1], resx[:, f, :], ALU.mult, ALU.add)
                        v.drain().then_inc(drained, 1)
                        if ctx and f % 2:
                            v.wait_ge(filled, me.next("filled"))
                            b = me.next_bank()
                            for q in range(2):
                                stt(resc[:, f - 1 + q, :], b[:, q * NC:(q + 1) * NC], mod[:, l, 5, f - 1 + q, 1:2], resc[:, f - 1 + q, :], ALU.mult, ALU.add)
                            v.drain().then_inc(drained, 1)

            moe(0, True)

            norm([segx, segc], [sqx, sqc], rstd, modulated(1, 0))
            v.drain()
            hxg = hx[:, :, :].rearrange("p k (r c) -> p k r c", c=64)
            dx, dxg = diff[:, NC:NC + NX], diff[:, NC:NC + NX].rearrange("p (r c) -> p r c", c=64)
            dc = diff[:, 0:NC]

            def shifted(k):
                g = hxg[:, k, :, :]
                src, dst, edge = [
                    ((slice(None), slice(0, 63)), (slice(None), slice(1, 64)), (slice(None), slice(0, 1))),
                    ((slice(None), slice(1, 64)), (slice(None), slice(0, 63)), (slice(None), slice(63, 64))),
                    ((slice(0, 7), slice(None)), (slice(1, 8), slice(None)), (slice(0, 1), slice(None))),
                    ((slice(1, 8), slice(None)), (slice(0, 7), slice(None)), (slice(7, 8), slice(None)))][k // 2]
                tt(dxg[:, dst[0], dst[1]], g[:, src[0], src[1]], g[:, dst[0], dst[1]], ALU.subtract)
                ts(dxg[:, edge[0], edge[1]], g[:, edge[0], edge[1]], -1.0, ALU.mult)
                c = hc[:, k, :]
                s, d, e = ((slice(0, NC - 1), slice(1, NC), slice(0, 1)) if k < KT // 2 else
                           (slice(1, NC), slice(0, NC - 1), slice(NC - 1, NC)))
                tt(dc[:, d], c[:, s], c[:, d], ALU.subtract)
                ts(dc[:, e], c[:, e], -1.0, ALU.mult)

            stream = 0
            v.drain().then_inc(asked, me.add("asked"))
            for j, what, mt, ns in W_MIX:
                for half in range(ns):
                    me.first_bank()
                    for k in range(KT):
                        shifted(k)
                        v.drain()
                        if k >= 2:
                            v.wait_ge(mix_used, stream * (KT - 1) + k - 1)
                        m = mixed[k % 2]
                        stt(m[:, NC:NC + NX], dx, mixes[:, j, k:k + 1], hx[:, k, :], ALU.mult, ALU.add)
                        stt(m[:, 0:NC], dc, mixes[:, j, k:k + 1], hc[:, k, :], ALU.mult, ALU.add)
                        v.drain().then_inc(fed, me.add("fed"))
                    stream += 1
                    if what in "wg":
                        v.wait_ge(filled, me.next("filled"))
                        me.next_bank()
                        if what == "w":
                            v.wait_ge(filled, me.next("filled"))
                            me.next_bank()
                        v.drain().then_inc(asked, me.add("asked"))
                        v.wait_ge(answered, me.next("answered"))
                        v.drain().then_inc(drained, 2 if what == "w" else 1)
                        continue
                    if what == "a":
                        v.wait_ge(filled, me.next("filled"))
                        b = me.next_bank()
                        v.tensor_copy(HA[:, NC:NC + NX], b[:, :])
                        v.drain().then_inc(drained, 1)
                        v.wait_ge(filled, me.next("filled"))
                        b = me.next_bank()
                        v.tensor_copy(HA[:, 0:NC], b[:, 0:NC])
                        v.drain().then_inc(drained, 1)
                        continue
                    for m4 in range(mt):
                        f = half * 4 + m4
                        v.wait_ge(filled, me.next("filled"))
                        b = me.next_bank()
                        v.tensor_copy({"r": Rx[:, 1:KT + 1, :], "k": Kx, "v": Vx}[what][:, f, :], b[:, :])
                        v.drain().then_inc(drained, 1)
                        if what != "r":
                            v.wait_ge(filled, me.next("filled"))
                            b = me.next_bank()
                            v.tensor_copy({"k": Kc, "v": Vc}[what][:, f, :], b[:, 0:NC])
                            v.drain().then_inc(drained, 1)

            s = t["slab"]
            s.n = LORA_SLAB
            lora = ring[s.n % RING]
            v.wait_ge(slab_loaded[s.n % RING], 16 * (s.n // RING + 1))
            lora2 = lora[:, :, :].rearrange("p a b -> p (a b)")
            v.wait_ge(spilled, 16)
            for z in (Y, Rx[:, 0, :], lnx, g2p):
                v.memset(z, 0.0)
            v.drain()

            def centred(b):
                stt(Y, b[:, :], -1.0 / CH, Y, ALU.mult, ALU.add)
                v.drain().then_inc(drained, 1)
                tt(squares, Y, Y, ALU.mult)
                v.drain().then_inc(fed, me.add("fed"))

            def variances(b):
                ts(squares, b[:, :], 1.0 / CH, ALU.mult, 64e-5, ALU.add)
                v.drain().then_inc(drained, 1)
                v.drain().then_inc(asked, me.add("asked"))

            def normed(out):
                v.wait_ge(answered, me.next("answered"))
                v.reciprocal(squares, squares)
                v.drain()
                tt(Y, Y, squares, ALU.mult)
                v.drain()
                ts(Y, Y, lnx[:, 0:1], ALU.mult, lnx[:, 1:2], ALU.add)
                v.drain()
                tt(Y, Y, out, ALU.add)
                v.drain()

            with me.loop("pair", KT) as p:
                me.pair = (p, {"dve": PER["pair"]["filled"], "act": PER["pair"]["afilled"]})
                v.tensor_copy(pp[:, 0:9], rwp[:, bass.ds(p, 1), :].rearrange("p a b -> p (a b)"))
                for q, dst in enumerate((w2p, a2p)):
                    v.tensor_copy(dst, lora2[:, bass.ds(p * 128 + 1024 * q, 128)])
                kx, kc, vx, vc, rx, result = (z[:, bass.ds(q, 1), :].rearrange("p a b -> p (a b)") for z, q in
                                              ((Kx, p), (Kc, p), (Vx, p), (Vc, p), (Rx, p + 1), (Rx, p)))
                v.tensor_copy(vp[:, 0:NC], vc)
                v.tensor_copy(vp[:, NC:768], vx)
                v.drain()
                ts(pp[:, 9:10], pp[:, 5:6], -1.0, ALU.mult, 1.0, ALU.add)
                ts(kkv[:, 0:NC], kc, pp[:, 4:5], ALU.mult)
                ts(kkv[:, NC:768], kx, pp[:, 4:5], ALU.mult)
                v.drain()
                tt(ksq, kkv, kkv, ALU.mult)
                v.drain().then_inc(fed, me.add("fed"))
                me.split_banks()
                for a, n in ((0, NC), (NC, NX)):
                    v.wait_ge(filled, me.next("filled"))
                    b = me.next_bank()
                    ts(ksq[:, a:a + n], b[:, 0:n], 1e-12, ALU.add)
                    v.drain().then_inc(drained, 1)
                v.drain().then_inc(asked, me.add("asked"))
                chunked = "p (c n) -> p c n"

                def decays(d):
                    v.wait_ge(drained_act, me.group("act", ("pre", d, 3)))
                    ts(lw[d], lw[d], -math.exp(-0.5), ALU.mult)
                    ts(kd[d], bd[d], pp[:, 5:6], ALU.mult, pp[:, 9:10], ALU.add)
                    v.drain()
                    v.tensor_tensor_scan(Lc[d], tab("chunk"), lw[d], 0.0, ALU.mult, ALU.add)
                    v.drain()
                    L3 = Lc[d].rearrange(chunked, c=NCH)
                    ET3 = ETd[d].unsqueeze(2)
                    v.tensor_copy(ET3, L3[:, :, CH - 1:CH])
                    v.drain()
                    if d == 1:
                        tt(L3, bc(ET3, 128, NCH, CH), L3, ALU.subtract)
                        v.drain()
                        tt(Lc[d], Lc[d], lw[d], ALU.add)
                        v.drain()
                    tt(E1[d], Lc[d], lw[d], ALU.subtract)
                    v.drain().then_inc(asked, me.add("asked"))

                def scaled_keys(d):
                    tt(kd[d][:, 0:NC], kd[d][:, 0:NC], kc, ALU.mult)
                    tt(kd[d][:, NC:768], kd[d][:, NC:768], kx, ALU.mult)
                    tt(bd[d], bd[d], kkn, ALU.mult)
                    v.drain()
                    if d == 0:
                        v.tensor_copy(ksum, kd[d][:, NC:768])
                    else:
                        tt(ksum, ksum, kd[d][:, NC:768], ALU.add)
                    v.drain()
                    v.wait_ge(answered, me.next("answered"))
                    L3 = Lc[d].rearrange(chunked, c=NCH)
                    stt(ar[d][:, :, 0:CH], kkn.rearrange(chunked, c=NCH), -1.0, E1[d].rearrange(chunked, c=NCH), ALU.mult, ALU.mult)
                    tt(ar[d][:, GC:NCH, CH:128], rx.rearrange(chunked, c=NCX), L3[:, GC:NCH, :], ALU.mult)
                    tt(bd[d], bd[d], E3[d], ALU.mult)
                    tt(kd[d], kd[d], E3[d], ALU.mult)
                    v.drain().then_inc(fed, me.add("fed"))

                decays(0)
                v.wait_ge(answered, me.next("answered"))
                v.reciprocal(ksq, ksq)
                v.drain()
                tt(kkn, kkv, ksq, ALU.mult)
                v.drain()
                scaled_keys(0)
                decays(1)
                for d, bi, b in UNITS:
                    if (d, bi) == (1, 0):
                        scaled_keys(1)
                    xb = slice(b.start - GC, b.stop - GC)
                    for dst, mask, q in ((NT[d], None, QB[d]), (MT[d], tab("strict")[:, d * CH:(d + 1) * CH], QK[d])):
                        v.wait_ge(filled, me.next("filled"))
                        p3 = me.next_bank()[:, :].rearrange(chunked, c=GC)
                        if mask is None:
                            v.tensor_copy(dst[:, b, :], p3[:, :, 0:CH])
                        else:
                            tt(dst[:, b, :], p3[:, :, 0:CH], bc(mask.unsqueeze(1), 128, GC, CH), ALU.mult)
                        if bi:
                            tt(q[:, xb, :], p3[:, :, CH:128], bc(tab("incl")[:, d * CH:(d + 1) * CH].unsqueeze(1), 128, GC, CH), ALU.mult)
                        v.drain().then_inc(drained, 1)
                tt(ksum, ksum, rx, ALU.mult)
                v.drain()
                ts(ksum, ksum, pp[:, 6:7], ALU.mult)
                v.drain().then_inc(fed, me.add("fed"))
                for b in BATCHES:
                    v.wait_ge(filled, me.next("filled"))
                    v.tensor_copy(Vt[:, b, :], me.next_bank()[:, 0:256].rearrange("p (c n) -> p c n", c=GC))
                    v.drain().then_inc(drained, 1)
                v.wait_ge(filled, me.next("filled"))
                b = me.next_bank()
                pass_on()
                tt(rx, b[:, :], vx, ALU.mult)
                v.drain().then_inc(drained, 1)
                for d, bi, b in UNITS:
                    v.wait_ge(filled, me.next("filled"))
                    tt(X[d][:, b, :], me.next_bank()[:, 0:256].rearrange(chunked, c=GC), bc(eye2.unsqueeze(1), 128, GC, CH), ALU.add)
                    v.drain().then_inc(drained, 1)
                v.wait_ge(filled, me.next("filled"))
                centred(me.next_bank())
                for l in range(1, 6):
                    if l == 2:
                        v.wait_ge(filled, me.next("filled"))
                        variances(me.next_bank())
                    if l == 3:
                        normed(result)
                        v.wait_ge(filled, me.next("filled"))
                        b = me.next_bank()
                        pass_on()
                        tt(result, Y, b[:, :], ALU.mult)
                        v.drain().then_inc(drained, 1)
                        v.tensor_copy(lnx, pp[:, 7:9])
                        v.tensor_copy(g2p, lora2[:, bass.ds(p * 128 + 2 * 1024, 128)])
                    for d, bi, b in UNITS:
                        v.wait_ge(filled, me.next("filled"))
                        p4 = me.next_bank()[:, :].rearrange("p (x c n) -> p x c n", x=2, c=GC)
                        if l < 5:
                            tt(XX[d][:, :, b, :], XX[d][:, :, b, :], p4, ALU.add)
                        else:
                            tt(XT[d][:, b, :], XT[d][:, b, :], p4[:, 1, :, :], ALU.add)
                        v.drain().then_inc(drained, 1)
                for d, bi, b in UNITS:
                    xb = slice(b.start - GC, b.stop - GC)
                    v.wait_ge(filled, me.next("filled"))
                    p3 = me.next_bank()[:, :].rearrange(chunked, c=GC)
                    tt(At[d][:, b, :], p3[:, :, 0:CH], bc(eye2.unsqueeze(1), 128, GC, CH), ALU.add)
                    if bi:
                        tt(Rt[d][:, xb, :], p3[:, :, CH:128], ar[d][:, b, CH:128], ALU.add)
                    v.drain().then_inc(drained, 1)
                    v.wait_ge(filled, me.next("filled"))
                    p3 = me.next_bank()[:, 0:256].rearrange(chunked, c=GC)
                    tt(Bc[d][:, b, :], p3, bc(ETd[d][:, b].unsqueeze(2), 128, GC, CH), ALU.mult)
                    v.drain().then_inc(drained, 1)
                    if bi:
                        v.wait_ge(filled, me.next("filled"))
                        p2 = me.next_bank()[:, 0:256]
                        y = Y[:, 256 * (bi - 1):256 * bi]
                        if d == 0:
                            v.tensor_copy(y, p2)
                        else:
                            tt(y, y, p2, ALU.add)
                        v.drain().then_inc(drained, 1)
                for d in range(2):
                    v.tensor_copy(Z[d], Bc[d][:, CHAIN[d][0], :])
                    v.drain().then_inc(fed, me.add("fed"))
                for j in range(1, NCH):
                    for d in range(2):
                        c = CHAIN[d][j]
                        v.wait_ge(filled, me.next("filled"))
                        p2 = me.next_bank()
                        if j < NCH - 1:
                            stt(Z[d], p2[:, 0:CH], ETd[d][:, c:c + 1], Bc[d][:, c, :], ALU.mult, ALU.add)
                            v.drain().then_inc(drained, 1)
                            v.drain().then_inc(fed, me.add("fed"))
                        else:
                            tt(Y, Y, P[4 + d][:, :], ALU.add)
                            v.drain().then_inc(drained, 1)
            v.drain().then_inc(fed, me.add("fed"))
            me.first_bank()
            v.wait_ge(filled, me.next("filled"))
            centred(me.next_bank())
            v.wait_ge(filled, me.next("filled"))
            variances(me.next_bank())
            normed(Rx[:, KT, :])
            v.wait_ge(filled, me.next("filled"))
            tt(Rx[:, KT, :], Y, me.next_bank()[:, :], ALU.mult)
            v.drain().then_inc(drained, 1)
            me.width = 8
            v.drain().then_inc(asked, me.add("asked"))
            v.wait_ge(spilled, 32)
            v.drain().then_inc(slab_used, 3)
            v.drain().then_inc(fed, me.add("fed"))
            me.first_bank()
            for f in range(KT):
                v.wait_ge(filled, me.next("filled"))
                b = me.next_bank()
                stt(resx[:, f, :], b[:, :], mod[:, 1, 2, f, 0:1], resx[:, f, :], ALU.mult, ALU.add)
                v.drain().then_inc(drained, 1)
            v.drain()
            moe(1, False)
            v.drain()
            norm([segx], [sqx], rstd, lambda k, j: (vec("final_g")[:, k:k + 1], None))
            v.drain()
            v.tensor_copy(resx[:, :, :], hx[:, :, :])

            v.drain().then_inc(asked, me.add("asked"))
            v.wait_ge(tables_loaded, 80)
            t["afilled"].n = KT * PER["pair"]["afilled"]
            with me.loop("layer", 2) as l:
                v.tensor_copy(pv, layer2[:, bass.ds(l, 1), :].rearrange("p a b -> p (a b)"))
                v.drain().then_inc(asked, me.add("asked"))
                segs = [(resx, hx, NX, 0)]
                norm(segs, [sq2], rstd2, lambda k, j: (pv[:, k:k + 1], None))
                v.drain().then_inc(fed, me.add("fed"))
                me.first_bank()
                for f in range(F_TILES):
                    v.wait_ge(filled, me.next("filled"))
                    b = me.next_bank()
                    v.tensor_copy(Fm[:, f, :], b[:, :])
                    v.drain().then_inc(drained, 1)
                for c0, n in ((0, 256), (256, TM_W - 256)):
                    for i in range(4):
                        v.wait_ge(filled, me.next("filled"))
                        b = me.next_bank()
                        v.tensor_copy(VT[:, i, c0:c0 + n], b[:, 0:n])
                        v.drain().then_inc(drained, 1)
                v.drain()
                tt(S[:, 0:3, :], Fm[:, 0:3, :], Fm[:, 0:3, :], ALU.mult)
                v.drain().then_inc(fed, me.add("fed"))
                me.first_bank()
                inverse_roots([(NX, 256), (NX, 128)], S[:, 0:2, :].rearrange("p a b -> p (a b)"), 1e-6)
                for k in range(3):
                    stt(Fm[:, k, :], Fm[:, k, :], pv[:, 16 + k:17 + k], S[:, k // 2, :], ALU.mult, ALU.mult)
                tt(lf, VT[:, :, TM_W - 4:TM_W], bc(pv[:, 23:27].unsqueeze(1), 128, 4, 4), ALU.add)
                v.drain()
                stt(le, lf, -1.0, lf, ALU.mult, ALU.min)
                v.drain().then_inc(asked, me.add("asked"))
                v.wait_ge(answered, me.next("answered"))
                ts(le, le, 1.0, ALU.add)
                v.drain().then_inc(asked, me.add("asked"))
                v.wait_ge(answered, me.next("answered"))
                stt(lf, lf, 0.0, le, ALU.min, ALU.subtract)
                v.drain()
                for h in range(HEADS):
                    v.tensor_copy(lfb[:, h, :, :], bc(lf[:, :, h:h + 1], 128, 4, 128))
                v.wait_ge(aux_loaded, l * 16 + 16)
                pass_on()
                v.drain().then_inc(fed, me.add("fed"))
                for dst, j in ((QN, 0), (QN, 1), (QR, None), (KN, 0), (KN, 1)):
                    v.wait_ge(filled, me.next("filled"))
                    b = me.next_bank()
                    v.tensor_copy(tile(dst, j), b[:, :])
                    v.drain().then_inc(drained, 1)
                for i in range(4):
                    v.wait_ge(filled, me.next("filled"))
                    b = me.next_bank()
                    v.tensor_copy(VA[:, i, :], b[:, 0:256])
                    v.drain().then_inc(drained, 1)
                v.drain().then_inc(fed, me.add("fed"))
                me.first_bank()
                for r, (dst, j, d) in enumerate(ROPED):
                    x = tile(dst, j)
                    v.wait_ge(filled, me.next("filled"))
                    b = me.next_bank()
                    tt(S[:, 0, :], b[:, :], tab2(f"sin{d}"), ALU.mult)
                    v.drain().then_inc(drained, 1)
                    tt(x, x, tab2(f"cos{d}"), ALU.mult)
                    v.drain()
                    tt(x, x, S[:, 0, :], ALU.add)
                    v.drain()
                    if r in FORGETS:
                        v.wait_ge(filled, me.next("filled"))
                        b = me.next_bank()
                        v.tensor_copy(cumk[:, FORGETS[r], :], b[:, :])
                        v.drain().then_inc(drained, 1)
                v.drain().then_inc(fed, me.add("fed"))
                me.split_banks()

                def weights(u):
                    v.wait_ge(answered, me.next("answered"))
                    if ATTENTION[u][0] == "swa":
                        tt(sums[u % 2], sums[u % 2], esink[u % 2], ALU.add)
                        v.drain()
                    v.reciprocal(sums[u % 2], sums[u % 2])
                    v.drain().then_inc(weighted, 1)

                def logits(u):
                    va, i = ATTENTION[u]
                    S = SS[u % 2]
                    k0, k1 = span(va, i)
                    n = k1 - k0
                    causal = tab2("causal")[:, 384 - 128 * i + k0:384 - 128 * i + k1]
                    mask = causal
                    if va == "swa":
                        mask = tab2("window")[:, 384 - 128 * i + k0:384 - 128 * i + k1]
                    if va == "dsa" and i > 0:
                        sc, rs = score[:, 0:n], rest[:, 0:n]
                        for h in range(8):
                            v.wait_ge(filled, me.next("filled"))
                            b = me.next_bank()
                            wcol = VT[:, i, 640 + h:641 + h]
                            ts(rs if h else sc, b[:, 0:n], 0.0, ALU.max, wcol, ALU.mult)
                            v.drain().then_inc(drained, 1)
                            if h:
                                tt(sc, sc, rs, ALU.add)
                                v.drain()
                        tt(rs, sc, causal, ALU.add)
                        for _ in range(TOPK // 8):
                            v.drain()
                            v.max(t8, rs)
                            v.drain()
                            v.match_replace(rs, t8, rs, -3e38)
                        v.drain()
                        ts(keep[:, 0:n], rs, -2e38, ALU.is_gt, NEG, ALU.mult)
                        v.drain()
                        mask = keep[:, 0:n]
                    for h, (parts, _, _, _) in enumerate(heads(va)):
                        if u >= 2:
                            v.wait_ge(filled_act, me.next("afilled"))
                        if va == "fox":
                            tt(S[:, h, 0:n], causal, cumk[:, h, 0:n], ALU.subtract)
                            v.drain()
                            mask = S[:, h, 0:n]
                        v.wait_ge(filled, me.next("filled"))
                        b = me.next_bank()
                        stt(S[:, h, 0:n], b[:, 0:n], SCALE[va], mask, ALU.mult, ALU.add)
                        v.drain().then_inc(drained, 1)
                        if len(parts) == 2:
                            v.wait_ge(filled, me.next("filled"))
                            b = me.next_bank()
                            stt(S[:, h, 0:n], b[:, 0:n], SCALE[va], S[:, h, 0:n], ALU.mult, ALU.add)
                            v.drain().then_inc(drained, 1)
                    v.tensor_reduce(mx[u % 2], S[:, :, 0:n], AX, ALU.max)
                    v.drain()
                    if va == "swa":
                        tt(mx[u % 2], mx[u % 2], pv[:, 19:23], ALU.max)
                        v.drain()
                        tt(esink[u % 2], pv[:, 19:23], mx[u % 2], ALU.subtract)
                    ts(mxn[u % 2], mx[u % 2], -1.0, ALU.mult)
                    v.drain().then_inc(asked, me.add("asked"))

                logits(0)
                logits(1)
                weights(0)
                for u, (va, i) in enumerate(ATTENTION):
                    if u + 1 < len(ATTENTION):
                        weights(u + 1)
                    if u + 2 < len(ATTENTION):
                        logits(u + 2)
                    for _, _, ot, rows in heads(va):
                        v.wait_ge(filled, me.next("filled"))
                        b = me.next_bank()
                        v.tensor_copy(OT[rows, ot, 128 * i:128 * i + 128], b[rows, 0:128])
                        v.drain().then_inc(drained, 1)
                me.width = 8
                me.t["afilled"].n += 2 * HEADS
                v.drain().then_inc(slab_used, 1)
                v.drain().then_inc(fed, me.add("fed"))
                me.first_bank()
                for f in range(KT):
                    v.wait_ge(filled, me.next("filled"))
                    b = me.next_bank()
                    tt(resx[:, f, :], resx[:, f, :], b[:, :], ALU.add)
                    v.drain().then_inc(drained, 1)
                v.drain()
                norm(segs, [sq2], rstd2, lambda k, j: (pv[:, 8 + k:9 + k], None))
                v.drain().then_inc(fed, me.add("fed"))
                me.first_bank()
                for f in range(32):
                    v.wait_ge(filled, me.next("filled"))
                    b = me.next_bank()
                    ts(up[:, f, :], b[:, :], 0.0, ALU.max)
                    v.drain().then_inc(drained, 1)
                    tt(up[:, f, :], up[:, f, :], up[:, f, :], ALU.mult)
                v.drain().then_inc(fed, me.add("fed"))
                me.first_bank()
                for f in range(KT):
                    v.wait_ge(filled, me.next("filled"))
                    b = me.next_bank()
                    tt(resx[:, f, :], resx[:, f, :], b[:, :], ALU.add)
                    v.drain().then_inc(drained, 1)
                v.drain()
            norm([(resx, hx, NX, 0)], [sq2], rstd2, lambda k, j: (vec("final2")[:, k:k + 1], None))
            v.drain().then_inc(asked, me.add("asked"))

        @block.gpsimd
        def _(pool):
            me = Side(pool, K)
            with me.loop("pair", KT) as i:
                me.pair = (i, {"dve": PER["pair"]["filled"], "act": PER["pair"]["afilled"]})
                for l in range(6):
                    m = [levels[:, d, l, :].unsqueeze(1).to_broadcast([128, GC, CH]) for d in range(2)]
                    for d, bi, b in UNITS:
                        if l == 0:
                            pool.wait_ge(drained, me.group("dve", ("NT", d, bi)))
                        elif l == 1:
                            pool.wait_ge(drained, me.group("dve", ("X0", d, bi)))
                        else:
                            pool.wait_ge(drained_act, me.group("act", ("T", d, l - 1, bi)))
                        pool.tensor_tensor(NL[d][:, b, :], NT[d][:, b, :], m[d], ALU.mult)
                        if l == 0:
                            pool.drain()
                            pool.tensor_tensor(XT[d][:, b, :], NL[d][:, b, :], eye2.unsqueeze(1).to_broadcast([128, GC, CH]), ALU.add)
                        pool.drain().then_inc(masked, me.add("masked"))

            with me.loop("layer", 2):
                for u, (va, i) in enumerate(ATTENTION):
                    n = span(va, i)[1] - span(va, i)[0]
                    pool.wait_ge(weighted, me.next("weighted"))
                    pool.tensor_tensor(SS[u % 2][:, :, 0:n], SS[u % 2][:, :, 0:n], sums[u % 2].unsqueeze(2).to_broadcast([128, HEADS, n]), ALU.mult)
                    pool.drain().then_inc(normalised, 1)

        if K.wrong:
            raise ValueError(f"counts of the loops: {sorted(K.wrong)}")


def shape_tables():
    f = np.float32
    p = np.arange(128)
    t1 = {}
    t1["ident"] = np.eye(128)
    t1["ones"] = np.ones((128, 128))
    t1["headones"] = (p[:, None] // 64 == p[None, :] // 64) * 1.0
    t1["iota_row"] = np.broadcast_to(np.arange(96), (128, 96))
    t1["iota_col"] = np.stack([p % CAPX, CAPX + p % CAPC], 1)
    t1["chunk"] = np.broadcast_to((np.arange(768) % CH != 0) * 1.0, (128, 768))
    s, t = p[:, None] % CH, np.arange(CH)[None, :]
    lev = []
    for d in range(2):
        a, b = (s, t) if d == 0 else (t, s)
        for l in range(6):
            n = 2 ** l
            lev.append((a // (2 * n) == b // (2 * n)) & (a // n % 2 == 0) & (b // n % 2 == 1))
    t1["level"] = np.concatenate(lev, 1)
    t1["strict"] = np.concatenate([s < t, s > t], 1)
    t1["incl"] = np.concatenate([s <= t, s >= t], 1)
    t1["eye2"] = (s == t) * 1.0
    t2 = {}
    pos = np.arange(512, dtype=f)
    for d in (64, 32):
        half = d // 2
        inv = (1.0 / (f(10000.0) ** (np.arange(half, dtype=f) * f(2.0) / f(d)))).astype(f)
        ang = (inv[p % half][:, None] * pos[None, :]).astype(f)
        t2[f"cos{d}"], t2[f"sin{d}"] = np.cos(ang), np.sin(ang)
        rot = np.zeros((128, 128))
        for r in range(128):
            if r % d < half:
                rot[r + half, r] = -1.0
            else:
                rot[r - half, r] = 1.0
        t2[f"rot{d}"] = rot
    x = np.arange(896)[None, :] - 384
    q = p[:, None]
    t2["causal"] = np.where(x <= q, 0.0, NEG)
    t2["window"] = np.where((x <= q) & (q - x < 128), 0.0, NEG)
    t2["upto"] = (x >= q) * 1.0
    pack = lambda t, order: np.ascontiguousarray(np.concatenate([t[n] for n in order], 1).astype(f))
    n = np.arange(256)
    ang = 2 * np.pi * (np.outer(n, n) % 256) / 256
    feat = np.concatenate([np.cos(ang), np.sin(ang)], 1)
    fc = feat.reshape(2, 128, 512).transpose(1, 0, 2).reshape(128, 1024)

    def seq(T):
        m = np.arange(T)
        a = 2 * np.pi * (np.outer(m, m) % T) / T
        r = 1.0 / math.sqrt(T * 256)
        both = np.stack([np.cos(a) * r, -np.sin(a) * r])
        return both.reshape(2, T // 128, 128, T).transpose(2, 0, 1, 3).reshape(128, -1)

    first = np.zeros((128, 4096))
    first[:, 0:1024] = fc
    first[:, 1024:2048] = seq(256)
    return pack(t1, TAB1), pack(t2, TAB2), first.astype(f), seq(512).astype(f)


def lay_out(i):
    f = np.float32
    g = {k: np.asarray(a) for k, a in i.items()}
    tabs1, tabs2, fnet1, fnet2 = shape_tables()
    slabs = np.zeros((SLABS, 128, 4096), f)
    n = 0

    def add(w):
        nonlocal n
        k, cols = w.shape
        for c in range(0, cols, 512):
            part = w[:, c:c + 512]
            slabs[n].reshape(128, 8, 512)[:, 0:k // 128, 0:part.shape[1]] = part.reshape(k // 128, 128, -1).transpose(1, 0, 2)
            n += 1

    def moe(l):
        for e in range(0, NE, 2):
            for j in range(2):
                for h in range(2):
                    add(g["moe_wg"][l, e + j][:, 512 * h:512 * h + 512])
                    add(g["moe_wu"][l, e + j][:, 512 * h:512 * h + 512])
            for h in range(2):
                for j in range(2):
                    add(g["moe_wd"][l, e + j][:, 512 * h:512 * h + 512])

    for l in range(2):
        add(g["ada_w"][l])
    slabs[n], slabs[n + 1] = fnet1, fnet2
    n += 2
    add(g["fnet_wo"][0])
    moe(0)
    add(np.concatenate([g["rw_w1"][0, 0], g["rw_w1"][0, 1], g["rw_a1"][0, 0], g["rw_a1"][0, 1], g["rw_g1"][0]], 1))
    for w in ("rw_wr", "rw_wk", "rw_wv"):
        add(g[w][0])
    slabs[n][:, 0:1024] = g["rw_w2"][0].reshape(128, D)
    slabs[n][:, 1024:2048] = g["rw_a2"][0].reshape(128, D)
    slabs[n][:, 2048:3072] = g["rw_g2"][0]
    n += 1
    add(g["rw_wo"][0])
    moe(1)
    sizes = [256, 128, 32, 256, 128, 128, 256, 256, 256, 256, 32, 8, 256, 256, 256, 4]
    ends = np.cumsum(sizes)
    cols = [np.arange(e - s, e) for s, e in zip(sizes, ends)]
    (acq, ackv, akr, bq, bk, bv, cq, ck, cv, cqi, cki, cw, dq, dk, dv, df) = cols
    swap = np.concatenate([np.arange(64 * h, 64 * h + 64) for h in (0, 2, 1, 3)])
    order = np.concatenate([acq, ackv, bq[swap], bk, cq, ck, cqi, dq, dk, np.tile(akr, 4), np.tile(cki, 4), bv, cv, dv, cw, df])
    mixed_rows = np.arange(D)
    mixed_rows[256:512] = 256 + swap
    aux = np.zeros((2, 128, 1280), f)
    nope = np.concatenate([np.arange(96 * h, 96 * h + 64) for h in range(4)] + [np.arange(96 * h + 64, 96 * h + 96) for h in range(4)])
    kv = np.concatenate([np.arange(128 * h, 128 * h + 64) for h in range(4)] + [np.arange(128 * h + 64, 128 * h + 128) for h in range(4)])
    for l in range(2):
        add(g["w_in_2"][l][:, order])
        add(g["w_out_2"][l][mixed_rows])
        add(g["w_up_2"][l])
        for h in range(2):
            for kg in range(4):
                add(g["w_down_2"][l][kg * D:(kg + 1) * D, 512 * h:512 * h + 512])
        aux[l][:, 0:768] = g["mla_w_uq_2"][l][:, nope].reshape(2, 128, 384).transpose(1, 0, 2).reshape(128, 768)
        aux[l][:, 768:] = g["mla_w_ukv_2"][l][:, kv]
    assert n == SLABS, n

    def tiles(v):
        return v.reshape(-1, 128).T

    def rows(v):
        return np.broadcast_to(v.reshape(1, -1), (128, v.size))

    parts = {
        "c": np.stack([tiles(g["c"][0]), tiles(g["c_ctx"])], 2).reshape(128, 16),
        "ada_b": tiles(g["ada_b"]), "norm_g": tiles(g["norm_g"]), "fnet_bo": tiles(g["fnet_bo"]),
        "final_g": tiles(g["final_g"]), "mix": tiles(g["rw_mix"][0]),
        "rwp": np.stack([tiles(z) for z in (g["rw_w0"][0, 0], g["rw_w0"][0, 1], g["rw_a0"][0, 0], g["rw_a0"][0, 1], g["rw_kk"][0],
                                            g["rw_ka"][0], g["rw_rk"][0].reshape(-1), g["rw_lnx_w"][0], g["rw_lnx_b"][0])], 2).reshape(128, 72),
        "router": g["moe_router"].reshape(2, 8, 128, 16).transpose(2, 0, 1, 3).reshape(128, 256),
        "layer2": np.concatenate([np.concatenate([
            tiles(g["norm1_2"][l]), tiles(g["norm2_2"][l]), tiles(g["mla_q_norm_2"][l]), tiles(g["mla_kv_norm_2"][l]),
            rows(g["swa_sinks_2"][l][[0, 2, 1, 3]]), rows(g["fox_b_f_2"][l])], 1) for l in range(2)], 1),
        "final2": tiles(g["final_norm_2"]),
    }
    vecs = np.ascontiguousarray(np.concatenate([parts[k] for k in VEC], 1))
    return {"slabs": slabs, "vecs": vecs, "tabs1": tabs1, "tabs2": tabs2, "aux": aux,
            "xT": np.ascontiguousarray(g["x"][0].T), "ctxT": np.ascontiguousarray(g["ctx"][0].T)}


def kernel(**inputs):
    import numpy as _np
    import concourse.bacc as _bacc
    from concourse import mybir as _mybir
    from concourse.bass_utils import run_bass_kernel_spmd as _run

    nc = _bacc.Bacc("TRN2", target_bir_lowering=False, num_devices=1)
    arrays = lay_out(inputs)
    args = [nc.dram_tensor(name, a.shape, _mybir.dt.from_np(a.dtype), kind="ExternalInput").ap() for name, a in arrays.items()]
    out = nc.dram_tensor("outT", (D, NX), _mybir.dt.float32, kind="ExternalOutput").ap()
    spill = nc.dram_tensor("spill", (128, KT * NX), _mybir.dt.float32, kind="Internal").ap()
    build(nc, *args, out, spill)
    r = _run(nc, [arrays], core_ids=[0])
    return _np.ascontiguousarray(r.results[0]["outT"].T)[None]
```
